# Optimizing a Trainium2 kernel written in Bass

```python
import jax, jax.numpy as jnp
from jax import lax
import numpy as np

D_MODEL = 1024
BATCH = 1
SEQ = 1024
DEPTH = 2
DEC_BATCH = 1
DEC_SEQ = 512
PAST_LEN = 128

GRID_W = 64
NA_HEADS = 8
NA_HEAD_DIM = 64
NA_WIN_ROWS = 8
NA_WIN_COLS = 16
NA_W = NA_HEADS * NA_HEAD_DIM
CONV_CH = 512
CONV_WIDTH = 31
MLA_HEADS = 8
MLA_NOPE = 64
MLA_ROPE = 32
MLA_V = 64
Q_LORA = 256
KV_LORA = 128
ROPE_THETA = 10000.0
ATTN_BLOCK = 128
MLA_W = MLA_HEADS * MLA_V
FNET_GROUPS = 4
FNET_GROUP_DIM = 128
FNET_W = FNET_GROUPS * FNET_GROUP_DIM
PLE_DIM = 256
EPS = 1e-6

N_EVEN = (DEPTH + 1) // 2
N_ODD = DEPTH // 2
EVEN_SPLITS = (NA_W, NA_W, NA_W, NA_W, CONV_CH, CONV_CH, CONV_CH)
ODD_SPLITS = (Q_LORA, KV_LORA, MLA_ROPE, MLA_W, FNET_W, FNET_W)
EVEN_IN = sum(EVEN_SPLITS)
ODD_IN = sum(ODD_SPLITS)

kernel_name = "hybrid_natten_conformer_mla_fnet_encoder"

def _split(z, sizes):
    idx = [int(c) for c in np.cumsum(sizes)[:-1]]
    return jnp.split(z, idx, axis=-1)

def _rmsnorm(x, g):
    xf = x.astype(jnp.float32)
    y = xf * lax.rsqrt(jnp.mean(xf * xf, axis=-1, keepdims=True) + EPS)
    return (y * g.astype(jnp.float32)).astype(x.dtype)

def _layernorm(x, g, b):
    xf = x.astype(jnp.float32)
    mu = jnp.mean(xf, axis=-1, keepdims=True)
    var = jnp.mean(jnp.square(xf - mu), axis=-1, keepdims=True)
    y = (xf - mu) * lax.rsqrt(var + EPS)
    return (y * g.astype(jnp.float32) + b.astype(jnp.float32)).astype(x.dtype)

def _rope(x, cos, sin):
    xf = x.astype(jnp.float32)
    x1, x2 = jnp.split(xf, 2, axis=-1)
    return jnp.concatenate([x1 * cos - x2 * sin, x2 * cos + x1 * sin], axis=-1).astype(x.dtype)

def _na_indices(rows):
    kh = min(NA_WIN_ROWS, rows)
    r = np.arange(rows)
    rs = np.clip(r - kh // 2, 0, rows - kh)
    key_r = rs[:, None] + np.arange(kh)[None, :]
    c = np.arange(GRID_W)
    cs = np.clip(c - NA_WIN_COLS // 2, 0, GRID_W - NA_WIN_COLS)
    key_c = cs[:, None] + np.arange(NA_WIN_COLS)[None, :]
    idx = (key_r[:, None, :, None] * GRID_W + key_c[None, :, None, :]).reshape(rows, GRID_W, kh * NA_WIN_COLS)
    dr = key_r - r[:, None] + NA_WIN_ROWS - 1
    dc = key_c - c[:, None] + NA_WIN_COLS - 1
    return (jnp.asarray(idx, jnp.int32), jnp.asarray(dr, jnp.int32), jnp.asarray(dc, jnp.int32))

def _neighbourhood_attention(q, k, v, rpb):
    b, s, h, dh = q.shape
    rows = s // GRID_W
    idx, dr, dc = _na_indices(rows)
    n_keys = idx.shape[-1]
    scale = NA_HEAD_DIM ** -0.5
    q_rows = jnp.moveaxis(q.reshape(b, rows, GRID_W, h, dh), 1, 0)

    def row(args):
        q_r, idx_r, dr_r = args
        kg = jnp.take(k, idx_r, axis=1)
        vg = jnp.take(v, idx_r, axis=1)
        bias = rpb[:, dr_r[None, :, None], dc[:, None, :]].reshape(h, GRID_W, n_keys)
        sc = jnp.einsum('bwhd,bwlhd->bhwl', q_r, kg).astype(jnp.float32) * scale + bias.astype(jnp.float32)[None]
        a = jax.nn.softmax(sc, axis=-1).astype(v.dtype)
        return jnp.einsum('bhwl,bwlhd->bwhd', a, vg)

    out = lax.map(row, (q_rows, idx, dr))
    return jnp.moveaxis(out, 0, 1).reshape(b, s, h * dh)

def _mla_attention(qn, qr, kn, kr, v):
    b, s, h, _ = qn.shape
    nb = s // ATTN_BLOCK
    scale = (MLA_NOPE + MLA_ROPE) ** -0.5
    qn_b = jnp.moveaxis(qn.reshape(b, nb, ATTN_BLOCK, h, MLA_NOPE), 1, 0)
    qr_b = jnp.moveaxis(qr.reshape(b, nb, ATTN_BLOCK, h, MLA_ROPE), 1, 0)

    def blk(args):
        qn_i, qr_i = args
        sc = (jnp.einsum('bqhd,bkhd->bhqk', qn_i, kn)
              + jnp.einsum('bqhr,bkr->bhqk', qr_i, kr)).astype(jnp.float32) * scale
        a = jax.nn.softmax(sc, axis=-1).astype(v.dtype)
        return jnp.einsum('bhqk,bkhd->bqhd', a, v)

    out = lax.map(blk, (qn_b, qr_b))
    return jnp.moveaxis(out, 0, 1).reshape(b, s, h * MLA_V)

def _even_mixer(h, w_in, rpb, dw_w, dw_b, cln_g, cln_b, w_out):
    b, s, _ = h.shape
    z = h @ w_in
    q, k, v, g_a, u_a, u_b, g_b = _split(z, EVEN_SPLITS)
    shp = (b, s, NA_HEADS, NA_HEAD_DIM)
    a_out = _neighbourhood_attention(q.reshape(shp), k.reshape(shp), v.reshape(shp), rpb)
    a_out = a_out * jax.nn.silu(g_a)
    u = u_a * jax.nn.sigmoid(u_b)
    u = lax.conv_general_dilated(u, dw_w[:, None, :], window_strides=(1,),
                                 padding=[(CONV_WIDTH // 2, CONV_WIDTH // 2)],
                                 dimension_numbers=('NWC', 'WIO', 'NWC'),
                                 feature_group_count=CONV_CH) + dw_b
    u = jax.nn.silu(_layernorm(u, cln_g, cln_b)) * jax.nn.silu(g_b)
    return jnp.concatenate([a_out, u], axis=-1) @ w_out

def _odd_mixer(h, w_in, q_norm_g, kv_norm_g, w_uq, w_ukv, w_out):
    b, s, _ = h.shape
    z = h @ w_in
    c_q, c_kv, k_rope, g_c, f_in, g_d = _split(z, ODD_SPLITS)
    pos = jnp.arange(s, dtype=jnp.float32)
    inv_freq = ROPE_THETA ** (-jnp.arange(0, MLA_ROPE, 2, dtype=jnp.float32) / MLA_ROPE)
    ang = pos[:, None] * inv_freq[None, :]
    cos, sin = jnp.cos(ang), jnp.sin(ang)
    q = (_rmsnorm(c_q, q_norm_g) @ w_uq).reshape(b, s, MLA_HEADS, MLA_NOPE + MLA_ROPE)
    qn, qr = q[..., :MLA_NOPE], q[..., MLA_NOPE:]
    qr = _rope(qr, cos[:, None, :], sin[:, None, :])
    kv = (_rmsnorm(c_kv, kv_norm_g) @ w_ukv).reshape(b, s, MLA_HEADS, MLA_NOPE + MLA_V)
    kn, vv = kv[..., :MLA_NOPE], kv[..., MLA_NOPE:]
    kr = _rope(k_rope, cos, sin)
    c_out = _mla_attention(qn, qr, kn, kr, vv) * jax.nn.silu(g_c)
    f = f_in.reshape(b, s, FNET_GROUPS, FNET_GROUP_DIM).astype(jnp.float32)
    f = jnp.fft.fft2(f, axes=(1, 3), norm='ortho').real.reshape(b, s, FNET_W).astype(h.dtype)
    d_out = f * jax.nn.silu(g_d)
    return jnp.concatenate([c_out, d_out], axis=-1) @ w_out

def _trunk(x, p, g_pre, g_post, w_ple, w_ple_gate,
           w_in_e, rpb, dw_w, dw_b, cln_g, cln_b, w_out_e,
           w_in_o, q_norm_g, kv_norm_g, w_uq, w_ukv, w_out_o):
    for i in range(DEPTH):
        h = _rmsnorm(x, g_pre[i])
        j = i // 2
        if i % 2 == 0:
            o = _even_mixer(h, w_in_e[j], rpb[j], dw_w[j], dw_b[j], cln_g[j], cln_b[j], w_out_e[j])
        else:
            o = _odd_mixer(h, w_in_o[j], q_norm_g[j], kv_norm_g[j], w_uq[j], w_ukv[j], w_out_o[j])
        x = x + _rmsnorm(o, g_post[i])
        x = x + jax.nn.sigmoid(x @ w_ple_gate[i]) * (p[i] @ w_ple[i])
    return x

def setup_inputs(seed: int = 0) -> dict:
    key = jax.random.key(seed)
    ks = jax.random.split(key, 24)
    f32 = jnp.float32

    def nrm(k, shape, fan_in):
        return jax.random.normal(k, shape, f32) * (fan_in ** -0.5)

    def gain(k, shape):
        return 1.0 + 0.02 * jax.random.normal(k, shape, f32)

    return {
        "x_prompt": jax.random.normal(ks[0], (BATCH, SEQ, D_MODEL), f32),
        "x_sample": jax.random.normal(ks[1], (DEC_BATCH, DEC_SEQ, D_MODEL), f32),
        "p_prompt": jax.random.normal(ks[2], (DEPTH, BATCH, SEQ, PLE_DIM), f32),
        "p_sample": jax.random.normal(ks[3], (DEPTH, DEC_BATCH, DEC_SEQ, PLE_DIM), f32),
        "g_pre": gain(ks[4], (DEPTH, D_MODEL)),
        "g_post": gain(ks[5], (DEPTH, D_MODEL)),
        "w_ple": nrm(ks[6], (DEPTH, PLE_DIM, D_MODEL), PLE_DIM),
        "w_ple_gate": nrm(ks[7], (DEPTH, D_MODEL, D_MODEL), D_MODEL),
        "w_in_e": nrm(ks[8], (N_EVEN, D_MODEL, EVEN_IN), D_MODEL),
        "rpb": 0.1 * jax.random.normal(ks[9], (N_EVEN, NA_HEADS, 2 * NA_WIN_ROWS - 1, 2 * NA_WIN_COLS - 1), f32),
        "dw_w": nrm(ks[10], (N_EVEN, CONV_WIDTH, CONV_CH), CONV_WIDTH),
        "dw_b": 0.02 * jax.random.normal(ks[11], (N_EVEN, CONV_CH), f32),
        "cln_g": gain(ks[12], (N_EVEN, CONV_CH)),
        "cln_b": 0.02 * jax.random.normal(ks[13], (N_EVEN, CONV_CH), f32),
        "w_out_e": nrm(ks[14], (N_EVEN, NA_W + CONV_CH, D_MODEL), NA_W + CONV_CH),
        "w_in_o": nrm(ks[15], (N_ODD, D_MODEL, ODD_IN), D_MODEL),
        "q_norm_g": gain(ks[16], (N_ODD, Q_LORA)),
        "kv_norm_g": gain(ks[17], (N_ODD, KV_LORA)),
        "w_uq": nrm(ks[18], (N_ODD, Q_LORA, MLA_HEADS * (MLA_NOPE + MLA_ROPE)), Q_LORA),
        "w_ukv": nrm(ks[19], (N_ODD, KV_LORA, MLA_HEADS * (MLA_NOPE + MLA_V)), KV_LORA),
        "w_out_o": nrm(ks[20], (N_ODD, MLA_W + FNET_W, D_MODEL), MLA_W + FNET_W),
    }

def reference(x_prompt, x_sample, p_prompt, p_sample, g_pre, g_post, w_ple, w_ple_gate,
              w_in_e, rpb, dw_w, dw_b, cln_g, cln_b, w_out_e,
              w_in_o, q_norm_g, kv_norm_g, w_uq, w_ukv, w_out_o):
    y_prompt = _trunk(x_prompt, p_prompt, g_pre, g_post, w_ple, w_ple_gate,
                      w_in_e, rpb, dw_w, dw_b, cln_g, cln_b, w_out_e,
                      w_in_o, q_norm_g, kv_norm_g, w_uq, w_ukv, w_out_o)
    y_sample = _trunk(x_sample, p_sample, g_pre, g_post, w_ple, w_ple_gate,
                      w_in_e, rpb, dw_w, dw_b, cln_g, cln_b, w_out_e,
                      w_in_o, q_norm_g, kv_norm_g, w_uq, w_ukv, w_out_o)
    return (y_prompt, y_sample)


_drawn_inputs = setup_inputs


def setup_inputs(seed=0):
    import zlib

    import numpy as np

    out = dict(_drawn_inputs(seed))
    spreads = {}
    factors = {'g_post': 2.951,
     'rpb': 3.265,
     'cln_g': 3.467,
     'cln_b': 3.714,
     'q_norm_g': 8.0,
     'kv_norm_g': 8.0}
    for name, (base, spread) in spreads.items():
        noise = np.random.default_rng([zlib.crc32(name.encode()), seed]).standard_normal(out[name].shape)
        drawn = base * np.exp(spread * noise) if base else spread * noise
        out[name] = __import__('jax').numpy.asarray(drawn.astype(out[name].dtype))
    for name, factor in factors.items():
        out[name] = (out[name] * factor).astype(out[name].dtype)
    return out
```

```python
from contextlib import ExitStack

import concourse.bass as bass
from concourse import mybir
import numpy as np

F32 = mybir.dt.float32
F32R = mybir.dt.float32r
ALU = mybir.AluOpType
ACT = mybir.ActivationFunctionType
AX = mybir.AxisListType

P = 128
D = 1024
SEQS = (1024, 512)
TOK = sum(SEQS)
NT = TOK // P
NB = TOK // 512
KC = D // P
HALF = 512
HEADS = 8
DH = 64
ROPE = 32
PLE = 256
GRID = 64
TAPS = 31
PAD = TAPS // 2
EPS = 1e-6
BIG = 1e30
PAIRCOLS = KC * HALF
QCOLS = PAIRCOLS // 4

PAIRS = ["ple0_w", "ple0_p", "ple1_w", "ple1_p",
         "u0", "q", "v", "u1", "k", "ga", "gb",
         "out0_a", "out0_b", "gate0_a", "gate0_b",
         "lat", "gc", "f", "gd",
         "up", "dft",
         "out1_a", "out1_b", "gate1_a", "gate1_b"]
PIDX = {n: i for i, n in enumerate(PAIRS)}
QUARTERS = [{"w": 3, "p": 2}[n[-1]] if n.startswith("ple") else 4 for n in PAIRS]
QBASE = [sum(QUARTERS[:i]) for i in range(len(PAIRS) + 1)]

THREE = ((0, 0), (0, 1), (1, 0))


class Ctx:

    def __init__(self, nc, stack):
        self.nc = nc
        self.stack = stack
        self.sems = []

    def block(self, name):
        self.cm = self.nc.Block()
        self.cur = self.cm.__enter__()
        return self.cur

    def end(self):
        self.cm.__exit__(None, None, None)

    def sem(self, name):
        s = self.nc.alloc_semaphore(name=name)
        self.sems.append(s)
        return s

    def renew_semaphores(self):
        self.nc.clear_and_free_semaphores(self.sems)
        self.nc.all_engine_barrier()
        self.sems = []

    def dram(self):
        d = lambda name, *shape: self.nc.dram_tensor(name, list(shape), F32).ap()
        self.ple = [d(f"ple{l}", TOK, D) for l in range(2)]
        self.q = d("q_parts", 2, HALF, TOK)
        self.k = d("k_parts", 2, HALF, TOK)
        self.v = d("v_parts", 2, TOK, HALF)
        self.gate_a = d("gate_a", TOK, HALF)
        self.gate_b = d("gate_b", TOK, HALF)
        self.bias = d("bias_by_distance", HEADS, P, 14 * GRID)
        self.conv = d("conv_fm", 4, P, TOK)
        self.attn = [d(f"attn{l}", TOK, HALF) for l in range(2)]
        self.o = d("o_half", TOK, HALF)
        self.x1 = d("x1", TOK, D)
        self.x2 = d("x2", TOK, D)
        self.lat = d("latents", TOK, HALF)
        self.gate_c = d("gate_c", TOK, HALF)
        self.f = d("f_fm", 4, P, TOK)
        self.gate_d = d("gate_d_fm", 4, P, TOK)
        self.qs = d("mla_q", HEADS, P, TOK)
        self.kn = d("mla_kn", HEADS, DH, TOK)
        self.kr = d("mla_kr", ROPE, TOK)
        self.vv = d("mla_v", TOK, HALF)
        self.dmix = d("fnet_out", 4, P, TOK)

    def sb(self, name, shape, dt=F32):
        return self.stack.enter_context(self.nc.sbuf_tensor(name, shape, dt))


def tiles_of(ap, t):
    return ap[t * P:(t + 1) * P, :]



def load_quarter(g, sp, n):
    pair = max(i for i in range(len(PAIRS)) if QBASE[i] <= n)
    off = (n - QBASE[pair]) * QCOLS
    if n >= 2:
        sp.wait_ge(g.w_ready, n - 1)
    sp.dma_start(g.raw[:, n % 2, :], g.wall[pair, :, off:off + QCOLS]).then_inc(g.raw_loaded[n % 2], 16)


def split_quarter(g, pool, n):
    pair = max(i for i in range(len(PAIRS)) if QBASE[i] <= n)
    off = (n - QBASE[pair]) * QCOLS
    hi = g.W[0][:, pair % 2, off:off + QCOLS]
    lo = g.W[1][:, pair % 2, off:off + QCOLS]
    raw = g.raw[:, n % 2, :]
    pool.wait_ge(g.raw_loaded[n % 2], 16 * (n // 2 + 1))
    pool.tensor_tensor(hi, raw, g.zero[:, 0:1].broadcast_to([P, QCOLS]), ALU.add).then_inc(g.w_hi, 1)
    pool.wait_ge(g.w_hi, n + 1)
    pool.tensor_tensor(lo, raw, hi.bitcast(F32), ALU.subtract).then_inc(g.w_ready, 1)


def quarters(name):
    i = PIDX[name]
    return range(QBASE[i], QBASE[i + 1])


def wait_pair(g, pe, name):
    pe.wait_ge(g.w_ready, QBASE[PIDX[name] + 1])


def w_at(g, name, part, lo, n):
    return g.W[part][:, PIDX[name] % 2, lo:lo + n]


def rms_scale(pool, g, ss, n, done, base):
    w = ss.shape[-1]
    pool.tensor_scalar(ss, ss, 1.0 / n, EPS, ALU.mult, ALU.add).then_inc(done, 1)
    pool.wait_ge(done, base + 1)
    pool.tensor_tensor(ss, ss, g.mhalf[:, 0:1].broadcast_to([P, w]), ALU.pow).then_inc(done, 1)



def prologue(g):
    nc = g.nc
    with ExitStack() as st:
        sb = lambda name, shape, dt=F32: st.enter_context(nc.sbuf_tensor(name, shape, dt))
        xb = sb("pro_x", [P, 2, 4, D])
        gpre = sb("pro_gpre", [P, KC])
        stage = sb("pro_stage", [P, 4, HALF])
        ss = sb("pro_ss", [P, NT])
        ps = st.enter_context(nc.psum_tensor("pro_ps", [P, 4, HALF], F32))
        pt = st.enter_context(nc.psum_tensor("pro_pt", [P, 2, HALF], F32))
        junk = st.enter_context(nc.psum_tensor("pro_junk", [P, D], F32))
        ident_in, x_in, gpre_in = g.sem("ident_in"), [g.sem(f"pro_x_in{i}") for i in range(3)], g.sem("pro_gpre_in")
        zeroed = g.sem("zeroed")
        ple_mm = g.sem("ple_mm")
        ple_out = [g.sem("ple_out_act"), g.sem("ple_out_dve")]
        stored = [g.sem(f"ple_stored{i}") for i in range(4)]
        squared, scaled, scaling, htr, h_hi, h_lo = [g.sem("pro_" + n) for n in ("squared", "scaled", "scaling", "htr", "h_hi", "h_lo")]
        NPL = 2 * NT
        NH = KC * NB
        N1, N2 = QBASE[2], QBASE[4]

        @g.block("prologue").sync
        def _(sp):
            def store(u):
                l, t, c = u // NPL, u // 2 % NT, u % 2
                sp.wait_ge(ple_out[u % 2], u // 2 + 1)
                sp.dma_start(tiles_of(g.ple[l], t)[:, c * HALF:(c + 1) * HALF], stage[:, u % 4]).then_inc(stored[u % 4], 16)

            load_quarter(g, sp, 0)
            load_quarter(g, sp, 1)
            for n in range(2, N1):
                load_quarter(g, sp, n)
            sp.dma_start(xb[:, 0], g.x[0:512, :].rearrange("(t p) d -> p t d", p=P)).then_inc(x_in[0], 16)
            sp.dma_start(g.ident[:], g.c_ident).then_inc(ident_in, 16)
            sp.dma_start(gpre[:], g.g_pre_cols).then_inc(gpre_in, 16)
            sp.dma_start(xb[:, 1], g.x[512:1024, :].rearrange("(t p) d -> p t d", p=P)).then_inc(x_in[1], 16)
            load_quarter(g, sp, N1)
            load_quarter(g, sp, N1 + 1)
            for u in range(NPL):
                store(u)
            for n in range(N1 + 2, N2):
                load_quarter(g, sp, n)
            sp.wait_ge(htr, KC)
            sp.dma_start(xb[:, 0], g.x[1024:TOK, :].rearrange("(t p) d -> p t d", p=P)).then_inc(x_in[2], 16)
            load_quarter(g, sp, N2)
            load_quarter(g, sp, N2 + 1)
            for u in range(NPL, 2 * NPL):
                store(u)
            load_quarter(g, sp, N2 + 2)
            load_quarter(g, sp, N2 + 3)
            for i in range(4):
                sp.wait_ge(stored[i], 16 * (2 * NPL // 4))

        @g.cur.gpsimd
        def _(pool):
            pool.memset(g.zero[:], 0.0).then_inc(zeroed, 1)
            pool.memset(g.mhalf[:], -0.5).then_inc(zeroed, 1)
            pool.wait_ge(zeroed, 2)
            for b in range(3):
                pool.wait_ge(squared, 4 * (b + 1))
                rms_scale(pool, g, ss[:, 4 * b:4 * b + 4], D, scaling, 2 * b)

        def part_of(n, part):
            pair = max(i for i in range(len(PAIRS)) if QBASE[i] <= n)
            off = (n - QBASE[pair]) * QCOLS
            return g.W[part][:, pair % 2, off:off + QCOLS]

        @g.cur.scalar
        def _(act):
            def squares(b):
                act.wait_ge(x_in[b], 16)
                for j in range(4):
                    if 4 * b + j:
                        act.wait_ge(squared, 4 * b + j)
                    act.activation(junk[:], xb[:, b % 2, j], ACT.Square, accum_out=ss[:, 4 * b + j:4 * b + j + 1]).then_inc(squared, 1)

            def split_hi(n):
                act.wait_ge(g.raw_loaded[n % 2], 16 * (n // 2 + 1))
                act.copy(part_of(n, 0), g.raw[:, n % 2]).then_inc(g.w_hi, 1)

            def half_row(u):
                act.wait_ge(ple_mm, u + 1)
                if u >= 4:
                    act.wait_ge(stored[u % 4], 16 * (u // 4))
                act.copy(stage[:, u % 4], ps[:, u % 4]).then_inc(ple_out[0], 1)

            for n in range(N1):
                split_hi(n)
            squares(0)
            for u in range(0, NPL, 2):
                half_row(u)
                if u == 12:
                    squares(1)
            act.wait_ge(ple_mm, NPL)
            act.wait_ge(gpre_in, 16)
            for v in range(NH):
                k, b = v % KC, v // KC
                act.wait_ge(htr, v + 1)
                act.activation(g.XT[0][:, k, b * 512:(b + 1) * 512], pt[:, v % 2], ACT.Copy,
                               scale=gpre[:, k:k + 1]).then_inc(h_hi, 1)
                if v % 2 == 1 and v // 2 < N2 - N1:
                    split_hi(N1 + v // 2)
                if v == 13:
                    squares(2)
            for u in range(NPL, 2 * NPL, 2):
                half_row(u)
            act.wait_ge(ple_mm, 2 * NPL)
            for n in range(N2, N2 + 4):
                split_hi(n)

        @g.cur.vector
        def _(dve):
            def split_lo(n):
                dve.wait_ge(g.w_hi, n + 1)
                dve.tensor_tensor(part_of(n, 1), g.raw[:, n % 2], part_of(n, 0).bitcast(F32),
                                  ALU.subtract).then_inc(g.w_ready, 1)

            def scale_rows(b):
                dve.wait_ge(scaling, 2 * (b + 1))
                for j in range(4):
                    dve.tensor_scalar(xb[:, b % 2, j], xb[:, b % 2, j], ss[:, 4 * b + j:4 * b + j + 1], None,
                                      ALU.mult).then_inc(scaled, 1)

            def half_row(u):
                dve.wait_ge(ple_mm, u + 1)
                if u >= 4:
                    dve.wait_ge(stored[u % 4], 16 * (u // 4))
                dve.tensor_copy(stage[:, u % 4], ps[:, u % 4]).then_inc(ple_out[1], 1)

            for n in range(N1):
                split_lo(n)
            for u in range(1, NPL, 2):
                half_row(u)
                if u == 9:
                    scale_rows(0)
            scale_rows(1)
            for v in range(NH):
                k, b = v % KC, v // KC
                dve.wait_ge(h_hi, v + 1)
                dve.scalar_tensor_tensor(g.XT[1][:, k, b * 512:(b + 1) * 512], pt[:, v % 2], gpre[:, k:k + 1],
                                         g.XT[0][:, k, b * 512:(b + 1) * 512].bitcast(F32),
                                         ALU.mult, ALU.subtract).then_inc(h_lo, 1)
                if v % 2 == 1 and v // 2 < N2 - N1:
                    split_lo(N1 + v // 2)
                if v == 14:
                    scale_rows(2)
            for u in range(NPL + 1, 2 * NPL, 2):
                half_row(u)
            for n in range(N2, N2 + 4):
                split_lo(n)

        @g.cur.tensor
        def _(pe):
            for l in range(2):
                wait_pair(g, pe, f"ple{l}_p")
                for u in range(l * NPL, (l + 1) * NPL):
                    t, c = u // 2 % NT, u % 2
                    if u >= 4:
                        pe.wait_ge(ple_out[u % 2], (u - 4) // 2 + 1)
                    i = 0
                    for k in range(2):
                        for a, m in THREE:
                            if t < 8:
                                lhs = w_at(g, f"ple{l}_p", a, k * 1024 + t * P, P)
                            else:
                                lhs = w_at(g, f"ple{l}_w", a, 2048 + k * 512 + (t - 8) * P, P)
                            mm = pe.matmul(ps[:, u % 4], lhs, w_at(g, f"ple{l}_w", m, k * 1024 + c * HALF, HALF),
                                           start=i == 0, stop=i == 5)
                            i += 1
                    mm.then_inc(ple_mm, 1)
                if l == 0:
                    pe.wait_ge(ident_in, 16)
                    for v in range(NH):
                        k, b = v % KC, v // KC
                        pe.wait_ge(scaled, 4 * (b + 1))
                        if v >= 2:
                            pe.wait_ge(h_lo, v - 1)
                        for j in range(4):
                            tr = pe.transpose(pt[:, v % 2, j * P:(j + 1) * P], xb[:, b % 2, j, k * P:(k + 1) * P], g.ident[:])
                        tr.then_inc(htr, 1)
        g.end()



UOFF = (PAD, PAD + 512, 2 * PAD + 1024)
UW = 3 * PAD + TOK
CW = PAD + TOK


def project(g, pe, name, fm, order, psum, unit0, free, done, banks=8):
    wait_pair(g, pe, name)
    for j in range(12):
        u = unit0 + j
        free(pe, u)
        i = 0
        for k in range(KC):
            for a, m in THREE:
                if fm:
                    c, b = order[j]
                    mm = pe.matmul(psum[:, u % banks], w_at(g, name, a, k * HALF + c * P, P),
                                   g.XT[m][:, k, b * 512:(b + 1) * 512], start=i == 0, stop=i == 3 * KC - 1)
                else:
                    mm = pe.matmul(psum[:, u % banks], g.XT[a][:, k, j * P:(j + 1) * P],
                                   w_at(g, name, m, k * HALF, HALF), start=i == 0, stop=i == 3 * KC - 1)
                i += 1
        mm.then_inc(done, 1)


FM_ORDER = [(c, b) for c in range(4) for b in range(NB)]
U_ORDER = [(2 * cc + s, b) for cc in range(2) for b in range(NB) for s in range(2)]


def in_even(g):
    nc = g.nc
    names = ["u0", "q", "v", "u1", "k", "ga", "gb"]
    with ExitStack() as st:
        sb = lambda name, shape, dt=F32: st.enter_context(nc.sbuf_tensor(name, shape, dt))
        stage = sb("ie_stage", [P, 4, HALF])
        stage_hi = sb("ie_stage_hi", [P, 4, HALF], F32R)
        th = sb("ie_tanh", [P, 2, HALF])
        ubuf = sb("ie_u", [P, 2, UW])
        acc = sb("ie_acc", [P, CW])
        wconv = sb("ie_wconv", [P, 4, TAPS + 1])
        ps = st.enter_context(nc.psum_tensor("ie_ps", [P, 8, HALF], F32))
        mm_done, cw_in, bias_out = g.sem("ie_mm"), g.sem("ie_cw_in"), g.sem("ie_bias_out")
        ev_act, ev_dve, tanhed = g.sem("ie_ev_act"), g.sem("ie_ev_dve"), g.sem("ie_tanhed")
        stored = [g.sem(f"ie_stored{i}") for i in range(4)]
        hi_stored = [g.sem(f"ie_hi_stored{i}") for i in range(4)]
        taps, conv_stored, padded = g.sem("ie_taps"), g.sem("ie_conv_stored"), g.sem("ie_padded")

        kinds = []
        for n in names:
            for j in range(12):
                kinds.append("tanh_u" if n[0] == "u" and j % 2 == 0 else "u" if n[0] == "u" else
                             "gate" if n[0] == "g" else "copy")
        by_act = [0]
        by_dve = [0]
        slot = []
        for kd in kinds:
            by_act.append(by_act[-1] + (kd in ("tanh_u", "copy")))
            by_dve.append(by_dve[-1] + (kd != "tanh_u"))
            slot.append(sum(x in ("copy", "gate") for x in kinds[:len(slot)]) if kd in ("copy", "gate") else None)
        n_tanh = [sum(x in ("tanh_u", "gate") for x in kinds[:i]) for i in range(len(kinds) + 1)]
        tanh_used = [by_dve[u + 1 + (kd == "tanh_u")] for u, kd in enumerate(kinds) if kd in ("tanh_u", "gate")]

        CONV_IN = [6, 12, 42, 48]
        TAPS_A_UNIT = 2
        order, cc, s, rest = [], 0, 0, 0
        conv_end = []
        for u in range(len(kinds)):
            order.append(("unit", u))
            if u < rest:
                continue
            for _ in range(TAPS_A_UNIT):
                if cc < 4 and u + 1 >= CONV_IN[cc] and u >= rest:
                    order.append(("tap", (cc, s)))
                    s += 1
                    if s > TAPS:
                        conv_end.append(u)
                        cc, s, rest = cc + 1, 0, u + 2

        SCALE = {"q": -DH ** -0.5, "v": 0.5, "k": 1.0}

        def free(pe, u):
            if u >= 8:
                if kinds[u - 8] == "tanh_u":
                    pe.wait_ge(ev_act, by_act[u - 7])
                else:
                    pe.wait_ge(ev_dve, by_dve[u - 7])

        def dest(u, part):
            n, j = names[u // 12], u % 12
            if n in ("q", "k"):
                c, b = FM_ORDER[j]
                return (g.q if n == "q" else g.k)[part, c * P:(c + 1) * P, b * 512:(b + 1) * 512]
            return tiles_of(g.v[part] if n == "v" else g.gate_a if n == "ga" else g.gate_b, j)

        def store_conv(sp, cc):
            sp.wait_ge(taps, (TAPS + 1) * (cc + 1))
            sp.dma_start(g.conv[cc, :, 0:1024], acc[:, 0:1024]).then_inc(conv_stored, 16)
            sp.dma_start(g.conv[cc, :, 1024:TOK], acc[:, 1024 + PAD:CW]).then_inc(conv_stored, 16)

        @g.block("in_even").sync
        def _(sp):
            sp.dma_start(wconv[:], g.dw).then_inc(cw_in, 16)
            for h in range(HEADS):
                for j in range(2):
                    row = g.rpb[h, 1 - j]
                    src = bass.AP(tensor=row.tensor, offset=row.offset + GRID - 1, ap=[[P, 14], [-1, GRID], [1, GRID]])
                    sp.dma_start(g.bias[h, j * GRID:(j + 1) * GRID, :].rearrange("c (d k) -> d c k", k=GRID),
                                 src).then_inc(bias_out, 16)
            for u, kd in enumerate(kinds):
                n, j = names[u // 12], u % 12
                i = PIDX[n]
                if j % 2 == 0 and j < 8 and i + 1 < PIDX["out0_a"]:
                    load_quarter(g, sp, QBASE[i + 1] + j // 2)
                if kd in ("copy", "gate"):
                    sp.wait_ge(ev_dve, by_dve[u + 1])
                    sp.dma_start(dest(u, 1), stage[:, slot[u] % 4]).then_inc(stored[slot[u] % 4], 16)
                    if kd == "copy":
                        sp.dma_start(dest(u, 0), stage_hi[:, slot[u] % 4].bitcast(F32)).then_inc(hi_stored[slot[u] % 4], 16)
                if u in conv_end:
                    store_conv(sp, conv_end.index(u))
            for i in range(4):
                sp.wait_ge(stored[i], 16 * (sum(x in ("copy", "gate") for x in kinds) // 4))
                sp.wait_ge(hi_stored[i], 16 * (kinds.count("copy") // 4))
            sp.wait_ge(conv_stored, 16 * 8)
            sp.wait_ge(bias_out, 16 * 2 * HEADS)

        @g.cur.gpsimd
        def _(pool):
            for i, n in enumerate(names[:-1]):
                for q in quarters(names[i + 1]):
                    if i >= 1 and q == QBASE[PIDX[names[i + 1]]]:
                        pool.wait_ge(mm_done, 12 * i)
                    split_quarter(g, pool, q)

        @g.cur.scalar
        def _(act):
            for u, kd in enumerate(kinds):
                if kd == "u":
                    continue
                act.wait_ge(mm_done, u + 1)
                if kd in ("tanh_u", "gate"):
                    i = n_tanh[u]
                    if i >= 2:
                        act.wait_ge(ev_dve, tanh_used[i - 2])
                    w = act.activation(th[:, i % 2], ps[:, u % 8], ACT.Tanh, scale=0.5)
                    w.then_inc(tanhed if kd == "gate" else ev_act, 1)
                else:
                    s = slot[u]
                    if s >= 4:
                        act.wait_ge(hi_stored[s % 4], 16 * (s // 4))
                    act.activation(stage_hi[:, s % 4], ps[:, u % 8], ACT.Copy, scale=SCALE[names[u // 12]]).then_inc(ev_act, 1)

        @g.cur.vector
        def _(dve):
            dve.memset(ubuf[:], 0.0).then_inc(padded, 1)
            dve.wait_ge(padded, 1)

            def u_unit(u):
                n, j = names[u // 12], u % 12
                cc = 2 * (n == "u1") + j // 6
                b = j // 2 % 3
                dve.wait_ge(mm_done, u + 1)
                dve.wait_ge(ev_act, by_act[u])
                i = n_tanh[u] - 1
                dve.scalar_tensor_tensor(ubuf[:, cc % 2, UOFF[b]:UOFF[b] + 512], th[:, i % 2], 1.0, ps[:, u % 8],
                                         ALU.add, ALU.mult).then_inc(ev_dve, 1)

            def gate_unit(u):
                s = slot[u]
                i = n_tanh[u]
                dve.wait_ge(tanhed, 1 + sum(x == "gate" for x in kinds[:u]))
                if s >= 4:
                    dve.wait_ge(stored[s % 4], 16 * (s // 4))
                dve.scalar_tensor_tensor(stage[:, s % 4], th[:, i % 2], 1.0, ps[:, u % 8],
                                         ALU.add, ALU.mult).then_inc(ev_dve, 1)

            def conv_step(cc, s):
                base = (TAPS + 1) * cc + s
                if s == 0:
                    dve.wait_ge(ev_dve, by_dve[CONV_IN[cc]])
                    if cc == 0:
                        dve.wait_ge(cw_in, 16)
                    else:
                        dve.wait_ge(conv_stored, 32 * cc)
                    dve.tensor_scalar(acc[:], ubuf[:, cc % 2, 0:CW], wconv[:, cc, 0:1], None, ALU.mult).then_inc(taps, 1)
                    return
                dve.wait_ge(taps, base)
                if s < TAPS:
                    dve.scalar_tensor_tensor(acc[:], ubuf[:, cc % 2, s:s + CW], wconv[:, cc, s:s + 1], acc[:],
                                             ALU.mult, ALU.add).then_inc(taps, 1)
                else:
                    dve.tensor_scalar(acc[:], acc[:], 0.5, wconv[:, cc, TAPS:TAPS + 1], ALU.mult, ALU.add).then_inc(taps, 1)

            def lo_unit(u):
                sl = slot[u] % 4
                dve.wait_ge(ev_act, by_act[u + 1])
                if slot[u] >= 4:
                    dve.wait_ge(stored[sl], 16 * (slot[u] // 4))
                dve.scalar_tensor_tensor(stage[:, sl], ps[:, u % 8], SCALE[names[u // 12]], stage_hi[:, sl].bitcast(F32),
                                         ALU.mult, ALU.subtract).then_inc(ev_dve, 1)

            steps = {"u": u_unit, "gate": gate_unit, "copy": lo_unit, "tanh_u": lambda u: None}
            for what, arg in order:
                if what == "unit":
                    steps[kinds[arg]](arg)
                else:
                    conv_step(*arg)

        @g.cur.tensor
        def _(pe):
            for i, n in enumerate(names):
                project(g, pe, n, n[0] in "uqk", U_ORDER if n[0] == "u" else FM_ORDER, ps, 12 * i, free, mm_done)
        g.end()



class Tile:
    def __init__(self, i):
        base, rows, r = (0, 16, 2 * i) if i < 8 else (8, 8, 2 * (i - 8))
        self.shifted = rows > 8 and 4 <= r <= 10
        first = r - 4 if self.shifted else min(max(r - 4, 0), rows - 8)
        self.width = 10 * GRID if self.shifted else 8 * GRID
        self.key0 = base * P + first * GRID
        self.chunk0 = base + first // 2
        self.table = (first - r + 6) * GRID
        self.batches = (3, 2) if self.shifted else (4,)


NA_TILES = [Tile(i) for i in range(NT)]
NA_GROUP0 = [min(NA_TILES[2 * q].chunk0, NA_TILES[2 * q + 1].chunk0) for q in range(NT // 2)]
NA_SPAN = [6 if NA_TILES[2 * q].shifted else 4 for q in range(NT // 2)]
NG = NT // 2
NBAT = sum(len(t.batches) for t in NA_TILES)


class Pipeline:

    CREDITS = {"scored": 0, "minned": 2, "exped": 0, "turned": 3, "hi": 0, "lo": 2, "weighed": NG + 1,
              "copied": 1, "back": 2, "reduced": 1, "inverted": 0, "normed": 0, "prepped": 1}

    def __init__(self, g, name, **credits):
        self.CREDIT = {**self.CREDITS, **credits}
        self.sems = {n: g.sem(f"{name}_{n}") for n in self.CREDIT}

    def __getitem__(self, name):
        return self.sems[name]

    def give(self, eng, *names):
        for n in names:
            if self.CREDIT[n]:
                eng.sem_inc(self[n], self.CREDIT[n])

    def wait(self, eng, name, count):
        eng.wait_ge(self[name], count + self.CREDIT[name])


J = 2 * NT
DRAIN = 10


def pair_loop(eng, body):
    body(0, range(J), lambda i: 0 <= i < J)
    with eng.Fori(1, HEADS // 2) as pair:
        body(pair * 2, range(J), lambda i: True)
    body(HEADS - 2, range(J, J + DRAIN), lambda i: i < J)


def attention_tail(g, pl, ps_pv, ps_back, pv_sb, sums, rinv, red, out):
    def act_copy(act, h6, q):
        pl.wait(act, "weighed", h6 + q + 1)
        pl.wait(act, "back", h6 + q - 1)
        act.copy(pv_sb[:, q % 2], ps_pv[:, 0:256]).then_inc(pl["copied"], 1)

    def pe_back(pe, h6, q):
        pl.wait(pe, "copied", h6 + q + 1)
        pl.wait(pe, "reduced", h6 + q)
        for a in range(2):
            tr = pe.transpose(ps_back[:, a * P:(a + 1) * P], pv_sb[:, q % 2, a * P:(a + 1) * P], g.ident[:])
        tr.then_inc(pl["back"], 1)

    def dve_add(dve, h6, q):
        dve.reciprocal(rinv[:, q % 2], sums[:, q % NG]).then_inc(pl["inverted"], 1)
        pl.wait(dve, "back", h6 + q + 1)
        dve.tensor_reduce(red[:, q % 2], ps_back[:, 0:256].rearrange("p (a two d) -> p a d two", a=2, two=2), AX.X,
                          ALU.add).then_inc(pl["reduced"], 1)

    def dve_norm(dve, h6, q, dst):
        pl.wait(dve, "reduced", h6 + q + 1)
        pl.wait(dve, "inverted", h6 + q + 1)
        dve.tensor_tensor(dst, red[:, q % 2], rinv[:, q % 2].rearrange("p (a o) -> p a o", o=1).broadcast_to([P, 2, DH]),
                          ALU.mult).then_inc(pl["normed"], 1)
    return act_copy, pe_back, dve_add, dve_norm


def natten(g):
    nc = g.nc
    with ExitStack() as st:
        sb = lambda name, shape, dt=F32: st.enter_context(nc.sbuf_tensor(name, shape, dt))
        xt = sb("na_xt", [P, 2, 14 * GRID])
        Q = sb("na_q", [P, 2, TOK], F32R)
        K = [sb("na_k_hi", [P, 2, TOK], F32R), sb("na_k_lo", [P, 2, TOK], F32R)]
        V = sb("na_v", [P, 2, NT, P], F32R)
        T = sb("na_table", [P, 2, 14 * GRID])
        TS = sb("na_table_shifted", [P, 2, 10 * GRID])
        cmask, imask = sb("na_cmask", [P, GRID]), sb("na_imask", [P, 10 * GRID])
        S = sb("na_s", [P, 3, 10 * GRID])
        mins, tick = sb("na_min", [P, 3]), sb("na_tick", [P, 3])
        sums = sb("na_sums", [P, NG, 2])
        rinv = sb("na_rinv", [P, 2, 2])
        red = sb("na_red", [P, 2, 2, DH])
        PT = [sb("na_pt_hi", [P, 2, 6, 256], F32R), sb("na_pt_lo", [P, 2, 6, 256], F32R)]
        pv_sb = sb("na_pv", [P, 2, 256])
        out = sb("na_out", [P, NT, HALF])
        ps_s = st.enter_context(nc.psum_tensor("na_ps_s", [P, 2, 2, HALF], F32))
        ps_t = st.enter_context(nc.psum_tensor("na_ps_t", [P, 2, HALF], F32))
        ps_pv = st.enter_context(nc.psum_tensor("na_ps_pv", [P, HALF], F32))
        ps_back = st.enter_context(nc.psum_tensor("na_ps_back", [P, HALF], F32))
        pl = Pipeline(g, "na")
        qkv_in, xt_in = [g.sem("na_qkv_in0"), g.sem("na_qkv_in1")], [g.sem("na_xt_in0"), g.sem("na_xt_in1")]
        QKV_IN = 16 * 8
        masks_in, cleared, attn_out = g.sem("na_masks_in"), g.sem("na_cleared"), g.sem("na_attn_out")
        act_copy, pe_back, dve_add, dve_norm = attention_tail(g, pl, ps_pv, ps_back, pv_sb, sums, rinv, red, out)

        def bat(j):
            return 2 * NBAT * (j // J) + sum(len(NA_TILES[i % NT].batches) for i in range(j % J))

        @g.block("natten").sync
        def _(sp):
            def load(h, s):
                rows = lambda ap, part: ap[part].rearrange("(h d) t -> h d t", d=DH)[h]
                half = lambda i: slice(i * DH, (i + 1) * DH)
                vcols = half(h) if isinstance(h, int) else bass.ds(h * DH, DH)
                for i in range(2):
                    sp.dma_start(Q[half(i), s].bitcast(F32), rows(g.q, i)).then_inc(qkv_in[s], 16)
                    for part in range(2):
                        sp.dma_start(K[part][half(i), s].bitcast(F32), rows(g.k, part)).then_inc(qkv_in[s], 16)
                sp.dma_start(xt[:, s], g.bias[h]).then_inc(xt_in[s], 16)
                for part in range(2):
                    sp.dma_start(V[:, s, :, half(part)].bitcast(F32),
                                 g.v[part].rearrange("(t p) c -> p t c", p=P)[:, :, vcols]).then_inc(qkv_in[s], 16)

            def store(cols):
                sp.dma_start(g.attn[0].rearrange("(t p) c -> p t c", p=P)[:, :, cols], out[:, :, cols]).then_inc(attn_out, 16)

            sp.dma_start(cmask[:], g.c_cmask).then_inc(masks_in, 16)
            load(0, 0)
            sp.dma_start(imask[:], g.c_imask).then_inc(masks_in, 16)
            load(1, 1)
            with sp.Fori(0, HEADS // 2 - 1) as pair:
                for s in range(2):
                    pl.wait(sp, "weighed", pair * 2 * NG + (s + 1) * NG)
                    load(pair * 2 + (s + 2), s)
                pl.wait(sp, "normed", pair * 2 * NG + 2 * NG)
                store(bass.ds(pair * 2 * DH, 2 * DH))
            for n in list(quarters("out0_a")) + list(quarters("out0_b")):
                load_quarter(g, sp, n)
            pl.wait(sp, "normed", HEADS * NG)
            store(slice(HALF - 2 * DH, HALF))
            sp.wait_ge(attn_out, 16 * HEADS // 2)

        @g.cur.gpsimd
        def _(pool):
            pl.give(pool, "prepped")
            pool.wait_ge(masks_in, 32)
            with pool.Fori(0, HEADS // 2) as pair:
                h = pair * 2
                for s in range(2):
                    pool.wait_ge(xt_in[s], pair * 16 + 16)
                    pl.wait(pool, "weighed", h * NG + NG * (s - 1))
                    pool.tensor_tensor(T[:, s].rearrange("p (r c) -> p r c", c=GRID),
                                       cmask[:].rearrange("p (o c) -> p o c", o=1).broadcast_to([P, 14, GRID]),
                                       xt[:, s].rearrange("p (r c) -> p r c", c=GRID), ALU.subtract).then_inc(pl["prepped"], 1)
                    pl.wait(pool, "prepped", h * 2 + 2 * s + 1)
                    pool.tensor_tensor(TS[:, s], T[:, s, 2 * GRID:12 * GRID], imask[:], ALU.add).then_inc(pl["prepped"], 1)
            for n in list(quarters("out0_a")) + list(quarters("out0_b")):
                split_quarter(g, pool, n)

        @g.cur.tensor
        def _(pe):
            pl.give(pe, "turned", "weighed", "back")

            def scores(h, j):
                t, s = NA_TILES[j % NT], j // NT % 2
                if j % NT == 0:
                    pe.wait_ge(qkv_in[s], h * (QKV_IN // 2) + QKV_IN)
                pl.wait(pe, "minned", h * NT + (j - 1))
                for half in range(2 if t.shifted else 1):
                    n = 5 * GRID if t.shifted else 8 * GRID
                    for part in range(2):
                        k0 = t.key0 + half * n
                        mm = pe.matmul(ps_s[:, j % 2, half, 0:n], Q[:, s, (j % NT) * P:(j % NT + 1) * P],
                                       K[part][:, s, k0:k0 + n], start=part == 0, stop=part == 1)
                mm.then_inc(pl["scored"], 1)

            def turn(h, j, b):
                batches = NA_TILES[j % NT].batches
                if b == 0:
                    pl.wait(pe, "exped", h * NT + (j + 1))
                q = bat(j) + b
                pl.wait(pe, "lo", h * NBAT + (q - 1))
                for i in range(batches[b]):
                    c = sum(batches[:b]) + i
                    tr = pe.transpose(ps_t[:, q % 2, i * P:(i + 1) * P], S[:, j % 3, c * P:(c + 1) * P], g.ident[:])
                tr.then_inc(pl["turned"], 1)

            def weigh(h, q, half):
                if half == 0:
                    pl.wait(pe, "lo", h * NBAT + bat(2 * q + 2))
                    pl.wait(pe, "copied", h * NG + q)
                span = NA_SPAN[q % NG]
                c0 = 0 if span == 6 else 1
                for c in range(half * span // 2, (half + 1) * span // 2):
                    for part in range(2):
                        mm = pe.matmul(ps_pv[:, 0:256], V[:, q // NG % 2, NA_GROUP0[q % NG] + c], PT[part][:, q % 2, c0 + c],
                                       start=c + part == 0, stop=c + part == span)
                if half:
                    mm.then_inc(pl["weighed"], 1)

            def body(h, steps, live):
                for step in steps:
                    if live(step):
                        scores(h, step)
                    if live(step - 2):
                        turn(h, step - 2, 0)
                    if live(step - 4 - step % 2):
                        weigh(h, (step - 4) // 2, step % 2)
                    if live(step - 2) and len(NA_TILES[(step - 2) % NT].batches) == 2:
                        turn(h, step - 2, 1)
                    if step % 2 and live(step - 7):
                        pe_back(pe, h * NG, (step - 7) // 2)

            pair_loop(pe, body)

        @g.cur.scalar
        def _(act):
            pl.give(act, "copied")

            def exp(h, j):
                pl.wait(act, "minned", h * NT + (j + 1))
                t = NA_TILES[j % NT]
                act.activation(S[:, j % 3, 0:t.width], S[:, j % 3, 0:t.width], ACT.Exp, bias=mins[:, j % 3:j % 3 + 1], scale=-1.0,
                               accum_out=sums[:, j % NT // 2, j % 2:j % 2 + 1]).then_inc(pl["exped"], 1)

            def hi(h, j):
                t = NA_TILES[j % NT]
                if j % 2 == 0:
                    pl.wait(act, "weighed", h * NG + (j // 2 - 1))
                if j == 0:
                    act.wait_ge(cleared, 4)
                c = t.chunk0 - NA_GROUP0[j % NT // 2] + (not t.shifted)
                for b, n in enumerate(t.batches):
                    q = bat(j) + b
                    pl.wait(act, "turned", h * NBAT + (q + 1))
                    act.copy(PT[0][:, j // 2 % 2, c:c + n, j % 2 * P:(j % 2 + 1) * P],
                             ps_t[:, q % 2, 0:n * P].rearrange("p (c k) -> p c k", k=P)).then_inc(pl["hi"], 1)
                    c += n

            def body(h, steps, live):
                for step in steps:
                    if live(step - 2):
                        hi(h, step - 2)
                    if step % 2 and live(step - 5):
                        act_copy(act, h * NG, (step - 5) // 2)
                    if live(step):
                        exp(h, step)

            pair_loop(act, body)

        @g.cur.vector
        def _(dve):
            pl.give(dve, "minned", "lo", "reduced")
            for part in range(2):
                dve.memset(PT[part][:, :, 5, 0:P].bitcast(F32), 0.0).then_inc(cleared, 1)
                dve.memset(PT[part][:, :, 0, P:2 * P].bitcast(F32), 0.0).then_inc(cleared, 1)

            def before_minimum(h, j):
                if j % NT == 0:
                    pl.wait(dve, "prepped", h * 2 + 2 * (j // NT + 1))
                pl.wait(dve, "scored", h * NT + (j + 1))
                dve.memset(tick[:, j % 3:j % 3 + 1], 0.0)

            def minimum(h, j):
                t, s = NA_TILES[j % NT], j // NT % 2
                if t.shifted:
                    src, tab = ps_s[:, j % 2, :, 0:5 * GRID], TS[:, s].rearrange("p (a k) -> p a k", a=2)
                    dst = S[:, j % 3].rearrange("p (a k) -> p a k", a=2)
                else:
                    src, tab = ps_s[:, j % 2, 0], T[:, s, t.table:t.table + t.width]
                    dst = S[:, j % 3, 0:t.width]
                dve.tensor_tensor_reduce(dst, src, tab, 1.0, 3e38, ALU.add, ALU.min, mins[:, j % 3:j % 3 + 1]).then_inc(pl["minned"], 1)

            def lo(h, j):
                t = NA_TILES[j % NT]
                c = t.chunk0 - NA_GROUP0[j % NT // 2] + (not t.shifted)
                for b, n in enumerate(t.batches):
                    q = bat(j) + b
                    pl.wait(dve, "hi", h * NBAT + (q + 1))
                    at = lambda part: PT[part][:, j // 2 % 2, c:c + n, j % 2 * P:(j % 2 + 1) * P]
                    dve.tensor_tensor(at(1), ps_t[:, q % 2, 0:n * P].rearrange("p (c k) -> p c k", k=P), at(0).bitcast(F32),
                                      ALU.subtract).then_inc(pl["lo"], 1)
                    c += n

            def body(h, steps, live):
                for step in steps:
                    if live(step):
                        before_minimum(h, step)
                        minimum(h, step)
                    if step % 2 and live(step - 9):
                        q = (step - 9) // 2
                        dst = out[:, 2 * (q % NG):2 * (q % NG) + 2, bass.ds(h * DH + q // NG * DH, DH)]
                        dve_norm(dve, h * NG, q, dst)
                    if step % 2 == 0 and live(step - 8):
                        dve_add(dve, h * NG, (step - 8) // 2)
                    if live(step - 2):
                        lo(h, step - 2)

            pair_loop(dve, body)
        g.end()



def rows_turned(pe, src, dst, ident, n):
    for k in range(n):
        tr = pe.transpose(dst[:, k * P:(k + 1) * P], src[:, k * P:(k + 1) * P], ident)
    return tr


def out_proj(g, l):
    nc = g.nc
    pre = f"op{l}_"
    x_src = g.x if l == 0 else g.x2
    nmix = 8 if l == 0 else 4
    with ExitStack() as st:
        sb = lambda name, shape, dt=F32: st.enter_context(nc.sbuf_tensor(pre + name, shape, dt))
        inb = sb("in", [P, 2, 4, HALF])
        mix = sb("mix", [P, 2, D])
        yb = sb("y", [P, 2, HALF])
        th = sb("tanh", [P, HALF])
        cln = sb("cln", [P, 2, HALF])
        gpost = sb("gpost", [P, D])
        ost = sb("ost", [P, 2, HALF])
        orl = sb("orl", [P, 2, HALF])
        bn = sb("bn", [P, 2, 6])
        mv = sb("mv", [P, 2, 2])
        ss = sb("ss", [P, 2, NT])
        ps_o = st.enter_context(nc.psum_tensor(pre + "ps_o", [P, 2, HALF], F32))
        ps_t = st.enter_context(nc.psum_tensor(pre + "ps_t", [P, 2, D], F32))
        ps_n = st.enter_context(nc.psum_tensor(pre + "ps_n", [P, 2, HALF], F32))
        sem = lambda n: g.sem(pre + n)
        rows_in, consts_in = [sem("rows_in0"), sem("rows_in1")], sem("consts_in")
        conv_in = [sem("conv_in0"), sem("conv_in1")]
        conv_t, stats, yrow, tanhed, urow = sem("conv_t"), sem("stats"), sem("yrow"), sem("tanhed"), sem("urow")
        cln_ready, mixed = sem("cln_ready"), sem("mixed")
        turned, hi, lo, mm_done = sem("turned"), sem("hi"), sem("lo"), sem("mm")
        staged, squared = sem("staged"), sem("squared")
        pooled = sem("pooled")
        stored, x_in, x1_rows, x1_stored = [sem("stored0"), sem("stored1")], [sem("x_in0"), sem("x_in1")], sem("x1_rows"), [sem("x1_stored0"), sem("x1_stored1")]
        n_in = 3
        L_CONV, L_Y, L_MIX, L_TURN = (4, 3, 2, 1) if l == 0 else (0, 0, 2, 1)
        pool0 = 2 * NT if l == 0 else 0
        nxt = f"gate{l}_a"

        fm_rows = lambda s: inb[:, s, 2].rearrange("p (c t) -> p c t", c=4)

        @g.block(pre + "phase").sync
        def _(sp):
            def load_conv(t):
                if t >= 2:
                    sp.wait_ge(conv_t, t - 1)
                sp.dma_start(fm_rows(t % 2), g.conv[:, :, t * P:(t + 1) * P].rearrange("c p t -> p c t")).then_inc(conv_in[t % 2], 16)

            if l == 0:
                load_conv(0)
                for i in range(2):
                    sp.dma_start(cln[:, i], g.cln[i:i + 1, :].broadcast_to([P, HALF])).then_inc(consts_in, 16)
            sp.dma_start(gpost[:], g.g_post[l:l + 1, :].broadcast_to([P, D])).then_inc(consts_in, 16)

            def load(t):
                s = t % 2
                if t >= 2:
                    sp.wait_ge(mixed, (2 if l == 0 else 1) * (t - 1))
                    if l == 1:
                        sp.wait_ge(lo, 2 * (t - 1))
                sp.dma_start(inb[:, s, 0], tiles_of(g.attn[l], t)).then_inc(rows_in[s], 16)
                sp.dma_start(inb[:, s, 1], tiles_of(g.gate_a if l == 0 else g.gate_c, t)).then_inc(rows_in[s], 16)
                if l == 0:
                    sp.dma_start(inb[:, s, 3], tiles_of(g.gate_b, t)).then_inc(rows_in[s], 16)
                else:
                    sp.dma_start(fm_rows(s), g.dmix[:, :, t * P:(t + 1) * P].rearrange("c p t -> p c t")).then_inc(rows_in[s], 16)

            lag = L_CONV + 1 if l == 0 else 3
            for i in range(NT + lag):
                if l == 0 and i + 1 < NT:
                    load_conv(i + 1)
                if i < NT:
                    load(i)
                t = i - lag
                if t >= 0:
                    sp.wait_ge(staged, t + 1)
                    sp.dma_start(tiles_of(g.o, t), ost[:, t % 2]).then_inc(stored[t % 2], 16)
            for n in quarters(nxt)[:2]:
                load_quarter(g, sp, n)
            rest = list(quarters(nxt)[2:])

            def load_x(t):
                s = t % 2
                if t < 2:
                    sp.wait_ge(mixed, (2 if l == 0 else 1) * NT)
                    if l == 1:
                        sp.wait_ge(lo, 2 * NT)
                    sp.wait_ge(stored[s], 16 * NT // 2)
                else:
                    sp.wait_ge(x1_rows, 3 * (t - 1))
                sp.dma_start(inb[:, s, 0:2].rearrange("p a c -> p (a c)"), tiles_of(x_src, t)).then_inc(x_in[s], 16)
                sp.dma_start(orl[:, s], tiles_of(g.o, t)).then_inc(x_in[s], 16)

            load_x(0)
            load_x(1)
            for t in range(NT):
                sp.wait_ge(x1_rows, 3 * (t + 1))
                sp.dma_start(tiles_of(g.x1, t), inb[:, t % 2, 2:4].rearrange("p a c -> p (a c)")).then_inc(x1_stored[t % 2], 16)
                if t + 2 < NT:
                    load_x(t + 2)
                if t in (3, 7):
                    load_quarter(g, sp, rest.pop(0))
            for i in range(2):
                sp.wait_ge(x1_stored[i], 16 * NT // 2)

        @g.cur.gpsimd
        def _(pool):
            def mix_a(t):
                s = t % 2
                pool.wait_ge(rows_in[s], 16 * n_in * (t // 2 + 1))
                if t >= 2:
                    pool.wait_ge(turned, t - 1)
                pool.tensor_tensor(mix[:, s, 0:HALF], inb[:, s, 0], inb[:, s, 1], ALU.mult).then_inc(mixed, 1)

            for step in range(-4, NT):
                t = step + L_CONV
                if l == 0 and t < NT:
                    pool.wait_ge(stats, 2 * (t + 1))
                    rms_scale(pool, g, mv[:, t % 2, 1:2], 1, pooled, 2 * t)
                t = step + L_MIX
                if 0 <= t < NT:
                    mix_a(t)
                    if l == 0:
                        pool.wait_ge(urow, t + 1)
                        pool.tensor_tensor(mix[:, t % 2, HALF:D], yb[:, t % 2], inb[:, t % 2, 3], ALU.mult).then_inc(mixed, 1)
            qs = list(quarters(nxt))
            pool.wait_ge(mm_done, NT)
            for t in range(NT):
                pool.wait_ge(squared, NT + t + 1)
                pool.tensor_tensor(ss[:, 1, t:t + 1], ss[:, 0, t:t + 1], ss[:, 1, t:t + 1], ALU.add).then_inc(pooled, 1)
                pool.wait_ge(pooled, pool0 + 3 * t + 1)
                rms_scale(pool, g, ss[:, 1, t:t + 1], D, pooled, pool0 + 3 * t + 1)
                if t % 3 == 1:
                    split_quarter(g, pool, qs.pop(0))

        @g.cur.scalar
        def _(act):
            def split_hi(t, n):
                s = t % 2
                act.wait_ge(turned, n)
                k = nmix if n <= NT else 8
                act.copy(g.XT[0][:, 0:k, t * P:(t + 1) * P], ps_t[:, s, 0:k * P].rearrange("p (k c) -> p k c", c=P)).then_inc(hi, 1)
                if k == 4:
                    act.wait_ge(rows_in[s], 16 * n_in * (t // 2 + 1))
                    act.copy(g.XT[0][:, 4:8, t * P:(t + 1) * P], inb[:, s, 2].rearrange("p (k c) -> p k c", c=P)).then_inc(hi, 1)

            def square(t, half):
                src = ps_o[:, t % 2]
                if half:
                    act.wait_ge(squared, NT + t)
                act.activation(ps_n[:, 1] if half else src, src, ACT.Square, accum_out=ss[:, half, t:t + 1]).then_inc(squared, 1)

            for step in range(-4, NT):
                if 0 <= step + L_TURN < NT:
                    split_hi(step + L_TURN, step + L_TURN + 1)
                t = step + L_Y
                if l == 0 and 0 <= t < NT:
                    act.wait_ge(yrow, 3 * (t + 1))
                    if t:
                        act.wait_ge(urow, t)
                    act.activation(th[:], yb[:, t % 2], ACT.Tanh, scale=2.0).then_inc(tanhed, 1)
                if step >= 0:
                    t = step
                    act.wait_ge(mm_done, t + 1)
                    if t >= 2:
                        act.wait_ge(stored[t % 2], 16 * (t // 2))
                    act.copy(ost[:, t % 2], ps_o[:, t % 2]).then_inc(staged, 1)
                    act.wait_ge(staged, t + 1)
                    square(t, 0)
            for step in range(NT + 2):
                if step < NT:
                    act.wait_ge(mm_done, NT + step + 1)
                    square(step, 1)
                if step >= 2:
                    split_hi(step - 2, NT + step - 1)

        @g.cur.vector
        def _(dve):
            nlo = 1 if l == 0 else 2

            def split_lo(t, n):
                s = t % 2
                k = nmix if n <= NT else 8
                per = (1 if l == 0 else 2)
                base = per * (n - 1) if n <= NT else per * NT + (n - NT - 1)
                at = lambda part, k0, k1: g.XT[part][:, k0:k1, t * P:(t + 1) * P]
                dve.wait_ge(hi, base + 1)
                dve.tensor_tensor(at(1, 0, k), ps_t[:, s, 0:k * P].rearrange("p (k c) -> p k c", c=P), at(0, 0, k).bitcast(F32),
                                  ALU.subtract).then_inc(lo, 1)
                if k == 4:
                    dve.wait_ge(hi, base + 2)
                    dve.tensor_tensor(at(1, 4, 8), inb[:, s, 2].rearrange("p (k c) -> p k c", c=P), at(0, 4, 8).bitcast(F32),
                                      ALU.subtract).then_inc(lo, 1)

            if l == 0:
                dve.wait_ge(consts_in, 48)
                dve.tensor_scalar(cln[:], cln[:], 0.25, None, ALU.mult).then_inc(cln_ready, 1)
                dve.wait_ge(cln_ready, 1)

            for step in range(-4, NT):
                t = step + L_CONV
                if l == 0 and t < NT:
                    dve.wait_ge(conv_t, t + 1)
                    dve.bn_stats(bn[:, t % 2], ps_n[:, t % 2]).then_inc(stats, 1)
                    dve.wait_ge(stats, 2 * t + 1)
                    dve.bn_aggr(mv[:, t % 2], bn[:, t % 2]).then_inc(stats, 1)
                t = step + L_MIX
                if l == 0 and 0 <= t < NT:
                    y = yb[:, t % 2]
                    dve.wait_ge(tanhed, t + 1)
                    dve.scalar_tensor_tensor(y, th[:], 1.0, y, ALU.add, ALU.mult).then_inc(urow, 1)
                t = step + L_Y
                if l == 0 and 0 <= t < NT:
                    y = yb[:, t % 2]
                    dve.wait_ge(pooled, 2 * (t + 1))
                    if t >= 2:
                        dve.wait_ge(mixed, 2 * (t - 1))
                    dve.tensor_scalar(y, ps_n[:, t % 2], mv[:, t % 2, 0:1], mv[:, t % 2, 1:2], ALU.subtract, ALU.mult).then_inc(yrow, 1)
                    dve.wait_ge(yrow, 3 * t + 1)
                    dve.tensor_tensor(y, y, cln[:, 0], ALU.mult).then_inc(yrow, 1)
                    dve.wait_ge(yrow, 3 * t + 2)
                    dve.tensor_tensor(y, y, cln[:, 1], ALU.add).then_inc(yrow, 1)
                if 0 <= step + L_TURN < NT:
                    split_lo(step + L_TURN, step + L_TURN + 1)
            dve.wait_ge(consts_in, 48 if l == 0 else 16)
            for step in range(NT + 2):
                if step < NT:
                    t, s = step, step % 2
                    x, x1 = inb[:, s, 0:2].rearrange("p a c -> p (a c)"), inb[:, s, 2:4].rearrange("p a c -> p (a c)")
                    r = ss[:, 1, t:t + 1]
                    dve.wait_ge(pooled, pool0 + 3 * (t + 1))
                    dve.wait_ge(x_in[s], 32 * (t // 2 + 1))
                    if t >= 2:
                        dve.wait_ge(x1_stored[s], 16 * (t // 2))
                        dve.wait_ge(turned, NT + t - 1)
                    dve.scalar_tensor_tensor(x1[:, HALF:D], ps_o[:, s], r, gpost[:, HALF:D], ALU.mult, ALU.mult).then_inc(x1_rows, 1)
                    dve.scalar_tensor_tensor(x1[:, 0:HALF], orl[:, s], r, gpost[:, 0:HALF], ALU.mult, ALU.mult).then_inc(x1_rows, 1)
                    dve.wait_ge(x1_rows, 3 * t + 2)
                    dve.tensor_tensor(x1, x1, x, ALU.add).then_inc(x1_rows, 1)
                if step >= 2:
                    split_lo(step - 2, NT + step - 1)

        @g.cur.tensor
        def _(pe):
            def product(t, c):
                name = f"out{l}_" + "ab"[c]
                n = c * NT + t
                if t == 0:
                    wait_pair(g, pe, name)
                if c == 0:
                    pe.wait_ge(lo, (1 if l == 0 else 2) * (t + 1))
                if n >= 2:
                    if n - 2 < NT:
                        pe.wait_ge(squared, n - 1)
                    else:
                        pe.wait_ge(x1_rows, 3 * (n - 2 - NT) + 2)
                i = 0
                for k in range(KC):
                    for a, m in THREE:
                        mm = pe.matmul(ps_o[:, t % 2], g.XT[a][:, k, t * P:(t + 1) * P], w_at(g, name, m, k * HALF, HALF),
                                       start=i == 0, stop=i == 3 * KC - 1)
                        i += 1
                mm.then_inc(mm_done, 1)

            for step in range(-4, NT):
                t = step + L_CONV
                if l == 0 and t < NT:
                    pe.wait_ge(conv_in[t % 2], 16 * (t // 2 + 1))
                    if t >= 2:
                        pe.wait_ge(yrow, 3 * (t - 2) + 1)
                    for c in range(4):
                        tr = pe.transpose(ps_n[:, t % 2, c * P:(c + 1) * P], inb[:, t % 2, 2, c * P:(c + 1) * P], g.ident[:])
                    tr.then_inc(conv_t, 1)
                t = step + L_TURN
                if 0 <= t < NT:
                    pe.wait_ge(mixed, (2 if l == 0 else 1) * (t + 1))
                    if t >= 2:
                        pe.wait_ge(lo, (1 if l == 0 else 2) * (t - 2) + 1)
                    rows_turned(pe, mix[:, t % 2], ps_t[:, t % 2], g.ident[:], nmix).then_inc(turned, 1)
                if step >= 0:
                    product(step, 0)
            for step in range(NT + 2):
                if step < NT:
                    product(step, 1)
                if step >= 2:
                    t = step - 2
                    pe.wait_ge(x1_rows, 3 * (t + 1))
                    base = (1 if l == 0 else 2) * NT
                    pe.wait_ge(lo, base if t < 2 else base + t - 1)
                    rows_turned(pe, inb[:, t % 2, 2:4].rearrange("p a c -> p (a c)"), ps_t[:, t % 2], g.ident[:], 8).then_inc(turned, 1)
        g.end()



def gate(g, l):
    nc = g.nc
    pre = f"gt{l}_"
    dst = g.x2 if l == 0 else g.y
    with ExitStack() as st:
        sb = lambda name, shape, dt=F32: st.enter_context(nc.sbuf_tensor(pre + name, shape, dt))
        inb = sb("in", [P, 3, 2, HALF])
        x2a = sb("x2a", [P, 2, HALF])
        th = sb("tanh", [P, 2, HALF])
        x2 = sb("x2", [P, 3, HALF])
        h = sb("h", [P, 2, D])
        gpre = sb("gpre", [P, D])
        ss = sb("ss", [P, 2, NT])
        ps = st.enter_context(nc.psum_tensor(pre + "ps", [P, 3, HALF], F32))
        ps_t = st.enter_context(nc.psum_tensor(pre + "ps_t", [P, 2, D], F32))
        junk = st.enter_context(nc.psum_tensor(pre + "junk", [P, HALF], F32))
        sem = lambda n: g.sem(pre + n)
        rows_in, gpre_in, x2a_in = [sem(f"rows_in{i}") for i in range(3)], sem("gpre_in"), [sem("x2a_in0"), sem("x2a_in1")]
        mm_done, tanhed, x2_rows, squared, pooled = sem("mm"), sem("tanhed"), sem("x2_rows"), sem("squared"), sem("pooled")
        stored = [sem(f"stored{i}") for i in range(3)]
        h_rows, turned, hi, lo = sem("h_rows"), sem("turned"), sem("hi"), sem("lo")
        U = 2 * NT

        def split_hi(act, t):
            act.wait_ge(turned, t + 1)
            act.copy(g.XT[0][:, :, t * P:(t + 1) * P], ps_t[:, t % 2].rearrange("p (k c) -> p k c", c=P)).then_inc(hi, 1)

        @g.block(pre + "phase").sync
        def _(sp):
            first = list(quarters(f"gate{l}_b"))
            nxt = list(quarters("lat")) if l == 0 else []
            if l == 0:
                sp.dma_start(gpre[:], g.g_pre_row.broadcast_to([P, D])).then_inc(gpre_in, 16)

            def load(u):
                c, t, s = u // NT, u % NT, u % 3
                if u >= 3:
                    sp.wait_ge(x2_rows, 2 * (u - 2))
                cols = slice(c * HALF, (c + 1) * HALF)
                sp.dma_start(inb[:, s, 0], tiles_of(g.x1, t)[:, cols]).then_inc(rows_in[s], 16)
                sp.dma_start(inb[:, s, 1], tiles_of(g.ple[l], t)[:, cols]).then_inc(rows_in[s], 16)
                if c == 1 and l == 0:
                    sp.wait_ge(stored[t % 3], 16 * (t // 3 + 1))
                    if t >= 2:
                        sp.wait_ge(h_rows, 2 * (t - 1))
                    sp.dma_start(x2a[:, t % 2], tiles_of(g.x2, t)[:, 0:HALF]).then_inc(x2a_in[t % 2], 16)

            for u in range(2):
                load(u)
            for u in range(U):
                if u + 2 < U:
                    load(u + 2)
                if u in (0, 2, 4, 6):
                    load_quarter(g, sp, first.pop(0))
                if u in (13, 15, 17, 19) and nxt:
                    load_quarter(g, sp, nxt.pop(0))
                sp.wait_ge(x2_rows, 2 * (u + 1))
                c, t = u // NT, u % NT
                sp.dma_start(tiles_of(dst, t)[:, c * HALF:(c + 1) * HALF], x2[:, u % 3]).then_inc(stored[u % 3], 16)
            for i in range(3):
                sp.wait_ge(stored[i], 16 * U // 3)

        @g.cur.gpsimd
        def _(pool):
            for n in quarters(f"gate{l}_b"):
                split_quarter(g, pool, n)
            if l == 0:
                qs = list(quarters("lat"))
                for t in range(NT):
                    pool.wait_ge(squared, NT + t + 1)
                    pool.tensor_tensor(ss[:, 1, t:t + 1], ss[:, 0, t:t + 1], ss[:, 1, t:t + 1], ALU.add).then_inc(pooled, 1)
                    pool.wait_ge(pooled, 3 * t + 1)
                    rms_scale(pool, g, ss[:, 1, t:t + 1], D, pooled, 3 * t + 1)
                    if t % 3 == 1:
                        split_quarter(g, pool, qs.pop(0))

        @g.cur.scalar
        def _(act):
            for u in range(U + 3):
                if u < U:
                    act.wait_ge(mm_done, u + 1)
                    if u >= 2:
                        act.wait_ge(x2_rows, 2 * (u - 2) + 1)
                    act.activation(th[:, u % 2], ps[:, u % 3], ACT.Tanh, scale=0.5).then_inc(tanhed, 1)
                if l == 0 and 1 <= u <= U:
                    v = u - 1
                    act.wait_ge(x2_rows, 2 * (v + 1))
                    if v:
                        act.wait_ge(squared, v)
                    act.activation(junk[:], x2[:, v % 3], ACT.Square, accum_out=ss[:, v // NT, v % NT:v % NT + 1]).then_inc(squared, 1)
                t = u - NT - 2
                if l == 0 and 0 <= t < NT:
                    split_hi(act, t)

        @g.cur.vector
        def _(dve):
            def split_lo(t):
                dve.wait_ge(hi, t + 1)
                at = lambda part: g.XT[part][:, :, t * P:(t + 1) * P]
                dve.tensor_tensor(at(1), ps_t[:, t % 2].rearrange("p (k c) -> p k c", c=P), at(0).bitcast(F32),
                                  ALU.subtract).then_inc(lo, 1)

            def h_row(t):
                if t == 0:
                    dve.wait_ge(gpre_in, 16)
                u, r = NT + t, ss[:, 1, t:t + 1]
                dve.wait_ge(pooled, 3 * (t + 1))
                dve.wait_ge(x2a_in[t % 2], 16 * (t // 2 + 1))
                if t >= 2:
                    dve.wait_ge(turned, t - 1)
                dve.scalar_tensor_tensor(h[:, t % 2, 0:HALF], x2a[:, t % 2], r, gpre[:, 0:HALF], ALU.mult, ALU.mult).then_inc(h_rows, 1)
                dve.scalar_tensor_tensor(h[:, t % 2, HALF:D], x2[:, u % 3], r, gpre[:, HALF:D], ALU.mult, ALU.mult).then_inc(h_rows, 1)

            for u in range(U + 3):
                if u < U:
                    s = u % 3
                    dve.wait_ge(tanhed, u + 1)
                    dve.wait_ge(rows_in[s], 32 * (u // 3 + 1))
                    dve.scalar_tensor_tensor(inb[:, s, 1], th[:, u % 2], 1.0, inb[:, s, 1], ALU.add, ALU.mult).then_inc(x2_rows, 1)
                    dve.wait_ge(x2_rows, 2 * u + 1)
                    if u >= 3:
                        dve.wait_ge(stored[s], 16 * (u // 3))
                        if l == 0:
                            dve.wait_ge(squared, u - 2)
                    dve.scalar_tensor_tensor(x2[:, s], inb[:, s, 1], 0.5, inb[:, s, 0], ALU.mult, ALU.add).then_inc(x2_rows, 1)
                if l == 0 and 0 <= u - NT - 1 < NT:
                    h_row(u - NT - 1)
                if l == 0 and 0 <= u - NT - 2 < NT:
                    split_lo(u - NT - 2)

        @g.cur.tensor
        def _(pe):
            for u in range(U + 3):
                c, t = u // NT, u % NT
                if u < U:
                    name = f"gate{l}_" + "ab"[c]
                    if t == 0:
                        wait_pair(g, pe, name)
                    if u >= 3:
                        pe.wait_ge(tanhed, u - 2)
                    i = 0
                    for k in range(KC):
                        for a, m in THREE:
                            mm = pe.matmul(ps[:, u % 3], g.XT[a][:, k, t * P:(t + 1) * P], w_at(g, name, m, k * HALF, HALF),
                                           start=i == 0, stop=i == 3 * KC - 1)
                            i += 1
                    mm.then_inc(mm_done, 1)
                v = u - NT - 2
                if l == 0 and 0 <= v < NT:
                    pe.wait_ge(h_rows, 2 * (v + 1))
                    if v >= 2:
                        pe.wait_ge(lo, v - 1)
                    rows_turned(pe, h[:, v % 2], ps_t[:, v % 2], g.ident[:], 8).then_inc(turned, 1)
        g.end()



def in_odd(g):
    nc = g.nc
    names = ["lat", "gc", "f", "gd"]
    NQ, NKV = 256, 128
    R0 = NQ + NKV
    with ExitStack() as st:
        sb = lambda name, shape, dt=F32: st.enter_context(nc.sbuf_tensor("io_" + name, shape, dt))
        stage = sb("stage", [P, 4, HALF])
        th = sb("tanh", [P, 2, HALF])
        rope = sb("rope", [P, NT, 2 * ROPE])
        ss = sb("ss", [P, NT, 2])
        tmp = sb("tmp", [P, 2, ROPE])
        ps = st.enter_context(nc.psum_tensor("io_ps", [P, 7, HALF], F32))
        junk = st.enter_context(nc.psum_tensor("io_junk", [P, HALF], F32))
        sem = lambda n: g.sem("io_" + n)
        mm_done, copied, tanhed, gated, squared, pooled, latent_ops, rope_in = (
            sem("mm"), sem("copied"), sem("tanhed"), sem("gated"), sem("squared"), sem("pooled"), sem("latent_ops"), sem("rope_in"))
        stored = [sem(f"stored{i}") for i in range(4)]
        NBANK = 7
        kinds = [k for n in names for k in [{"lat": "lat", "gc": "gate", "f": "copy", "gd": "gate"}[n]] * 12]
        n_copy = [sum(k != "gate" for k in kinds[:i]) for i in range(len(kinds) + 1)]
        n_gate = [sum(k == "gate" for k in kinds[:i]) for i in range(len(kinds) + 1)]
        LAT = 5

        def dest(u):
            n, j = names[u // 12], u % 12
            if n in ("lat", "gc"):
                return tiles_of(g.lat if n == "lat" else g.gate_c, j)
            c, b = FM_ORDER[j]
            return (g.f if n == "f" else g.gate_d)[c, :, b * 512:(b + 1) * 512]

        @g.block("in_odd").sync
        def _(sp):
            sp.dma_start(rope[:], g.c_rope_k).then_inc(rope_in, 16)
            for u, kd in enumerate(kinds):
                j, i = u % 12, PIDX[names[u // 12]]
                if j % 2 == 0 and j < 8:
                    load_quarter(g, sp, QBASE[i + 1] + j // 2)
                if kd == "lat":
                    sp.wait_ge(latent_ops, LAT * (u + 1))
                elif kd == "copy":
                    sp.wait_ge(copied, n_copy[u + 1])
                else:
                    sp.wait_ge(gated, n_gate[u + 1])
                sp.dma_start(dest(u), stage[:, u % 4]).then_inc(stored[u % 4], 16)
            for i in range(4):
                sp.wait_ge(stored[i], 16 * len(kinds) // 4)

        @g.cur.gpsimd
        def _(pool):
            qs = list(quarters("gc"))
            for t in range(NT):
                pool.wait_ge(squared, 2 * (t + 1))
                rms_scale(pool, g, ss[:, t, :], 1, pooled, 2 * t)
                if t % 2 == 1 and qs:
                    split_quarter(g, pool, qs.pop(0))
            for i, n in ((1, "f"), (2, "gd"), (3, "up")):
                for q in quarters(n):
                    if q == quarters(n)[0]:
                        pool.wait_ge(mm_done, 12 * i)
                    split_quarter(g, pool, q)

        @g.cur.scalar
        def _(act):
            def squares(t):
                for i, (a, b) in enumerate(((0, NQ), (NQ, R0))):
                    n = 2 * t + i
                    if n:
                        act.wait_ge(squared, n)
                    act.activation(junk[:, a:b], ps[:, t % NBANK, a:b], ACT.Square, scale=(b - a) ** -0.5,
                                   accum_out=ss[:, t, i:i + 1]).then_inc(squared, 1)

            for u, kd in enumerate(kinds):
                act.wait_ge(mm_done, u + 1)
                if kd == "gate":
                    i = n_gate[u]
                    if i >= 2:
                        act.wait_ge(gated, i - 1)
                    act.activation(th[:, i % 2], ps[:, u % NBANK], ACT.Tanh, scale=0.5).then_inc(tanhed, 1)
                else:
                    if kd == "lat":
                        squares(u)
                    if u >= 4:
                        act.wait_ge(stored[u % 4], 16 * (u // 4))
                    act.copy(stage[:, u % 4], ps[:, u % NBANK]).then_inc(copied, 1)

        @g.cur.vector
        def _(dve):
            dve.wait_ge(rope_in, 16)
            for u, kd in enumerate(kinds):
                x = stage[:, u % 4]
                if kd == "lat":
                    dve.wait_ge(copied, n_copy[u + 1])
                    dve.wait_ge(pooled, 2 * (u + 1))
                    n = LAT * u
                    dve.tensor_tensor(tmp[:, 0], x[:, R0:R0 + ROPE], rope[:, u, 0:ROPE], ALU.mult).then_inc(latent_ops, 1)
                    dve.tensor_tensor(tmp[:, 1], x[:, R0 + ROPE:R0 + 2 * ROPE], rope[:, u, ROPE:], ALU.mult).then_inc(latent_ops, 1)
                    dve.tensor_scalar(x[:, 0:NQ], x[:, 0:NQ], ss[:, u, 0:1], None, ALU.mult).then_inc(latent_ops, 1)
                    dve.tensor_scalar(x[:, NQ:R0], x[:, NQ:R0], ss[:, u, 1:2], None, ALU.mult).then_inc(latent_ops, 1)
                    dve.wait_ge(latent_ops, n + 2)
                    dve.tensor_tensor(x[:, R0 + DH:R0 + DH + ROPE], tmp[:, 0], tmp[:, 1], ALU.add).then_inc(latent_ops, 1)
                    dve.wait_ge(latent_ops, n + 5)
                elif kd == "gate":
                    i = n_gate[u]
                    dve.wait_ge(tanhed, i + 1)
                    if u >= 4:
                        dve.wait_ge(stored[u % 4], 16 * (u // 4))
                    dve.scalar_tensor_tensor(x, th[:, i % 2], 1.0, ps[:, u % NBANK], ALU.add, ALU.mult).then_inc(gated, 1)

        def free(pe, u):
            v = u - NBANK
            if v >= 0:
                if kinds[v] == "gate":
                    pe.wait_ge(gated, n_gate[v + 1])
                else:
                    pe.wait_ge(copied, n_copy[v + 1])

        @g.cur.tensor
        def _(pe):
            for i, n in enumerate(names):
                project(g, pe, n, n in ("f", "gd"), FM_ORDER, ps, 12 * i, free, mm_done, NBANK)
        g.end()



def latent(g):
    nc = g.nc
    with ExitStack() as st:
        sb = lambda name, shape, dt=F32: st.enter_context(nc.sbuf_tensor("la_" + name, shape, dt))
        rows = sb("rows", [P, 2, 4, HALF])
        L = [sb("hi_part", [P, 3, TOK], F32R), sb("lo_part", [P, 3, TOK], F32R)]
        kr = sb("kr", [P, TOK])
        stage = sb("stage", [P, 3, TOK])
        qscale = sb("qscale", [P, TOK])
        latg = sb("gain", [P, 3])
        ps_t = st.enter_context(nc.psum_tensor("la_ps_t", [P, 2, HALF], F32))
        ps = st.enter_context(nc.psum_tensor("la_ps", [P, 4, HALF], F32))
        sem = lambda n: g.sem("la_" + n)
        rows_in, consts_in, turned, hi, lo = [sem(f"rows_in{i}") for i in range(NB)], sem("consts_in"), sem("turned"), sem("hi"), sem("lo")
        mm_done, by_act, by_dve = sem("mm"), sem("by_act"), sem("by_dve")
        stored, kr_stored = [sem(f"stored{i}") for i in range(3)], sem("kr_stored")
        groups = [x for i in range(4) for x in (("k", i), ("q", 2 * i), ("q", 2 * i + 1), ("v", i))]
        n_act = [3 * sum(x[0] != "q" for x in groups[:i]) for i in range(len(groups) + 1)]
        n_dve = [3 * sum(x[0] == "q" for x in groups[:i]) for i in range(len(groups) + 1)]

        def evacuated(eng, u):
            if groups[u // 3][0] == "q":
                eng.wait_ge(by_dve, n_dve[u // 3] + u % 3 + 1)
            else:
                eng.wait_ge(by_act, n_act[u // 3] + u % 3 + 1)

        @g.block("latent").sync
        def _(sp):
            def load(b):
                if b >= 2:
                    sp.wait_ge(turned, 4 * (b - 1))
                sp.dma_start(rows[:, b % 2], g.lat[b * 512:(b + 1) * 512, :].rearrange("(t p) c -> p t c", p=P)).then_inc(rows_in[b], 16)

            load(0)
            sp.dma_start(latg[:], g.lat_g).then_inc(consts_in, 16)
            load(1)
            sp.dma_start(qscale[:], g.c_qscale).then_inc(consts_in, 16)
            load(2)
            for n in quarters("dft"):
                load_quarter(g, sp, n)
            sp.wait_ge(lo, 4 * NB)
            sp.dma_start(g.kr, kr[DH:DH + ROPE, :]).then_inc(kr_stored, 16)
            for i, (kind, n) in enumerate(groups):
                evacuated(sp, 3 * i + 2)
                src = stage[:, i % 3]
                if kind == "v":
                    dst = g.vv[3 * n * P:(3 * n + 3) * P, :].rearrange("(t p) c -> p t c", p=P)
                    src = src.rearrange("p (t c) -> p t c", c=HALF)
                elif kind == "k":
                    dst = g.kn[2 * n:2 * n + 2].rearrange("h d t -> (h d) t")
                else:
                    dst = g.qs[n]
                sp.dma_start(dst, src).then_inc(stored[i % 3], 16)
            for i in range(3):
                sp.wait_ge(stored[i], 16 * len(range(i, len(groups), 3)))
            sp.wait_ge(kr_stored, 16)

        @g.cur.gpsimd
        def _(pool):
            for n in quarters("dft"):
                split_quarter(g, pool, n)

        @g.cur.scalar
        def _(act):
            act.wait_ge(consts_in, 32)
            for b in range(NB):
                for k in range(3):
                    act.wait_ge(turned, 4 * b + k + 1)
                    act.activation(L[0][:, k, b * 512:(b + 1) * 512], ps_t[:, (4 * b + k) % 2], ACT.Copy,
                                   scale=latg[:, k:k + 1]).then_inc(hi, 1)
            for i, (kind, n) in enumerate(groups):
                if kind == "q":
                    continue
                if i >= 3:
                    act.wait_ge(stored[i % 3], 16 * (i // 3))
                for j in range(3):
                    u = 3 * i + j
                    act.wait_ge(mm_done, u + 1)
                    act.activation(stage[:, i % 3, j * 512:(j + 1) * 512], ps[:, u % 4], ACT.Copy,
                                   scale=0.5 if kind == "v" else 1.0).then_inc(by_act, 1)

        @g.cur.vector
        def _(dve):
            dve.wait_ge(consts_in, 32)
            for b in range(NB):
                for k in range(4):
                    r = 4 * b + k
                    cols = slice(b * 512, (b + 1) * 512)
                    if k < 3:
                        dve.wait_ge(hi, 3 * b + k + 1)
                        dve.scalar_tensor_tensor(L[1][:, k, cols], ps_t[:, r % 2], latg[:, k:k + 1], L[0][:, k, cols].bitcast(F32),
                                                 ALU.mult, ALU.subtract).then_inc(lo, 1)
                    else:
                        dve.wait_ge(turned, r + 1)
                        dve.tensor_copy(kr[:, cols], ps_t[:, r % 2]).then_inc(lo, 1)
            for i, (kind, n) in enumerate(groups):
                if kind != "q":
                    continue
                if i >= 3:
                    dve.wait_ge(stored[i % 3], 16 * (i // 3))
                for j in range(3):
                    u = 3 * i + j
                    cols = slice(j * 512, (j + 1) * 512)
                    dve.wait_ge(mm_done, u + 1)
                    dve.tensor_tensor(stage[:, i % 3, cols], ps[:, u % 4], qscale[:, cols], ALU.mult).then_inc(by_dve, 1)

        @g.cur.tensor
        def _(pe):
            for b in range(NB):
                pe.wait_ge(rows_in[b], 16)
                for k in range(4):
                    r = 4 * b + k
                    if r >= 2:
                        pe.wait_ge(lo, r - 1)
                    for j in range(4):
                        tr = pe.transpose(ps_t[:, r % 2, j * P:(j + 1) * P], rows[:, b % 2, j, k * P:(k + 1) * P], g.ident[:])
                    tr.then_inc(turned, 1)
            wait_pair(g, pe, "up")
            pe.wait_ge(lo, 4 * NB)
            for i, (kind, n) in enumerate(groups):
                for j in range(3):
                    u = 3 * i + j
                    cols = slice(j * 512, (j + 1) * 512)
                    if u >= 4:
                        evacuated(pe, u - 4)
                    terms = []
                    for a, m in THREE:
                        if kind == "v":
                            terms.append((L[a][:, 2, (3 * n + j) * P:(3 * n + j + 1) * P], w_at(g, "up", m, 2560, 512)))
                        elif kind == "k":
                            terms.append((w_at(g, "up", a, 2048 + n * P, P), L[m][:, 2, cols]))
                        else:
                            terms += [(w_at(g, "up", a, k * 1024 + n * P, P), L[m][:, k, cols]) for k in range(2)]
                    for x, (lhs, rhs) in enumerate(terms):
                        mm = pe.matmul(ps[:, u % 4], lhs, rhs, start=x == 0, stop=x == len(terms) - 1)
                    mm.then_inc(mm_done, 1)
        g.end()



class Operands:
    LOADS, PREPS = 48, 6

    def __init__(self, g, st):
        sb = lambda name, shape, dt=F32: st.enter_context(g.nc.sbuf_tensor("ml_" + name, shape, dt))
        self.xq, self.xk = sb("xq", [P, TOK]), sb("xk", [P, TOK])
        self.xv = sb("xv", [P, NT, DH])
        self.Q = [sb("q_hi", [P, 2, TOK], F32R), sb("q_lo", [P, 2, TOK], F32R)]
        self.K = [sb("k_hi", [P, 2, TOK], F32R), sb("k_lo", [P, 2, TOK], F32R)]
        self.V = sb("v", [P, 2, NT, P], F32R)
        self.loaded, self.rope_loaded = g.sem("ml_loaded"), g.sem("ml_rope_loaded")
        self.prepped = g.sem("ml_prepped")

    def load_rope(self, g, sp):
        for r in (DH, DH + ROPE):
            sp.dma_start(self.xk[r:r + ROPE, :], g.kr).then_inc(self.rope_loaded, 16)

    def load(self, g, sp, h, cols):
        sp.dma_start(self.xq[:], g.qs[h]).then_inc(self.loaded, 16)
        sp.dma_start(self.xk[0:DH, :], g.kn[h]).then_inc(self.loaded, 16)
        sp.dma_start(self.xv[:], g.vv.rearrange("(t p) c -> p t c", p=P)[:, :, cols]).then_inc(self.loaded, 16)

    def prep(self, g, pool, h, s):
        zeros = g.zero[:, 0:1].broadcast_to([P, TOK])
        pool.wait_ge(self.loaded, h * self.LOADS + self.LOADS)
        pool.tensor_tensor(self.Q[0][:, s], self.xq[:], zeros, ALU.add).then_inc(self.prepped, 1)
        pool.tensor_tensor(self.K[0][:, s], self.xk[:], zeros, ALU.add).then_inc(self.prepped, 1)
        pool.tensor_tensor(self.V[:, s, :, 0:DH], self.xv[:], g.zero3, ALU.add).then_inc(self.prepped, 1)
        pool.wait_ge(self.prepped, h * self.PREPS + 3)
        pool.tensor_tensor(self.Q[1][:, s], self.xq[:], self.Q[0][:, s].bitcast(F32), ALU.subtract).then_inc(self.prepped, 1)
        pool.tensor_tensor(self.K[1][:, s], self.xk[:], self.K[0][:, s].bitcast(F32), ALU.subtract).then_inc(self.prepped, 1)
        pool.tensor_tensor(self.V[:, s, :, DH:P], self.xv[:], self.V[:, s, :, 0:DH].bitcast(F32), ALU.subtract).then_inc(self.prepped, 1)



def fnet(g, ml):
    nc = g.nc
    with ExitStack() as st:
        sb = lambda name, shape, dt=F32: st.enter_context(nc.sbuf_tensor("fn_" + name, shape, dt))
        f = sb("f", [P, 2, TOK])
        gd = sb("gate", [P, 2, TOK])
        EO = sb("eo", [P, 2, TOK // 2])
        Y = [sb("y_hi", [P, 2, NT // 2, 2, P], F32R), sb("y_lo", [P, 2, NT // 2, 2, P], F32R)]
        yh = sb("y_half", [1, 2, 2, P])
        a_sb = sb("a", [P, 2, HALF])
        S = sb("s", [P, TOK])
        dft_ch = sb("dft_ch", [P, 2 * P])
        alt, altc = sb("alt", [1, 2, 513]), sb("altc", [P, 2])
        ps_y = st.enter_context(nc.psum_tensor("fn_ps_y", [P, 2, HALF], F32))
        ps_yh = st.enter_context(nc.psum_tensor("fn_ps_yh", [P, HALF], F32))
        ps_a = st.enter_context(nc.psum_tensor("fn_ps_a", [P, 2, HALF], F32))
        ps_b = st.enter_context(nc.psum_tensor("fn_ps_b", [P, 2, HALF], F32))
        ps_half = st.enter_context(nc.psum_tensor("fn_ps_half", [P, HALF], F32))
        sem = lambda n: g.sem("fn_" + n)
        consts_in, f_in, gd_in = sem("consts_in"), [sem("f_in0"), sem("f_in1")], [sem("gd_in0"), sem("gd_in1")]
        odd_zero, folded, y_mm, y_hi, y_lo, yh_done = sem("odd_zero"), sem("folded"), sem("y_mm"), sem("y_hi"), sem("y_lo"), sem("yh_done")
        a_mm, b_mm, half_mm, a_copied, half_copied, unfolded = (
            sem("a_mm"), sem("b_mm"), sem("half_mm"), sem("a_copied"), sem("half_copied"), sem("unfolded"))
        mixed, stored = sem("mixed"), [sem("stored0"), sem("stored1")]
        NGR = 4
        FOLDS, ROUNDS = 5, NT // 4
        SEQ = [(0, SEQS[0]), (SEQS[0], SEQS[1])]

        @g.block("fnet").sync
        def _(sp):
            def load(c):
                if c >= 2:
                    sp.wait_ge(y_mm, (ROUNDS + 1) * (c - 1))
                sp.dma_start(f[:, c % 2], g.f[c]).then_inc(f_in[c % 2], 16)

            def load_gate(c):
                if c >= 2:
                    sp.wait_ge(stored[c % 2], 16 * (c // 2))
                sp.dma_start(gd[:, c % 2], g.gate_d[c]).then_inc(gd_in[c % 2], 16)

            load(0)
            for dst, src in ((dft_ch[:], g.c_dft_ch), (alt[:], g.c_alt.rearrange("s o n -> o s n")), (altc[:], g.c_altc)):
                sp.dma_start(dst, src).then_inc(consts_in, 16)
            ml.load_rope(g, sp)
            load(1)
            ml.load(g, sp, 0, slice(0, DH))
            load_gate(0)
            load_gate(1)
            for c in range(NGR):
                if c + 2 < NGR:
                    load(c + 2)
                sp.wait_ge(mixed, c + 1)
                sp.dma_start(g.dmix[c], gd[:, c % 2]).then_inc(stored[c % 2], 16)
                if c + 2 < NGR:
                    load_gate(c + 2)
            for i in range(2):
                sp.wait_ge(stored[i], 16 * NGR // 2)

        @g.cur.gpsimd
        def _(pool):
            pool.wait_ge(ml.rope_loaded, 32)
            ml.prep(g, pool, 0, 0)

        @g.cur.vector
        def _(dve):
            dve.memset(EO[:, 1, 0:513:512], 0.0).then_inc(odd_zero, 1)

            def fold(c):
                x = f[:, c % 2]
                dve.wait_ge(f_in[c % 2], 16 * (c // 2 + 1))
                if c:
                    dve.wait_ge(y_mm, (ROUNDS + 1) * c)
                dve.tensor_copy(EO[:, 0, 0:513:512], x[:, 0:1025:1024]).then_inc(folded, 1)
                for t0, n in SEQ:
                    for i, op in enumerate((ALU.add, ALU.subtract)):
                        dve.tensor_tensor(EO[:, i, t0 // 2 + 1:t0 // 2 + n // 2], x[:, t0 + 1:t0 + n // 2],
                                          x[:, t0 + n - 1:t0 + n // 2:-1], op).then_inc(folded, 1)

            def split_lo(c):
                for r in range(ROUNDS):
                    i = ROUNDS * c + r
                    at = lambda part: Y[part][:, c % 2, 2 * r:2 * r + 2]
                    dve.wait_ge(y_hi, i + 1)
                    dve.tensor_tensor(at(1), ps_y[:, i % 2].rearrange("p (c e k) -> p c e k", c=2, e=2), at(0).bitcast(F32),
                                      ALU.subtract).then_inc(y_lo, 1)

            def unfold(c):
                for i, (t0, n) in enumerate(SEQ):
                    w, m = 2 * c + i, n // 2
                    dve.wait_ge(a_copied, w + 1)
                    dve.wait_ge(b_mm, w + 1)
                    if i == 0 and c:
                        dve.wait_ge(mixed, c)
                    dve.tensor_tensor(S[:, t0:t0 + m], a_sb[:, w % 2, 0:m], ps_b[:, w % 2, 0:m], ALU.add).then_inc(unfolded, 1)
                    dve.tensor_tensor(S[:, t0 + m + 1:t0 + n], a_sb[:, w % 2, m - 1:0:-1], ps_b[:, w % 2, m - 1:0:-1],
                                      ALU.subtract).then_inc(unfolded, 1)

            def gated(c):
                dve.wait_ge(gd_in[c % 2], 16 * (c // 2 + 1))
                dve.wait_ge(unfolded, 4 * (c + 1))
                dve.wait_ge(half_copied, 2 * (c + 1))
                dve.tensor_tensor(gd[:, c % 2], S[:], gd[:, c % 2], ALU.mult).then_inc(mixed, 1)

            fold(0)
            for c in range(NGR + 1):
                if c < NGR:
                    split_lo(c)
                if c + 1 < NGR:
                    fold(c + 1)
                if c >= 1:
                    unfold(c - 1)
                    gated(c - 1)

        @g.cur.scalar
        def _(act):
            def split_hi(c):
                for r in range(ROUNDS):
                    i = ROUNDS * c + r
                    act.wait_ge(y_mm, i + c + 1)
                    if r == 0 and c >= 2:
                        act.wait_ge(b_mm, 2 * (c - 1))
                    act.copy(Y[0][:, c % 2, 2 * r:2 * r + 2], ps_y[:, i % 2].rearrange("p (c e k) -> p c e k", c=2, e=2)).then_inc(y_hi, 1)
                act.wait_ge(y_mm, (ROUNDS + 1) * (c + 1))
                if c >= 2:
                    act.wait_ge(half_mm, 2 * (c - 1))
                act.copy(yh[:, c % 2], ps_yh[0:1, 0:2 * P].rearrange("p (s k) -> p s k", k=P)).then_inc(yh_done, 1)

            def middle(c):
                for i, (t0, n) in enumerate(SEQ):
                    w, m = 2 * c + i, n // 2
                    act.wait_ge(a_mm, w + 1)
                    if w >= 2:
                        act.wait_ge(unfolded, 2 * (w - 1))
                    act.copy(a_sb[:, w % 2, 0:m], ps_a[:, w % 2, 0:m]).then_inc(a_copied, 1)
                    act.wait_ge(half_mm, w + 1)
                    if i == 0 and c:
                        act.wait_ge(mixed, c)
                    act.copy(S[:, t0 + m:t0 + m + 1], ps_half[:, 0:1]).then_inc(half_copied, 1)

            for c in range(NGR + 1):
                if c < NGR:
                    split_hi(c)
                if c >= 1:
                    middle(c - 1)

        @g.cur.tensor
        def _(pe):
            def channels(c):
                pe.wait_ge(folded, FOLDS * (c + 1))
                if c == 0:
                    pe.wait_ge(odd_zero, 1)
                    pe.wait_ge(consts_in, 48)
                for r in range(ROUNDS):
                    i = ROUNDS * c + r
                    if i >= 2:
                        pe.wait_ge(y_lo, i - 1)
                    for j in range(2):
                        for e in range(2):
                            mm = pe.matmul(ps_y[:, i % 2, (2 * j + e) * P:(2 * j + e + 1) * P],
                                           EO[:, e, (2 * r + j) * P:(2 * r + j + 1) * P], dft_ch[:, e * P:(e + 1) * P],
                                           start=True, stop=True)
                    mm.then_inc(y_mm, 1)
                if c:
                    pe.wait_ge(yh_done, c)
                for i, (t0, n) in enumerate(SEQ):
                    mm = pe.matmul(ps_yh[0:1, i * P:(i + 1) * P], f[:, c % 2, t0 + n // 2:t0 + n // 2 + 1], dft_ch[:, 0:P],
                                   start=True, stop=True)
                mm.then_inc(y_mm, 1)

            def tokens(c):
                s = c % 2
                pe.wait_ge(y_lo, ROUNDS * (c + 1))
                pe.wait_ge(yh_done, c + 1)
                for i, (t0, n) in enumerate(SEQ):
                    w, m = 2 * c + i, n // 2
                    nk = m // P
                    if i == 0:
                        table = lambda e, part, k: w_at(g, "dft", part, (e * nk + k) * m, m)
                    else:
                        table = lambda e, part, k: w_at(g, "up", part, 3072 + (e * nk + k) * m, m)
                    k0 = t0 // 2 // P
                    for e, dst, done in ((0, ps_a, a_mm), (1, ps_b, b_mm)):
                        if w >= 2:
                            if e == 0:
                                pe.wait_ge(a_copied, w - 1)
                            else:
                                pe.wait_ge(unfolded, 2 * (w - 1))
                        if e == 0:
                            pe.matmul(dst[:, w % 2, 0:m], yh[:, s, i], alt[:, i, 0:m], start=True, stop=False)
                        for k in range(nk):
                            for a, b in THREE:
                                mm = pe.matmul(dst[:, w % 2, 0:m], Y[a][:, s, k0 + k, e], table(e, b, k),
                                               start=e == 1 and k + a + b == 0, stop=k == nk - 1 and a == 1)
                        mm.then_inc(done, 1)
                    if w:
                        pe.wait_ge(half_copied, w)
                    pe.matmul(ps_half[:, 0:1], yh[:, s, i], alt[:, i, 0:1], start=True, stop=False)
                    for k in range(nk):
                        for a in range(2):
                            mm = pe.matmul(ps_half[:, 0:1], Y[a][:, s, k0 + k, 0].bitcast(F32), altc[:, i:i + 1],
                                           start=False, stop=k == nk - 1 and a == 1)
                    mm.then_inc(half_mm, 1)

            for c in range(NGR + 1):
                if c < NGR:
                    channels(c)
                if c >= 1:
                    tokens(c - 1)
        g.end()



KEYS = [(0, 8) if t < 8 else (8, 4) for t in range(NT)]
ML_BATCHES = [KEYS[t][1] // 4 for t in range(NT)]


def mla(g, ml):
    nc = g.nc
    with ExitStack() as st:
        sb = lambda name, shape, dt=F32: st.enter_context(nc.sbuf_tensor("mla_" + name, shape, dt))
        S = sb("s", [P, 2, 2 * HALF])
        mins = sb("min", [P, 3])
        sums, rinv = sb("sums", [P, NG, 2]), sb("rinv", [P, 2, 2])
        red = sb("red", [P, 2, 2, DH])
        PT = [sb("pt_hi", [P, 2, 8, 256], F32R), sb("pt_lo", [P, 2, 8, 256], F32R)]
        pv_sb = sb("pv", [P, 2, 256])
        out = sb("out", [P, NT, HALF])
        ps_s = st.enter_context(nc.psum_tensor("mla_ps_s", [P, 2, 2 * HALF], F32))
        ps_t = st.enter_context(nc.psum_tensor("mla_ps_t", [P, 2, HALF], F32))
        ps_pv = st.enter_context(nc.psum_tensor("mla_ps_pv", [P, HALF], F32))
        ps_back = st.enter_context(nc.psum_tensor("mla_ps_back", [P, HALF], F32))
        pl = Pipeline(g, "mla", minned=0, exped=2)
        attn_out = g.sem("mla_attn_out")
        act_copy, pe_back, dve_add, dve_norm = attention_tail(g, pl, ps_pv, ps_back, pv_sb, sums, rinv, red, out)

        nb = sum(ML_BATCHES)

        def bat(j):
            return nb * (j // NT) + sum(ML_BATCHES[:j % NT])

        @g.block("mla").sync
        def _(sp):
            def store(cols):
                sp.dma_start(g.attn[1].rearrange("(t p) c -> p t c", p=P)[:, :, cols], out[:, :, cols]).then_inc(attn_out, 16)

            sp.wait_ge(ml.prepped, ml.PREPS)
            ml.load(g, sp, 1, slice(DH, 2 * DH))
            with sp.Fori(0, HEADS // 2 - 1) as pair:
                for s in (2, 3):
                    sp.wait_ge(ml.prepped, pair * 2 * ml.PREPS + s * ml.PREPS)
                    ml.load(g, sp, pair * 2 + s, bass.ds(pair * 2 * DH + s * DH, DH))
                pl.wait(sp, "normed", pair * 2 * NG + 2 * NG)
                store(bass.ds(pair * 2 * DH, 2 * DH))
            for n in list(quarters("out1_a")) + list(quarters("out1_b")):
                load_quarter(g, sp, n)
            pl.wait(sp, "normed", HEADS * NG)
            store(slice(HALF - 2 * DH, HALF))
            sp.wait_ge(attn_out, 16 * HEADS // 2)

        @g.cur.gpsimd
        def _(pool):
            with pool.Fori(0, HEADS // 2 - 1) as pair:
                for s in (1, 2):
                    pl.wait(pool, "weighed", pair * 2 * NG + (s - 1) * NG)
                    ml.prep(g, pool, pair * 2 + s, s % 2)
            pl.wait(pool, "weighed", (HEADS - 2) * NG)
            ml.prep(g, pool, HEADS - 1, 1)
            for n in list(quarters("out1_a")) + list(quarters("out1_b")):
                split_quarter(g, pool, n)

        @g.cur.tensor
        def _(pe):
            pl.give(pe, "turned", "weighed", "back")

            def scores(h, j):
                t, s = j % NT, j // NT
                if t == 0:
                    pe.wait_ge(ml.prepped, h * ml.PREPS + (s + 1) * ml.PREPS)
                pl.wait(pe, "exped", h * NT + (j - 1))
                for half in range(KEYS[t][1] // 4):
                    k0 = KEYS[t][0] * P + half * 512
                    for a, m in THREE:
                        mm = pe.matmul(ps_s[:, j % 2, half * 512:(half + 1) * 512], ml.Q[a][:, s, t * P:(t + 1) * P],
                                       ml.K[m][:, s, k0:k0 + 512], start=a + m == 0, stop=a == 1)
                mm.then_inc(pl["scored"], 1)

            def turn(h, j, b):
                if b == 0:
                    pl.wait(pe, "exped", h * NT + (j + 1))
                q = bat(j) + b
                pl.wait(pe, "lo", h * nb + (q - 1))
                for i in range(4):
                    tr = pe.transpose(ps_t[:, q % 2, i * P:(i + 1) * P], S[:, j % 2, (4 * b + i) * P:(4 * b + i + 1) * P], g.ident[:])
                tr.then_inc(pl["turned"], 1)

            def weigh(h, q, half):
                if half == 0:
                    pl.wait(pe, "lo", h * nb + bat(2 * q + 2))
                    pl.wait(pe, "copied", h * NG + q)
                k0, n = KEYS[2 * q % NT]
                for c in range(half * n // 2, (half + 1) * n // 2):
                    for part in range(2):
                        mm = pe.matmul(ps_pv[:, 0:256], ml.V[:, q // NG % 2, k0 + c], PT[part][:, q % 2, c],
                                       start=c + part == 0, stop=c + part == n)
                if half:
                    mm.then_inc(pl["weighed"], 1)

            def body(h, steps, live):
                for step in steps:
                    if live(step):
                        scores(h, step)
                    if live(step - 2):
                        turn(h, step - 2, 0)
                    if live(step - 4 - step % 2):
                        weigh(h, (step - 4) // 2, step % 2)
                    if live(step - 2) and ML_BATCHES[(step - 2) % NT] == 2:
                        turn(h, step - 2, 1)
                    if step % 2 and live(step - 7):
                        pe_back(pe, h * NG, (step - 7) // 2)

            pair_loop(pe, body)

        @g.cur.scalar
        def _(act):
            pl.give(act, "copied", "exped")

            def exp(h, j):
                pl.wait(act, "minned", h * NT + (j + 1))
                w = KEYS[j % NT][1] * P
                act.activation(S[:, j % 2, 0:w], ps_s[:, j % 2, 0:w], ACT.Exp, bias=mins[:, j % 3:j % 3 + 1], scale=-1.0,
                               accum_out=sums[:, j % NT // 2, j % 2:j % 2 + 1]).then_inc(pl["exped"], 1)

            def hi(h, j):
                if j % 2 == 0:
                    pl.wait(act, "weighed", h * NG + (j // 2 - 1))
                for b in range(ML_BATCHES[j % NT]):
                    q = bat(j) + b
                    pl.wait(act, "turned", h * nb + (q + 1))
                    act.copy(PT[0][:, j // 2 % 2, 4 * b:4 * b + 4, j % 2 * P:(j % 2 + 1) * P],
                             ps_t[:, q % 2].rearrange("p (c k) -> p c k", k=P)).then_inc(pl["hi"], 1)

            def body(h, steps, live):
                for step in steps:
                    if live(step - 2):
                        hi(h, step - 2)
                    if step % 2 and live(step - 5):
                        act_copy(act, h * NG, (step - 5) // 2)
                    if live(step):
                        exp(h, step)

            pair_loop(act, body)

        @g.cur.vector
        def _(dve):
            pl.give(dve, "lo", "reduced")

            def minimum(h, j):
                pl.wait(dve, "scored", h * NT + (j + 1))
                dve.tensor_reduce(mins[:, j % 3:j % 3 + 1], ps_s[:, j % 2, 0:KEYS[j % NT][1] * P], AX.X, ALU.min).then_inc(pl["minned"], 1)

            def lo(h, j):
                for b in range(ML_BATCHES[j % NT]):
                    q = bat(j) + b
                    pl.wait(dve, "hi", h * nb + (q + 1))
                    at = lambda part: PT[part][:, j // 2 % 2, 4 * b:4 * b + 4, j % 2 * P:(j % 2 + 1) * P]
                    dve.tensor_tensor(at(1), ps_t[:, q % 2].rearrange("p (c k) -> p c k", k=P), at(0).bitcast(F32),
                                      ALU.subtract).then_inc(pl["lo"], 1)

            def body(h, steps, live):
                for step in steps:
                    if live(step):
                        minimum(h, step)
                    if step % 2 and live(step - 9):
                        q = (step - 9) // 2
                        dst = out[:, 2 * (q % NG):2 * (q % NG) + 2, bass.ds(h * DH + q // NG * DH, DH)]
                        dve_norm(dve, h * NG, q, dst)
                    if step % 2 == 0 and live(step - 8):
                        dve_add(dve, h * NG, (step - 8) // 2)
                    if live(step - 2):
                        lo(h, step - 2)

            pair_loop(dve, body)
        g.end()



def build(nc, io, phases=99):
    with ExitStack() as stack:
        g = Ctx(nc, stack)
        g.x, g.y, g.wall, g.dw, g.rpb, g.cln, g.lat_g = (io[n] for n in ("x", "y", "wall", "dw", "rpb", "cln", "lat_g"))
        g.g_pre_cols, g.g_pre_row, g.g_post = io["g_pre_cols"], io["g_pre_row"], io["g_post"]
        g.c_ident, g.c_cmask, g.c_imask, g.c_rope_k, g.c_qscale, g.c_dft_ch, g.c_alt, g.c_altc = (
            io["c_" + n] for n in ("ident", "cmask", "imask", "rope_k", "qscale", "dft_ch", "alt", "altc"))
        g.dram()
        g.raw = g.sb("w_raw", [P, 2, QCOLS])
        g.W = [g.sb("w_hi_part", [P, 2, PAIRCOLS], F32R), g.sb("w_lo_part", [P, 2, PAIRCOLS], F32R)]
        g.ident = g.sb("ident", [P, P])
        g.zero = g.sb("zero", [P, 1])
        g.zero3 = g.zero[:].rearrange("p (a b) -> p a b", a=1).broadcast_to([P, NT, DH])
        g.mhalf = g.sb("minus_half", [P, 1])
        ring_sem = lambda name: nc.alloc_semaphore(name=name)
        g.raw_loaded = [ring_sem("raw_loaded0"), ring_sem("raw_loaded1")]
        g.w_hi, g.w_ready = ring_sem("w_hi"), ring_sem("w_ready")

        def with_rows(name, *fs):
            with nc.sbuf_tensor(f"{name}_xt_hi", [P, KC, TOK], F32R) as hi, nc.sbuf_tensor(f"{name}_xt_lo", [P, KC, TOK], F32R) as lo:
                g.XT = [hi, lo]
                for f in fs:
                    f()

        def with_operands(*fs):
            with ExitStack() as st:
                ml = Operands(g, st)
                for f in fs:
                    f(g, ml)

        steps = [
            lambda: with_rows("l0in", lambda: prologue(g), lambda: in_even(g)),
            lambda: natten(g),
            lambda: with_rows("l0out", lambda: out_proj(g, 0), lambda: gate(g, 0), lambda: in_odd(g)),
            lambda: (g.renew_semaphores(), latent(g)),
            lambda: with_operands(fnet, mla),
            lambda: with_rows("l1out", lambda: out_proj(g, 1), lambda: gate(g, 1)),
        ]
        for f in steps[:phases]:
            f()


def lay_out(inputs):
    f = {k: np.ascontiguousarray(np.asarray(v)) for k, v in inputs.items()}
    chunks = lambda w: w.reshape(-1, P, w.shape[-1]).transpose(1, 0, 2).reshape(P, -1)

    def pair(*parts):
        a = np.concatenate([chunks(x) for x in parts], axis=1)
        return np.concatenate([a, np.zeros((P, PAIRCOLS - a.shape[1]), np.float32)], axis=1)

    pT = [np.concatenate([f["p_prompt"][l, 0], f["p_sample"][l, 0]], 0).T for l in range(2)]
    we, wo = f["w_in_e"][0], f["w_in_o"][0]
    q, k, v, ga, ua, ub, gb = np.split(we, 7, axis=1)
    cq, ckv, kr, gc, fi, gd = np.split(wo, [256, 384, 416, 928, 1440], axis=1)
    swap = lambda w: np.concatenate([w[..., ROPE // 2:], w[..., :ROPE // 2]], -1)
    uq = f["w_uq"][0].reshape(256, HEADS, DH + ROPE)
    uq = np.concatenate([uq, swap(uq[..., DH:])], -1).reshape(256, HEADS * P)
    ukv = f["w_ukv"][0].reshape(P, HEADS, 2 * DH)
    un, uv = ukv[..., :DH].reshape(P, 512), ukv[..., DH:].reshape(P, 512)
    ublk = lambda c: [ub[:, c * P:(c + 1) * P], ua[:, c * P:(c + 1) * P]]
    by = {
        "u0": pair(np.concatenate(ublk(0) + ublk(1), 1)), "u1": pair(np.concatenate(ublk(2) + ublk(3), 1)),
        "q": pair(q), "v": pair(v), "k": pair(k), "ga": pair(ga), "gb": pair(gb),
        "lat": pair(np.concatenate([cq, ckv, kr, swap(kr), np.zeros((D, 64), np.float32)], 1)),
        "gc": pair(gc), "f": pair(fi), "gd": pair(gd),
    }
    for l in range(2):
        by[f"ple{l}_w"] = pair(f["w_ple"][l], pT[l][:, 1024:])
        by[f"ple{l}_p"] = pair(pT[l][:, :1024])
        w_out = f["w_out_e" if l == 0 else "w_out_o"][0]
        for h, c in (("a", 0), ("b", 1)):
            by[f"out{l}_{h}"] = pair(w_out[:, c * HALF:(c + 1) * HALF])
            by[f"gate{l}_{h}"] = pair(f["w_ple_gate"][l][:, c * HALF:(c + 1) * HALF])

    def dft(n, fn):
        a = np.arange(n // 2)
        return (fn(2 * np.pi * (np.outer(a, a) % n) / n) * 0.5 / np.sqrt(n * P)).astype(np.float32)

    by["up"] = pair(uq, un, uv, dft(512, np.cos), dft(512, np.sin))
    by["dft"] = pair(dft(1024, np.cos), dft(1024, np.sin))
    a = np.outer(np.arange(P), np.arange(P)) % P * (2 * np.pi / P)
    dft_ch = np.concatenate([np.cos(a), -np.sin(a)], 1).astype(np.float32)
    alt = np.zeros((P, 513), np.float32)
    alt[:] = 1.0 - 2.0 * (np.arange(513) % 2)
    alts = np.stack([alt * np.float32(0.5 / np.sqrt(n * P)) for n in SEQS])
    altc = np.stack([(1.0 - 2.0 * (np.arange(P) % 2)) * 0.5 / np.sqrt(n * P) for n in SEQS], 1).astype(np.float32)

    pos = np.concatenate([np.arange(s, dtype=np.float32) for s in SEQS])
    inv = (np.float32(10000.0) ** (-np.arange(0, ROPE, 2, dtype=np.float32) / np.float32(ROPE))).astype(np.float32)
    ang = pos[:, None] * inv[None, :]
    cos, sin = np.cos(ang).astype(np.float32), np.sin(ang).astype(np.float32)
    rope_k = np.concatenate([cos, cos, -sin, sin], 1).reshape(NT, P, 2 * ROPE).transpose(1, 0, 2)
    c = np.float32((DH + ROPE) ** -0.5)
    qscale = np.full((P, TOK), -c, np.float32)
    qscale[DH:] = -c * np.concatenate([cos, cos, -sin, sin], 1).T

    qc = np.arange(P) % GRID
    cs = np.clip(qc - 8, 0, GRID - 16)
    kc = np.arange(GRID)
    cmask = np.where((kc[None] >= cs[:, None]) & (kc[None] < cs[:, None] + 16), 0.0, BIG).astype(np.float32)
    imask = np.zeros((P, 10, GRID), np.float32)
    imask[:, 9] = BIG
    imask[:64, 8] = BIG
    imask[64:, 0] = BIG
    rpb = np.zeros((HEADS, 15, P), np.float32)
    rpb[:, :, 48:79] = f["rpb"][0]

    dw = np.concatenate([f["dw_w"][0].T, f["dw_b"][0][:, None]], 1).reshape(4, P, TAPS + 1).transpose(1, 0, 2)
    cols = lambda v: v.reshape(-1, P).T
    arrays = {
        "x": np.concatenate([f["x_prompt"][0], f["x_sample"][0]], 0),
        "wall": np.stack([by[n] for n in PAIRS]),
        "c_ident": np.eye(P, dtype=np.float32),
        "g_pre_cols": cols(f["g_pre"][0]), "g_pre_row": f["g_pre"][1:2], "g_post": f["g_post"],
        "cln": np.stack([f["cln_g"][0], f["cln_b"][0]]),
        "lat_g": np.concatenate([cols(f["q_norm_g"][0]), cols(f["kv_norm_g"][0])], 1),
        "dw": dw, "rpb": rpb, "c_cmask": cmask, "c_imask": imask.reshape(P, 640),
        "c_rope_k": rope_k, "c_qscale": qscale, "c_dft_ch": dft_ch, "c_alt": alts[:, :1].copy(), "c_altc": altc,
    }
    return {k: np.ascontiguousarray(v, np.float32) for k, v in arrays.items()}


def kernel(**inputs):
    import concourse.bacc as bacc
    from concourse.bass_utils import run_bass_kernel_spmd as run

    nc = bacc.Bacc("TRN2", target_bir_lowering=False, num_devices=1, dynamic_dma_scratch_size=1024)
    arrays = lay_out(inputs)
    io = {n: nc.dram_tensor(n, a.shape, F32, kind="ExternalInput").ap() for n, a in arrays.items()}
    io["y"] = nc.dram_tensor("y", (TOK, D), F32, kind="ExternalOutput").ap()
    build(nc, io)
    y = run(nc, [arrays], core_ids=[0]).results[0]["y"]
    return y[:SEQS[0]][None], y[SEQS[0]:][None]
```

```python
from contextlib import ExitStack

import concourse.bass as bass
from concourse import mybir
import numpy as np

F32 = mybir.dt.float32
F32R = mybir.dt.float32r
ALU = mybir.AluOpType
ACT = mybir.ActivationFunctionType
AX = mybir.AxisListType

P = 128
D = 1024
SEQS = (1024, 512)
TOK = sum(SEQS)
NT = TOK // P
NB = TOK // 512
KC = D // P
HALF = 512
HEADS = 8
DH = 64
ROPE = 32
PLE = 256
GRID = 64
TAPS = 31
PAD = TAPS // 2
EPS = 1e-6
BIG = 1e30
PAIRCOLS = KC * HALF
QCOLS = PAIRCOLS // 4

PAIRS = ["u0", "q", "v", "u1", "k", "ga", "gb",
         "out0_a", "out0_b", "gate0_a", "gate0_b",
         "lat", "gc", "f", "gd",
         "up", "dft",
         "out1_a", "out1_b", "gate1_a", "gate1_b"]
PIDX = {n: i for i, n in enumerate(PAIRS)}
QBASE = [4 * i for i in range(len(PAIRS) + 1)]

THREE = ((0, 0), (0, 1), (1, 0))


class Ctx:

    def __init__(self, nc, stack):
        self.nc = nc
        self.stack = stack
        self.sems = []

    def block(self, name):
        self.cm = self.nc.Block()
        self.cur = self.cm.__enter__()
        return self.cur

    def end(self):
        self.cm.__exit__(None, None, None)

    def sem(self, name):
        s = self.nc.alloc_semaphore(name=name)
        self.sems.append(s)
        return s

    def renew_semaphores(self):
        self.nc.clear_and_free_semaphores(self.sems)
        self.nc.all_engine_barrier()
        self.sems = []

    def dram(self):
        d = lambda name, *shape: self.nc.dram_tensor(name, list(shape), F32).ap()
        self.q = d("q_parts", 2, HALF, TOK)
        self.k = d("k_parts", 2, HALF, TOK)
        self.v = d("v_parts", 2, TOK, HALF)
        self.gate_a = d("gate_a", TOK, HALF)
        self.gate_b = d("gate_b", TOK, HALF)
        self.bias = d("bias_by_distance", HEADS, P, 14 * GRID)
        self.conv = d("conv_fm", 4, P, TOK)
        self.attn = [d(f"attn{l}", TOK, HALF) for l in range(2)]
        self.o = d("o_half", TOK, HALF)
        self.x1 = d("x1", TOK, D)
        self.x2 = d("x2", TOK, D)
        self.lat = d("latents", TOK, HALF)
        self.gate_c = d("gate_c", TOK, HALF)
        self.f = d("f_fm", 4, P, TOK)
        self.gate_d = d("gate_d_fm", 4, P, TOK)
        self.qs = d("mla_q", HEADS, P, TOK)
        self.kn = d("mla_kn", HEADS, DH, TOK)
        self.kr = d("mla_kr", ROPE, TOK)
        self.vv = d("mla_v", TOK, HALF)
        self.dmix = d("fnet_out", 4, P, TOK)

    def sb(self, name, shape, dt=F32):
        return self.stack.enter_context(self.nc.sbuf_tensor(name, shape, dt))


def tiles_of(ap, t):
    return ap[t * P:(t + 1) * P, :]



def load_quarter(g, sp, n):
    pair = max(i for i in range(len(PAIRS)) if QBASE[i] <= n)
    off = (n - QBASE[pair]) * QCOLS
    if n >= 2:
        sp.wait_ge(g.w_ready, n - 1)
    sp.dma_start(g.raw[:, n % 2, :], g.wall[pair, :, off:off + QCOLS]).then_inc(g.raw_loaded[n % 2], 16)


def split_quarter(g, pool, n):
    pair = max(i for i in range(len(PAIRS)) if QBASE[i] <= n)
    off = (n - QBASE[pair]) * QCOLS
    hi = g.W[0][:, pair % 2, off:off + QCOLS]
    lo = g.W[1][:, pair % 2, off:off + QCOLS]
    raw = g.raw[:, n % 2, :]
    pool.wait_ge(g.raw_loaded[n % 2], 16 * (n // 2 + 1))
    pool.tensor_tensor(hi, raw, g.zero[:, 0:1].broadcast_to([P, QCOLS]), ALU.add).then_inc(g.w_hi, 1)
    pool.wait_ge(g.w_hi, n + 1)
    pool.tensor_tensor(lo, raw, hi.bitcast(F32), ALU.subtract).then_inc(g.w_ready, 1)


def quarters(name):
    i = PIDX[name]
    return range(QBASE[i], QBASE[i + 1])


def wait_pair(g, pe, name):
    pe.wait_ge(g.w_ready, QBASE[PIDX[name] + 1])


def wait_quarter(g, pe, name, j, k):
    if j == 0 and k % 2 == 0:
        pe.wait_ge(g.w_ready, QBASE[PIDX[name]] + k // 2 + 1)


def w_at(g, name, part, lo, n):
    return g.W[part][:, PIDX[name] % 2, lo:lo + n]


def rms_scale(pool, g, ss, n, done, base):
    w = ss.shape[-1]
    pool.tensor_scalar(ss, ss, 1.0 / n, EPS, ALU.mult, ALU.add).then_inc(done, 1)
    pool.wait_ge(done, base + 1)
    pool.tensor_tensor(ss, ss, g.mhalf[:, 0:1].broadcast_to([P, w]), ALU.pow).then_inc(done, 1)



def prologue(g):
    nc = g.nc
    with ExitStack() as st:
        sb = lambda name, shape, dt=F32: st.enter_context(nc.sbuf_tensor(name, shape, dt))
        x = sb("pro_x", [P, NT, D])
        gpre = sb("pro_gpre", [P, KC])
        ss = sb("pro_ss", [P, NT])
        pt = st.enter_context(nc.psum_tensor("pro_pt", [P, 4, HALF], F32))
        junk = st.enter_context(nc.psum_tensor("pro_junk", [P, D], F32))
        ident_in, x_in, gpre_in = g.sem("ident_in"), [g.sem(f"pro_x_in{t}") for t in range(NT)], g.sem("pro_gpre_in")
        zeroed = g.sem("zeroed")
        squared, scaled, scaling, htr, h_hi, h_lo = [g.sem("pro_" + n) for n in ("squared", "scaled", "scaling", "htr", "h_hi", "h_lo")]
        UNITS = [(k, b) for b in range(NB) for k in range(KC)]

        @g.block("prologue").sync
        def _(sp):
            for t in range(NT):
                sp.dma_start(x[:, t], tiles_of(g.x, t)).then_inc(x_in[t], 16)
                if t == 1:
                    sp.dma_start(g.ident[:], g.c_ident).then_inc(ident_in, 16)
                    sp.dma_start(gpre[:], g.g_pre_cols).then_inc(gpre_in, 16)
            load_quarter(g, sp, 0)
            load_quarter(g, sp, 1)

        @g.cur.gpsimd
        def _(pool):
            pool.memset(g.zero[:], 0.0).then_inc(zeroed, 1)
            pool.memset(g.mhalf[:], -0.5).then_inc(zeroed, 1)
            pool.wait_ge(zeroed, 2)
            for b in range(NB):
                pool.wait_ge(squared, 4 * (b + 1))
                rms_scale(pool, g, ss[:, 4 * b:4 * b + 4], D, scaling, 2 * b)

        @g.cur.scalar
        def _(act):
            def squares(b):
                for t in range(4 * b, 4 * b + 4):
                    act.wait_ge(x_in[t], 16)
                    if t:
                        act.wait_ge(squared, t)
                    act.activation(junk[:], x[:, t], ACT.Square, accum_out=ss[:, t:t + 1]).then_inc(squared, 1)

            squares(0)
            squares(1)
            act.wait_ge(gpre_in, 16)
            for v, (k, b) in enumerate(UNITS):
                if v == 6:
                    squares(2)
                act.wait_ge(htr, v + 1)
                act.activation(g.XT[0][:, k, b * 512:(b + 1) * 512], pt[:, v % 4], ACT.Copy,
                               scale=gpre[:, k:k + 1]).then_inc(h_hi, 1)

        @g.cur.vector
        def _(dve):
            def scale_rows(b):
                dve.wait_ge(scaling, 2 * (b + 1))
                for t in range(4 * b, 4 * b + 4):
                    dve.tensor_scalar(x[:, t], x[:, t], ss[:, t:t + 1], None, ALU.mult).then_inc(scaled, 1)

            scale_rows(0)
            scale_rows(1)
            dve.wait_ge(gpre_in, 16)
            for v, (k, b) in enumerate(UNITS):
                if v == 10:
                    scale_rows(2)
                dve.wait_ge(h_hi, v + 1)
                dve.scalar_tensor_tensor(g.XT[1][:, k, b * 512:(b + 1) * 512], pt[:, v % 4], gpre[:, k:k + 1],
                                         g.XT[0][:, k, b * 512:(b + 1) * 512].bitcast(F32),
                                         ALU.mult, ALU.subtract).then_inc(h_lo, 1)

        @g.cur.tensor
        def _(pe):
            pe.wait_ge(ident_in, 16)
            for v, (k, b) in enumerate(UNITS):
                pe.wait_ge(scaled, 4 * (b + 1))
                if v >= 4:
                    pe.wait_ge(h_lo, v - 3)
                for j in range(4):
                    tr = pe.transpose(pt[:, v % 4, j * P:(j + 1) * P], x[:, 4 * b + j, k * P:(k + 1) * P], g.ident[:])
                tr.then_inc(htr, 1)
        g.end()



UOFF = (PAD, PAD + 512, 2 * PAD + 1024)
UW = 3 * PAD + TOK
CW = PAD + TOK


def project(g, pe, name, fm, order, psum, unit0, free, done, banks=8):
    for j in range(12):
        u = unit0 + j
        free(pe, u)
        i = 0
        for k in range(KC):
            wait_quarter(g, pe, name, j, k)
            for a, m in THREE:
                if fm:
                    c, b = order[j]
                    mm = pe.matmul(psum[:, u % banks], w_at(g, name, a, k * HALF + c * P, P),
                                   g.XT[m][:, k, b * 512:(b + 1) * 512], start=i == 0, stop=i == 3 * KC - 1)
                else:
                    mm = pe.matmul(psum[:, u % banks], g.XT[a][:, k, j * P:(j + 1) * P],
                                   w_at(g, name, m, k * HALF, HALF), start=i == 0, stop=i == 3 * KC - 1)
                i += 1
        mm.then_inc(done, 1)


FM_ORDER = [(c, b) for c in range(4) for b in range(NB)]
U_ORDER = [(2 * cc + s, b) for cc in range(2) for b in range(NB) for s in range(2)]


def in_even(g):
    nc = g.nc
    names = ["u0", "q", "v", "u1", "k", "ga", "gb"]
    with ExitStack() as st:
        sb = lambda name, shape, dt=F32: st.enter_context(nc.sbuf_tensor(name, shape, dt))
        stage = sb("ie_stage", [P, 4, HALF])
        stage_hi = sb("ie_stage_hi", [P, 4, HALF], F32R)
        th = sb("ie_tanh", [P, 2, HALF])
        ubuf = sb("ie_u", [P, 2, UW])
        acc = sb("ie_acc", [P, CW])
        wconv = sb("ie_wconv", [P, 4, TAPS + 1])
        ps = st.enter_context(nc.psum_tensor("ie_ps", [P, 8, HALF], F32))
        mm_done, cw_in, bias_out = g.sem("ie_mm"), g.sem("ie_cw_in"), g.sem("ie_bias_out")
        ev_act, ev_dve, tanhed = g.sem("ie_ev_act"), g.sem("ie_ev_dve"), g.sem("ie_tanhed")
        stored = [g.sem(f"ie_stored{i}") for i in range(4)]
        hi_stored = [g.sem(f"ie_hi_stored{i}") for i in range(4)]
        taps, conv_stored, padded = g.sem("ie_taps"), g.sem("ie_conv_stored"), g.sem("ie_padded")

        kinds = []
        for n in names:
            for j in range(12):
                kinds.append("tanh_u" if n[0] == "u" and j % 2 == 0 else "u" if n[0] == "u" else
                             "gate" if n[0] == "g" else "copy")
        by_act = [0]
        by_dve = [0]
        slot = []
        for kd in kinds:
            by_act.append(by_act[-1] + (kd in ("tanh_u", "copy")))
            by_dve.append(by_dve[-1] + (kd != "tanh_u"))
            slot.append(sum(x in ("copy", "gate") for x in kinds[:len(slot)]) if kd in ("copy", "gate") else None)
        n_tanh = [sum(x in ("tanh_u", "gate") for x in kinds[:i]) for i in range(len(kinds) + 1)]
        tanh_used = [by_dve[u + 1 + (kd == "tanh_u")] for u, kd in enumerate(kinds) if kd in ("tanh_u", "gate")]

        CONV_IN = [6, 12, 42, 48]
        TAPS_A_UNIT = 2
        order, cc, s, rest = [], 0, 0, 0
        conv_end = []
        for u in range(len(kinds)):
            order.append(("unit", u))
            if u < rest:
                continue
            for _ in range(TAPS_A_UNIT):
                if cc < 4 and u + 1 >= CONV_IN[cc] and u >= rest:
                    order.append(("tap", (cc, s)))
                    s += 1
                    if s > TAPS:
                        conv_end.append(u)
                        cc, s, rest = cc + 1, 0, u + 2

        SCALE = {"q": -DH ** -0.5, "v": 0.5, "k": 1.0}

        def free(pe, u):
            if u >= 8:
                if kinds[u - 8] == "tanh_u":
                    pe.wait_ge(ev_act, by_act[u - 7])
                else:
                    pe.wait_ge(ev_dve, by_dve[u - 7])

        def dest(u, part):
            n, j = names[u // 12], u % 12
            if n in ("q", "k"):
                c, b = FM_ORDER[j]
                return (g.q if n == "q" else g.k)[part, c * P:(c + 1) * P, b * 512:(b + 1) * 512]
            return tiles_of(g.v[part] if n == "v" else g.gate_a if n == "ga" else g.gate_b, j)

        def store_conv(sp, cc):
            sp.wait_ge(taps, (TAPS + 1) * (cc + 1))
            sp.dma_start(g.conv[cc, :, 0:1024], acc[:, 0:1024]).then_inc(conv_stored, 16)
            sp.dma_start(g.conv[cc, :, 1024:TOK], acc[:, 1024 + PAD:CW]).then_inc(conv_stored, 16)

        @g.block("in_even").sync
        def _(sp):
            load_quarter(g, sp, 2)
            load_quarter(g, sp, 3)
            sp.dma_start(wconv[:], g.dw).then_inc(cw_in, 16)
            for h in range(HEADS):
                for j in range(2):
                    row = g.rpb[h, 1 - j]
                    src = bass.AP(tensor=row.tensor, offset=row.offset + GRID - 1, ap=[[P, 14], [-1, GRID], [1, GRID]])
                    sp.dma_start(g.bias[h, j * GRID:(j + 1) * GRID, :].rearrange("c (d k) -> d c k", k=GRID),
                                 src).then_inc(bias_out, 16)
            for u, kd in enumerate(kinds):
                n, j = names[u // 12], u % 12
                i = PIDX[n]
                if j % 2 == 0 and j < 8 and i + 1 < PIDX["out0_a"]:
                    load_quarter(g, sp, QBASE[i + 1] + j // 2)
                if kd in ("copy", "gate"):
                    sp.wait_ge(ev_dve, by_dve[u + 1])
                    sp.dma_start(dest(u, 1), stage[:, slot[u] % 4]).then_inc(stored[slot[u] % 4], 16)
                    if kd == "copy":
                        sp.dma_start(dest(u, 0), stage_hi[:, slot[u] % 4].bitcast(F32)).then_inc(hi_stored[slot[u] % 4], 16)
                if u in conv_end:
                    store_conv(sp, conv_end.index(u))
            for i in range(4):
                sp.wait_ge(stored[i], 16 * (sum(x in ("copy", "gate") for x in kinds) // 4))
                sp.wait_ge(hi_stored[i], 16 * (kinds.count("copy") // 4))
            sp.wait_ge(conv_stored, 16 * 8)
            sp.wait_ge(bias_out, 16 * 2 * HEADS)

        first = lambda part, n: w_at(g, names[0], part, n * QCOLS, QCOLS)

        @g.cur.gpsimd
        def _(pool):
            pool.wait_ge(g.w_ready, 4)
            for i, n in enumerate(names[:-1]):
                for q in quarters(names[i + 1]):
                    if i >= 1 and q == QBASE[PIDX[names[i + 1]]]:
                        pool.wait_ge(mm_done, 12 * i)
                    split_quarter(g, pool, q)

        @g.cur.scalar
        def _(act):
            for n in range(4):
                act.wait_ge(g.raw_loaded[n % 2], 16 * (n // 2 + 1))
                act.copy(first(0, n), g.raw[:, n % 2]).then_inc(g.w_hi, 1)
            for u, kd in enumerate(kinds):
                if kd == "u":
                    continue
                act.wait_ge(mm_done, u + 1)
                if kd in ("tanh_u", "gate"):
                    i = n_tanh[u]
                    if i >= 2:
                        act.wait_ge(ev_dve, tanh_used[i - 2])
                    w = act.activation(th[:, i % 2], ps[:, u % 8], ACT.Tanh, scale=0.5)
                    w.then_inc(tanhed if kd == "gate" else ev_act, 1)
                else:
                    s = slot[u]
                    if s >= 4:
                        act.wait_ge(hi_stored[s % 4], 16 * (s // 4))
                    act.activation(stage_hi[:, s % 4], ps[:, u % 8], ACT.Copy, scale=SCALE[names[u // 12]]).then_inc(ev_act, 1)

        @g.cur.vector
        def _(dve):
            for n in range(4):
                dve.wait_ge(g.w_hi, n + 1)
                dve.tensor_tensor(first(1, n), g.raw[:, n % 2], first(0, n).bitcast(F32), ALU.subtract).then_inc(g.w_ready, 1)
            dve.memset(ubuf[:], 0.0).then_inc(padded, 1)
            dve.wait_ge(padded, 1)

            def u_unit(u):
                n, j = names[u // 12], u % 12
                cc = 2 * (n == "u1") + j // 6
                b = j // 2 % 3
                dve.wait_ge(mm_done, u + 1)
                dve.wait_ge(ev_act, by_act[u])
                i = n_tanh[u] - 1
                dve.scalar_tensor_tensor(ubuf[:, cc % 2, UOFF[b]:UOFF[b] + 512], th[:, i % 2], 1.0, ps[:, u % 8],
                                         ALU.add, ALU.mult).then_inc(ev_dve, 1)

            def gate_unit(u):
                s = slot[u]
                i = n_tanh[u]
                dve.wait_ge(tanhed, 1 + sum(x == "gate" for x in kinds[:u]))
                if s >= 4:
                    dve.wait_ge(stored[s % 4], 16 * (s // 4))
                dve.scalar_tensor_tensor(stage[:, s % 4], th[:, i % 2], 1.0, ps[:, u % 8],
                                         ALU.add, ALU.mult).then_inc(ev_dve, 1)

            def conv_step(cc, s):
                base = (TAPS + 1) * cc + s
                if s == 0:
                    dve.wait_ge(ev_dve, by_dve[CONV_IN[cc]])
                    if cc == 0:
                        dve.wait_ge(cw_in, 16)
                    else:
                        dve.wait_ge(conv_stored, 32 * cc)
                    dve.tensor_scalar(acc[:], ubuf[:, cc % 2, 0:CW], wconv[:, cc, 0:1], None, ALU.mult).then_inc(taps, 1)
                    return
                dve.wait_ge(taps, base)
                if s < TAPS:
                    dve.scalar_tensor_tensor(acc[:], ubuf[:, cc % 2, s:s + CW], wconv[:, cc, s:s + 1], acc[:],
                                             ALU.mult, ALU.add).then_inc(taps, 1)
                else:
                    dve.tensor_scalar(acc[:], acc[:], 0.5, wconv[:, cc, TAPS:TAPS + 1], ALU.mult, ALU.add).then_inc(taps, 1)

            def lo_unit(u):
                sl = slot[u] % 4
                dve.wait_ge(ev_act, by_act[u + 1])
                if slot[u] >= 4:
                    dve.wait_ge(stored[sl], 16 * (slot[u] // 4))
                dve.scalar_tensor_tensor(stage[:, sl], ps[:, u % 8], SCALE[names[u // 12]], stage_hi[:, sl].bitcast(F32),
                                         ALU.mult, ALU.subtract).then_inc(ev_dve, 1)

            steps = {"u": u_unit, "gate": gate_unit, "copy": lo_unit, "tanh_u": lambda u: None}
            for what, arg in order:
                if what == "unit":
                    steps[kinds[arg]](arg)
                else:
                    conv_step(*arg)

        @g.cur.tensor
        def _(pe):
            for i, n in enumerate(names):
                project(g, pe, n, n[0] in "uqk", U_ORDER if n[0] == "u" else FM_ORDER, ps, 12 * i, free, mm_done)
        g.end()



class Tile:
    def __init__(self, i):
        base, rows, r = (0, 16, 2 * i) if i < 8 else (8, 8, 2 * (i - 8))
        self.shifted = rows > 8 and 4 <= r <= 10
        first = r - 4 if self.shifted else min(max(r - 4, 0), rows - 8)
        self.width = 10 * GRID if self.shifted else 8 * GRID
        self.key0 = base * P + first * GRID
        self.chunk0 = base + first // 2
        self.table = (first - r + 6) * GRID
        self.batches = (3, 2) if self.shifted else (4,)


NA_TILES = [Tile(i) for i in range(NT)]
NA_GROUP0 = [min(NA_TILES[2 * q].chunk0, NA_TILES[2 * q + 1].chunk0) for q in range(NT // 2)]
NA_SPAN = [6 if NA_TILES[2 * q].shifted else 4 for q in range(NT // 2)]
NG = NT // 2
NBAT = sum(len(t.batches) for t in NA_TILES)


class Pipeline:

    CREDITS = {"scored": 0, "minned": 2, "exped": 0, "turned": 3, "hi": 0, "lo": 2, "weighed": NG + 1,
              "copied": 1, "back": 2, "reduced": 1, "inverted": 0, "normed": 0, "prepped": 1}

    def __init__(self, g, name, **credits):
        self.CREDIT = {**self.CREDITS, **credits}
        self.sems = {n: g.sem(f"{name}_{n}") for n in self.CREDIT}

    def __getitem__(self, name):
        return self.sems[name]

    def give(self, eng, *names):
        for n in names:
            if self.CREDIT[n]:
                eng.sem_inc(self[n], self.CREDIT[n])

    def wait(self, eng, name, count):
        eng.wait_ge(self[name], count + self.CREDIT[name])


J = 2 * NT
DRAIN = 10


def pair_loop(eng, body):
    body(0, range(J), lambda i: 0 <= i < J)
    with eng.Fori(1, HEADS // 2) as pair:
        body(pair * 2, range(J), lambda i: True)
    body(HEADS - 2, range(J, J + DRAIN), lambda i: i < J)


def attention_tail(g, pl, ps_pv, ps_back, pv_sb, sums, rinv, red, out):
    def act_copy(act, h6, q):
        pl.wait(act, "weighed", h6 + q + 1)
        pl.wait(act, "back", h6 + q - 1)
        act.copy(pv_sb[:, q % 2], ps_pv[:, 0:256]).then_inc(pl["copied"], 1)

    def pe_back(pe, h6, q):
        pl.wait(pe, "copied", h6 + q + 1)
        pl.wait(pe, "reduced", h6 + q)
        for a in range(2):
            tr = pe.transpose(ps_back[:, a * P:(a + 1) * P], pv_sb[:, q % 2, a * P:(a + 1) * P], g.ident[:])
        tr.then_inc(pl["back"], 1)

    def dve_add(dve, h6, q):
        dve.reciprocal(rinv[:, q % 2], sums[:, q % NG]).then_inc(pl["inverted"], 1)
        pl.wait(dve, "back", h6 + q + 1)
        dve.tensor_reduce(red[:, q % 2], ps_back[:, 0:256].rearrange("p (a two d) -> p a d two", a=2, two=2), AX.X,
                          ALU.add).then_inc(pl["reduced"], 1)

    def dve_norm(dve, h6, q, dst):
        pl.wait(dve, "reduced", h6 + q + 1)
        pl.wait(dve, "inverted", h6 + q + 1)
        dve.tensor_tensor(dst, red[:, q % 2], rinv[:, q % 2].rearrange("p (a o) -> p a o", o=1).broadcast_to([P, 2, DH]),
                          ALU.mult).then_inc(pl["normed"], 1)
    return act_copy, pe_back, dve_add, dve_norm


def natten(g):
    nc = g.nc
    with ExitStack() as st:
        sb = lambda name, shape, dt=F32: st.enter_context(nc.sbuf_tensor(name, shape, dt))
        xt = sb("na_xt", [P, 2, 14 * GRID])
        Q = sb("na_q", [P, 2, TOK], F32R)
        K = [sb("na_k_hi", [P, 2, TOK], F32R), sb("na_k_lo", [P, 2, TOK], F32R)]
        V = sb("na_v", [P, 2, NT, P], F32R)
        T = sb("na_table", [P, 2, 14 * GRID])
        TS = sb("na_table_shifted", [P, 2, 10 * GRID])
        cmask, imask = sb("na_cmask", [P, GRID]), sb("na_imask", [P, 10 * GRID])
        S = sb("na_s", [P, 3, 10 * GRID])
        mins, tick = sb("na_min", [P, 3]), sb("na_tick", [P, 3])
        sums = sb("na_sums", [P, NG, 2])
        rinv = sb("na_rinv", [P, 2, 2])
        red = sb("na_red", [P, 2, 2, DH])
        PT = [sb("na_pt_hi", [P, 2, 6, 256], F32R), sb("na_pt_lo", [P, 2, 6, 256], F32R)]
        pv_sb = sb("na_pv", [P, 2, 256])
        out = sb("na_out", [P, NT, HALF])
        ps_s = st.enter_context(nc.psum_tensor("na_ps_s", [P, 2, 2, HALF], F32))
        ps_t = st.enter_context(nc.psum_tensor("na_ps_t", [P, 2, HALF], F32))
        ps_pv = st.enter_context(nc.psum_tensor("na_ps_pv", [P, HALF], F32))
        ps_back = st.enter_context(nc.psum_tensor("na_ps_back", [P, HALF], F32))
        pl = Pipeline(g, "na")
        qk_in = [[g.sem(f"na_qk_in{s}{i}") for i in range(2)] for s in range(2)]
        v_in, xt_in = [g.sem("na_v_in0"), g.sem("na_v_in1")], [g.sem("na_xt_in0"), g.sem("na_xt_in1")]
        QK_IN, V_IN = 16 * 6, 16 * 2
        masks_in, cleared, attn_out = [g.sem("na_cmask_in"), g.sem("na_imask_in")], g.sem("na_cleared"), g.sem("na_attn_out")
        act_copy, pe_back, dve_add, dve_norm = attention_tail(g, pl, ps_pv, ps_back, pv_sb, sums, rinv, red, out)

        def bat(j):
            return 2 * NBAT * (j // J) + sum(len(NA_TILES[i % NT].batches) for i in range(j % J))

        @g.block("natten").sync
        def _(sp):
            def load(h, s):
                rows = lambda ap, part: ap[part].rearrange("(h d) t -> h d t", d=DH)[h]
                half = lambda i: slice(i * DH, (i + 1) * DH)
                vcols = half(h) if isinstance(h, int) else bass.ds(h * DH, DH)
                sp.dma_start(xt[:, s], g.bias[h]).then_inc(xt_in[s], 16)
                for group, cols in enumerate((slice(0, SEQS[0]), slice(SEQS[0], TOK))):
                    for i in range(2):
                        sp.dma_start(Q[half(i), s, cols].bitcast(F32), rows(g.q, i)[:, cols]).then_inc(qk_in[s][group], 16)
                        for part in range(2):
                            sp.dma_start(K[part][half(i), s, cols].bitcast(F32), rows(g.k, part)[:, cols]).then_inc(qk_in[s][group], 16)
                    if group == 0 and isinstance(h, int) and h == 0:
                        sp.dma_start(imask[:], g.c_imask).then_inc(masks_in[1], 16)
                for part in range(2):
                    sp.dma_start(V[:, s, :, half(part)].bitcast(F32),
                                 g.v[part].rearrange("(t p) c -> p t c", p=P)[:, :, vcols]).then_inc(v_in[s], 16)

            def store(cols, tiles=slice(0, NT)):
                sp.dma_start(g.attn[0].rearrange("(t p) c -> p t c", p=P)[:, tiles, cols], out[:, tiles, cols]).then_inc(attn_out, 16)

            sp.dma_start(cmask[:], g.c_cmask).then_inc(masks_in[0], 16)
            load(0, 0)
            load(1, 1)
            with sp.Fori(0, HEADS // 2 - 1) as pair:
                for s in range(2):
                    pl.wait(sp, "weighed", pair * 2 * NG + (s + 1) * NG)
                    load(pair * 2 + (s + 2), s)
                pl.wait(sp, "normed", pair * 2 * NG + 2 * NG)
                store(bass.ds(pair * 2 * DH, 2 * DH))
            for n in quarters("out0_a"):
                load_quarter(g, sp, n)
            for q, tiles in ((4, slice(0, 8)), (NG, slice(8, NT))):
                pl.wait(sp, "normed", (HEADS - 1) * NG + q)
                store(slice(HALF - 2 * DH, HALF), tiles)
            sp.wait_ge(attn_out, 16 * (HEADS // 2 + 1))

        @g.cur.gpsimd
        def _(pool):
            pl.give(pool, "prepped")
            pool.wait_ge(masks_in[0], 16)
            with pool.Fori(0, HEADS // 2) as pair:
                h = pair * 2
                for s in range(2):
                    pool.wait_ge(xt_in[s], pair * 16 + 16)
                    pl.wait(pool, "weighed", h * NG + NG * (s - 1))
                    pool.tensor_tensor(T[:, s].rearrange("p (r c) -> p r c", c=GRID),
                                       cmask[:].rearrange("p (o c) -> p o c", o=1).broadcast_to([P, 14, GRID]),
                                       xt[:, s].rearrange("p (r c) -> p r c", c=GRID), ALU.subtract).then_inc(pl["prepped"], 1)
                    pool.wait_ge(masks_in[1], 16)
                    pl.wait(pool, "prepped", h * 2 + 2 * s + 1)
                    pool.tensor_tensor(TS[:, s], T[:, s, 2 * GRID:12 * GRID], imask[:], ALU.add).then_inc(pl["prepped"], 1)
            for n in quarters("out0_a"):
                split_quarter(g, pool, n)

        @g.cur.tensor
        def _(pe):
            pl.give(pe, "turned", "weighed", "back")

            def scores(h, j):
                t, s = NA_TILES[j % NT], j // NT % 2
                if j % NT in (0, 8):
                    pe.wait_ge(qk_in[s][j % NT // 8], h * (QK_IN // 2) + QK_IN)
                pl.wait(pe, "minned", h * NT + (j - 1))
                for half in range(2 if t.shifted else 1):
                    n = 5 * GRID if t.shifted else 8 * GRID
                    for part in range(2):
                        k0 = t.key0 + half * n
                        mm = pe.matmul(ps_s[:, j % 2, half, 0:n], Q[:, s, (j % NT) * P:(j % NT + 1) * P],
                                       K[part][:, s, k0:k0 + n], start=part == 0, stop=part == 1)
                mm.then_inc(pl["scored"], 1)

            def turn(h, j, b):
                batches = NA_TILES[j % NT].batches
                if b == 0:
                    pl.wait(pe, "exped", h * NT + (j + 1))
                q = bat(j) + b
                pl.wait(pe, "lo", h * NBAT + (q - 1))
                for i in range(batches[b]):
                    c = sum(batches[:b]) + i
                    tr = pe.transpose(ps_t[:, q % 2, i * P:(i + 1) * P], S[:, j % 3, c * P:(c + 1) * P], g.ident[:])
                tr.then_inc(pl["turned"], 1)

            def weigh(h, q, half):
                if q % NG == 0 and half == 0:
                    pe.wait_ge(v_in[q // NG % 2], (h + q // (2 * NG) * 2) * (V_IN // 2) + V_IN)
                if half == 0:
                    pl.wait(pe, "lo", h * NBAT + bat(2 * q + 2))
                    pl.wait(pe, "copied", h * NG + q)
                span = NA_SPAN[q % NG]
                c0 = 0 if span == 6 else 1
                for c in range(half * span // 2, (half + 1) * span // 2):
                    for part in range(2):
                        mm = pe.matmul(ps_pv[:, 0:256], V[:, q // NG % 2, NA_GROUP0[q % NG] + c], PT[part][:, q % 2, c0 + c],
                                       start=c + part == 0, stop=c + part == span)
                if half:
                    mm.then_inc(pl["weighed"], 1)

            def body(h, steps, live):
                for step in steps:
                    if live(step):
                        scores(h, step)
                    if live(step - 2):
                        turn(h, step - 2, 0)
                    if live(step - 4 - step % 2):
                        weigh(h, (step - 4) // 2, step % 2)
                    if live(step - 2) and len(NA_TILES[(step - 2) % NT].batches) == 2:
                        turn(h, step - 2, 1)
                    if step % 2 and live(step - 7):
                        pe_back(pe, h * NG, (step - 7) // 2)

            pair_loop(pe, body)

        @g.cur.scalar
        def _(act):
            pl.give(act, "copied")

            def exp(h, j):
                pl.wait(act, "minned", h * NT + (j + 1))
                t = NA_TILES[j % NT]
                act.activation(S[:, j % 3, 0:t.width], S[:, j % 3, 0:t.width], ACT.Exp, bias=mins[:, j % 3:j % 3 + 1], scale=-1.0,
                               accum_out=sums[:, j % NT // 2, j % 2:j % 2 + 1]).then_inc(pl["exped"], 1)

            def hi(h, j):
                t = NA_TILES[j % NT]
                if j % 2 == 0:
                    pl.wait(act, "weighed", h * NG + (j // 2 - 1))
                if j == 0:
                    act.wait_ge(cleared, 4)
                c = t.chunk0 - NA_GROUP0[j % NT // 2] + (not t.shifted)
                for b, n in enumerate(t.batches):
                    q = bat(j) + b
                    pl.wait(act, "turned", h * NBAT + (q + 1))
                    act.copy(PT[0][:, j // 2 % 2, c:c + n, j % 2 * P:(j % 2 + 1) * P],
                             ps_t[:, q % 2, 0:n * P].rearrange("p (c k) -> p c k", k=P)).then_inc(pl["hi"], 1)
                    c += n

            def body(h, steps, live):
                for step in steps:
                    if live(step - 2):
                        hi(h, step - 2)
                    if step % 2 and live(step - 5):
                        act_copy(act, h * NG, (step - 5) // 2)
                    if live(step):
                        exp(h, step)

            pair_loop(act, body)

        @g.cur.vector
        def _(dve):
            pl.give(dve, "minned", "lo", "reduced")
            for part in range(2):
                dve.memset(PT[part][:, :, 5, 0:P].bitcast(F32), 0.0).then_inc(cleared, 1)
                dve.memset(PT[part][:, :, 0, P:2 * P].bitcast(F32), 0.0).then_inc(cleared, 1)

            def before_minimum(h, j):
                if j % NT in (0, 2):
                    pl.wait(dve, "prepped", h * 2 + 2 * (j // NT) + (j % NT or 1))
                pl.wait(dve, "scored", h * NT + (j + 1))
                dve.memset(tick[:, j % 3:j % 3 + 1], 0.0)

            def minimum(h, j):
                t, s = NA_TILES[j % NT], j // NT % 2
                if t.shifted:
                    src, tab = ps_s[:, j % 2, :, 0:5 * GRID], TS[:, s].rearrange("p (a k) -> p a k", a=2)
                    dst = S[:, j % 3].rearrange("p (a k) -> p a k", a=2)
                else:
                    src, tab = ps_s[:, j % 2, 0], T[:, s, t.table:t.table + t.width]
                    dst = S[:, j % 3, 0:t.width]
                dve.tensor_tensor_reduce(dst, src, tab, 1.0, 3e38, ALU.add, ALU.min, mins[:, j % 3:j % 3 + 1]).then_inc(pl["minned"], 1)

            def lo(h, j):
                t = NA_TILES[j % NT]
                c = t.chunk0 - NA_GROUP0[j % NT // 2] + (not t.shifted)
                for b, n in enumerate(t.batches):
                    q = bat(j) + b
                    pl.wait(dve, "hi", h * NBAT + (q + 1))
                    at = lambda part: PT[part][:, j // 2 % 2, c:c + n, j % 2 * P:(j % 2 + 1) * P]
                    dve.tensor_tensor(at(1), ps_t[:, q % 2, 0:n * P].rearrange("p (c k) -> p c k", k=P), at(0).bitcast(F32),
                                      ALU.subtract).then_inc(pl["lo"], 1)
                    c += n

            def body(h, steps, live):
                for step in steps:
                    if live(step):
                        before_minimum(h, step)
                        minimum(h, step)
                    if step % 2 and live(step - 9):
                        q = (step - 9) // 2
                        dst = out[:, 2 * (q % NG):2 * (q % NG) + 2, bass.ds(h * DH + q // NG * DH, DH)]
                        dve_norm(dve, h * NG, q, dst)
                    if step % 2 == 0 and live(step - 8):
                        dve_add(dve, h * NG, (step - 8) // 2)
                    if live(step - 2):
                        lo(h, step - 2)

            pair_loop(dve, body)
        g.end()



def rows_turned(pe, src, dst, ident, n):
    for k in range(n):
        tr = pe.transpose(dst[:, k * P:(k + 1) * P], src[:, k * P:(k + 1) * P], ident)
    return tr


def out_proj(g, l):
    nc = g.nc
    pre = f"op{l}_"
    x_src = g.x if l == 0 else g.x2
    nmix = 8 if l == 0 else 4
    with ExitStack() as st:
        sb = lambda name, shape, dt=F32: st.enter_context(nc.sbuf_tensor(pre + name, shape, dt))
        inb = sb("in", [P, 2, 4, HALF])
        mix = sb("mix", [P, 2, D])
        yb = sb("y", [P, 2, HALF])
        th = sb("tanh", [P, HALF])
        cln = sb("cln", [P, 2, HALF])
        gpost = sb("gpost", [P, D])
        ost = sb("ost", [P, 2, HALF])
        orl = sb("orl", [P, 2, HALF])
        bn = sb("bn", [P, 2, 6])
        mv = sb("mv", [P, 2, 2])
        ss = sb("ss", [P, 2, NT])
        ps_o = st.enter_context(nc.psum_tensor(pre + "ps_o", [P, 2, HALF], F32))
        ps_t = st.enter_context(nc.psum_tensor(pre + "ps_t", [P, 2, D], F32))
        ps_n = st.enter_context(nc.psum_tensor(pre + "ps_n", [P, 2, HALF], F32))
        sem = lambda n: g.sem(pre + n)
        rows_in, cln_in, gpost_in = [sem("rows_in0"), sem("rows_in1")], sem("cln_in"), sem("gpost_in")
        conv_in = [sem("conv_in0"), sem("conv_in1")]
        conv_t, stats, yrow, tanhed, urow = sem("conv_t"), sem("stats"), sem("yrow"), sem("tanhed"), sem("urow")
        cln_ready, mixed = sem("cln_ready"), sem("mixed")
        turned, hi, lo, mm_done = sem("turned"), sem("hi"), sem("lo"), sem("mm")
        staged, squared = sem("staged"), sem("squared")
        pooled = sem("pooled")
        x1_rows = sem("x1_rows")
        stored, x_in, x1_stored = [[sem(f"{n}{i}") for i in range(2)] for n in ("stored", "x_in", "x1_stored")]
        n_in = 3
        L_CONV, L_Y, L_MIX, L_TURN = (4, 3, 2, 1) if l == 0 else (0, 0, 2, 1)
        pool0 = 2 * NT if l == 0 else 0
        nxt = f"gate{l}_a"

        fm_rows = lambda s: inb[:, s, 2].rearrange("p (c t) -> p c t", c=4)

        @g.block(pre + "phase").sync
        def _(sp):
            def load_conv(t):
                if t >= 2:
                    sp.wait_ge(conv_t, t - 1)
                sp.dma_start(fm_rows(t % 2), g.conv[:, :, t * P:(t + 1) * P].rearrange("c p t -> p c t")).then_inc(conv_in[t % 2], 16)

            if l == 0:
                load_conv(0)
                for i in range(2):
                    sp.dma_start(cln[:, i], g.cln[i:i + 1, :].broadcast_to([P, HALF])).then_inc(cln_in, 16)

            def load(t):
                s = t % 2
                if t >= 2:
                    sp.wait_ge(mixed, (2 if l == 0 else 1) * (t - 1))
                    if l == 1:
                        sp.wait_ge(lo, 2 * (t - 1))
                sp.dma_start(inb[:, s, 0], tiles_of(g.attn[l], t)).then_inc(rows_in[s], 16)
                sp.dma_start(inb[:, s, 1], tiles_of(g.gate_a if l == 0 else g.gate_c, t)).then_inc(rows_in[s], 16)
                if l == 0:
                    sp.dma_start(inb[:, s, 3], tiles_of(g.gate_b, t)).then_inc(rows_in[s], 16)
                else:
                    sp.dma_start(fm_rows(s), g.dmix[:, :, t * P:(t + 1) * P].rearrange("c p t -> p c t")).then_inc(rows_in[s], 16)

            second = list(quarters(f"out{l}_b"))
            lag = L_CONV + 1 if l == 0 else 3
            for i in range(NT + lag):
                if l == 0 and i + 1 < NT:
                    load_conv(i + 1)
                if i < NT:
                    load(i)
                if i == 3:
                    sp.dma_start(gpost[:], g.g_post[l:l + 1, :].broadcast_to([P, D])).then_inc(gpost_in, 16)
                if i in (4, 5, 7, 9):
                    load_quarter(g, sp, second.pop(0))
                t = i - lag
                if t >= 0:
                    sp.wait_ge(staged, t + 1)
                    sp.dma_start(tiles_of(g.o, t), ost[:, t % 2]).then_inc(stored[t % 2], 16)
            for n in quarters(nxt)[:2]:
                load_quarter(g, sp, n)
            rest = list(quarters(nxt)[2:])

            def load_x(t):
                s = t % 2
                if t < 2:
                    sp.wait_ge(mixed, (2 if l == 0 else 1) * NT)
                    if l == 1:
                        sp.wait_ge(lo, 2 * NT)
                    sp.wait_ge(stored[s], 16 * NT // 2)
                else:
                    sp.wait_ge(x1_rows, 3 * (t - 1))
                sp.dma_start(inb[:, s, 0:2].rearrange("p a c -> p (a c)"), tiles_of(x_src, t)).then_inc(x_in[s], 16)
                sp.dma_start(orl[:, s], tiles_of(g.o, t)).then_inc(x_in[s], 16)

            load_x(0)
            load_x(1)
            for t in range(NT):
                sp.wait_ge(x1_rows, 3 * (t + 1))
                sp.dma_start(tiles_of(g.x1, t), inb[:, t % 2, 2:4].rearrange("p a c -> p (a c)")).then_inc(x1_stored[t % 2], 16)
                if t + 2 < NT:
                    load_x(t + 2)
                if t in (3, 7):
                    load_quarter(g, sp, rest.pop(0))
            for i in range(2):
                sp.wait_ge(x1_stored[i], 16 * NT // 2)

        @g.cur.gpsimd
        def _(pool):
            def mix_a(t):
                s = t % 2
                pool.wait_ge(rows_in[s], 16 * n_in * (t // 2 + 1))
                if t >= 2:
                    pool.wait_ge(turned, t - 1)
                pool.tensor_tensor(mix[:, s, 0:HALF], inb[:, s, 0], inb[:, s, 1], ALU.mult).then_inc(mixed, 1)

            second = list(quarters(f"out{l}_b"))
            for step in range(-4, NT):
                t = step + L_CONV
                if l == 0 and t < NT:
                    pool.wait_ge(stats, 2 * (t + 1))
                    rms_scale(pool, g, mv[:, t % 2, 1:2], 1, pooled, 2 * t)
                t = step + L_MIX
                if 0 <= t < NT:
                    mix_a(t)
                    if l == 0:
                        pool.wait_ge(urow, t + 1)
                        pool.tensor_tensor(mix[:, t % 2, HALF:D], yb[:, t % 2], inb[:, t % 2, 3], ALU.mult).then_inc(mixed, 1)
                    if t in (4, 6, 8, 10):
                        split_quarter(g, pool, second.pop(0))
            qs = list(quarters(nxt))
            pool.wait_ge(mm_done, NT)
            for t in range(NT):
                pool.wait_ge(squared, NT + t + 1)
                pool.tensor_tensor(ss[:, 1, t:t + 1], ss[:, 0, t:t + 1], ss[:, 1, t:t + 1], ALU.add).then_inc(pooled, 1)
                pool.wait_ge(pooled, pool0 + 3 * t + 1)
                rms_scale(pool, g, ss[:, 1, t:t + 1], D, pooled, pool0 + 3 * t + 1)
                if t % 3 == 1:
                    split_quarter(g, pool, qs.pop(0))

        @g.cur.scalar
        def _(act):
            def split_hi(t, n):
                s = t % 2
                act.wait_ge(turned, n)
                k = nmix if n <= NT else 8
                act.copy(g.XT[0][:, 0:k, t * P:(t + 1) * P], ps_t[:, s, 0:k * P].rearrange("p (k c) -> p k c", c=P)).then_inc(hi, 1)
                if k == 4:
                    act.wait_ge(rows_in[s], 16 * n_in * (t // 2 + 1))
                    act.copy(g.XT[0][:, 4:8, t * P:(t + 1) * P], inb[:, s, 2].rearrange("p (k c) -> p k c", c=P)).then_inc(hi, 1)

            def square(t, half):
                src = ps_o[:, t % 2]
                if half:
                    act.wait_ge(squared, NT + t)
                act.activation(ps_n[:, 1] if half else src, src, ACT.Square, accum_out=ss[:, half, t:t + 1]).then_inc(squared, 1)

            for step in range(-4, NT):
                if 0 <= step + L_TURN < NT:
                    split_hi(step + L_TURN, step + L_TURN + 1)
                t = step + L_Y
                if l == 0 and 0 <= t < NT:
                    act.wait_ge(yrow, 3 * (t + 1))
                    if t:
                        act.wait_ge(urow, t)
                    act.activation(th[:], yb[:, t % 2], ACT.Tanh, scale=2.0).then_inc(tanhed, 1)
                if step >= 0:
                    t = step
                    act.wait_ge(mm_done, t + 1)
                    if t >= 2:
                        act.wait_ge(stored[t % 2], 16 * (t // 2))
                    act.copy(ost[:, t % 2], ps_o[:, t % 2]).then_inc(staged, 1)
                    act.wait_ge(staged, t + 1)
                    square(t, 0)
            for step in range(NT + 2):
                if step < NT:
                    act.wait_ge(mm_done, NT + step + 1)
                    square(step, 1)
                if step >= 2:
                    split_hi(step - 2, NT + step - 1)

        @g.cur.vector
        def _(dve):
            def split_lo(t, n):
                s = t % 2
                k = nmix if n <= NT else 8
                per = (1 if l == 0 else 2)
                base = per * (n - 1) if n <= NT else per * NT + (n - NT - 1)
                at = lambda part, k0, k1: g.XT[part][:, k0:k1, t * P:(t + 1) * P]
                dve.wait_ge(hi, base + 1)
                dve.tensor_tensor(at(1, 0, k), ps_t[:, s, 0:k * P].rearrange("p (k c) -> p k c", c=P), at(0, 0, k).bitcast(F32),
                                  ALU.subtract).then_inc(lo, 1)
                if k == 4:
                    dve.wait_ge(hi, base + 2)
                    dve.tensor_tensor(at(1, 4, 8), inb[:, s, 2].rearrange("p (k c) -> p k c", c=P), at(0, 4, 8).bitcast(F32),
                                      ALU.subtract).then_inc(lo, 1)

            for step in range(-4, NT):
                t = step + L_CONV
                if l == 0 and t < NT:
                    dve.wait_ge(conv_t, t + 1)
                    dve.bn_stats(bn[:, t % 2], ps_n[:, t % 2]).then_inc(stats, 1)
                    dve.wait_ge(stats, 2 * t + 1)
                    dve.bn_aggr(mv[:, t % 2], bn[:, t % 2]).then_inc(stats, 1)
                    if t == 0:
                        dve.wait_ge(cln_in, 32)
                        dve.tensor_scalar(cln[:], cln[:], 0.25, None, ALU.mult).then_inc(cln_ready, 1)
                        dve.wait_ge(cln_ready, 1)
                t = step + L_MIX
                if l == 0 and 0 <= t < NT:
                    y = yb[:, t % 2]
                    dve.wait_ge(tanhed, t + 1)
                    dve.scalar_tensor_tensor(y, th[:], 1.0, y, ALU.add, ALU.mult).then_inc(urow, 1)
                t = step + L_Y
                if l == 0 and 0 <= t < NT:
                    y = yb[:, t % 2]
                    dve.wait_ge(pooled, 2 * (t + 1))
                    if t >= 2:
                        dve.wait_ge(mixed, 2 * (t - 1))
                    dve.tensor_scalar(y, ps_n[:, t % 2], mv[:, t % 2, 0:1], mv[:, t % 2, 1:2], ALU.subtract, ALU.mult).then_inc(yrow, 1)
                    dve.wait_ge(yrow, 3 * t + 1)
                    dve.tensor_tensor(y, y, cln[:, 0], ALU.mult).then_inc(yrow, 1)
                    dve.wait_ge(yrow, 3 * t + 2)
                    dve.tensor_tensor(y, y, cln[:, 1], ALU.add).then_inc(yrow, 1)
                if 0 <= step + L_TURN < NT:
                    split_lo(step + L_TURN, step + L_TURN + 1)
            dve.wait_ge(gpost_in, 16)
            for step in range(NT + 2):
                if step < NT:
                    t, s = step, step % 2
                    x, x1 = inb[:, s, 0:2].rearrange("p a c -> p (a c)"), inb[:, s, 2:4].rearrange("p a c -> p (a c)")
                    r = ss[:, 1, t:t + 1]
                    dve.wait_ge(pooled, pool0 + 3 * (t + 1))
                    dve.wait_ge(x_in[s], 32 * (t // 2 + 1))
                    if t >= 2:
                        dve.wait_ge(x1_stored[s], 16 * (t // 2))
                        dve.wait_ge(turned, NT + t - 1)
                    dve.scalar_tensor_tensor(x1[:, HALF:D], ps_o[:, s], r, gpost[:, HALF:D], ALU.mult, ALU.mult).then_inc(x1_rows, 1)
                    dve.scalar_tensor_tensor(x1[:, 0:HALF], orl[:, s], r, gpost[:, 0:HALF], ALU.mult, ALU.mult).then_inc(x1_rows, 1)
                    dve.wait_ge(x1_rows, 3 * t + 2)
                    dve.tensor_tensor(x1, x1, x, ALU.add).then_inc(x1_rows, 1)
                if step >= 2:
                    split_lo(step - 2, NT + step - 1)

        @g.cur.tensor
        def _(pe):
            def product(t, c):
                name = f"out{l}_" + "ab"[c]
                n = c * NT + t
                if c == 0:
                    pe.wait_ge(lo, (1 if l == 0 else 2) * (t + 1))
                if n >= 2:
                    if n - 2 < NT:
                        pe.wait_ge(squared, n - 1)
                    else:
                        pe.wait_ge(x1_rows, 3 * (n - 2 - NT) + 2)
                i = 0
                for k in range(KC):
                    wait_quarter(g, pe, name, t, k)
                    for a, m in THREE:
                        mm = pe.matmul(ps_o[:, t % 2], g.XT[a][:, k, t * P:(t + 1) * P], w_at(g, name, m, k * HALF, HALF),
                                       start=i == 0, stop=i == 3 * KC - 1)
                        i += 1
                mm.then_inc(mm_done, 1)

            for step in range(-4, NT):
                t = step + L_CONV
                if l == 0 and t < NT:
                    pe.wait_ge(conv_in[t % 2], 16 * (t // 2 + 1))
                    if t >= 2:
                        pe.wait_ge(yrow, 3 * (t - 2) + 1)
                    for c in range(4):
                        tr = pe.transpose(ps_n[:, t % 2, c * P:(c + 1) * P], inb[:, t % 2, 2, c * P:(c + 1) * P], g.ident[:])
                    tr.then_inc(conv_t, 1)
                t = step + L_TURN
                if 0 <= t < NT:
                    pe.wait_ge(mixed, (2 if l == 0 else 1) * (t + 1))
                    if t >= 2:
                        pe.wait_ge(lo, (1 if l == 0 else 2) * (t - 2) + 1)
                    rows_turned(pe, mix[:, t % 2], ps_t[:, t % 2], g.ident[:], nmix).then_inc(turned, 1)
                if step >= 0:
                    product(step, 0)
            for step in range(NT + 2):
                if step < NT:
                    product(step, 1)
                if step >= 2:
                    t = step - 2
                    pe.wait_ge(x1_rows, 3 * (t + 1))
                    base = (1 if l == 0 else 2) * NT
                    pe.wait_ge(lo, base if t < 2 else base + t - 1)
                    rows_turned(pe, inb[:, t % 2, 2:4].rearrange("p a c -> p (a c)"), ps_t[:, t % 2], g.ident[:], 8).then_inc(turned, 1)
        g.end()



def gate(g, l):
    nc = g.nc
    pre = f"gt{l}_"
    dst = g.x2 if l == 0 else g.y
    with ExitStack() as st:
        sb = lambda name, shape, dt=F32: st.enter_context(nc.sbuf_tensor(pre + name, shape, dt))
        x1 = sb("x1", [P, 3, HALF])
        th = sb("tanh", [P, 2, HALF])
        x2 = sb("x2", [P, 3, HALF])
        pw_raw, pp_raw = sb("w_ple_raw", [P, 2 * HALF]), sb("p_raw", [P, 2, PLE])
        pw = [sb("w_ple_hi", [P, 2, 2 * HALF], F32R), sb("w_ple_lo", [P, 2, 2 * HALF], F32R)]
        pp = [sb("p_hi", [P, 2, PLE], F32R), sb("p_lo", [P, 2, PLE], F32R)]
        if l == 0:
            h = sb("h", [P, 2, D])
            gpre = sb("gpre", [P, D])
        ss = sb("ss", [P, 2, NT])
        ps = st.enter_context(nc.psum_tensor(pre + "ps", [P, 2, HALF], F32))
        ps_p = st.enter_context(nc.psum_tensor(pre + "ps_p", [P, 2, HALF], F32))
        ps_t = st.enter_context(nc.psum_tensor(pre + "ps_t", [P, 2, D], F32))
        sem = lambda n: g.sem(pre + n)
        rows_in, gpre_in, x2a_in = [sem(f"rows_in{i}") for i in range(3)], sem("gpre_in"), [sem("x2a_in0"), sem("x2a_in1")]
        pw_in, pw_split, pp_in, pp_split, ple_mm = sem("pw_in"), sem("pw_split"), [sem("pp_in0"), sem("pp_in1")], sem("pp_split"), sem("ple_mm")
        mm_done, tanhed, x2_rows, squared, pooled = sem("mm"), sem("tanhed"), sem("x2_rows"), sem("squared"), sem("pooled")
        stored = [sem(f"stored{i}") for i in range(3)]
        h_rows, turned, hi, lo = sem("h_rows"), sem("turned"), sem("hi"), sem("lo")
        U = 2 * NT

        def split_hi(act, t):
            act.wait_ge(turned, t + 1)
            act.copy(g.XT[0][:, :, t * P:(t + 1) * P], ps_t[:, t % 2].rearrange("p (k c) -> p k c", c=P)).then_inc(hi, 1)

        @g.block(pre + "phase").sync
        def _(sp):
            first = list(quarters(f"gate{l}_b"))
            nxt = list(quarters("lat")) if l == 0 else []
            sp.dma_start(pw_raw[:], g.w_ple[l, :, 0]).then_inc(pw_in, 16)
            if l == 0:
                sp.dma_start(gpre[:], g.g_pre_row.broadcast_to([P, D])).then_inc(gpre_in, 16)

            def load(u):
                c, t, s = u // NT, u % NT, u % 3
                if u >= 3:
                    sp.wait_ge(x2_rows, 2 * (u - 2))
                cols = slice(c * HALF, (c + 1) * HALF)
                sp.dma_start(x1[:, s], tiles_of(g.x1, t)[:, cols]).then_inc(rows_in[s], 16)
                if u >= 2:
                    sp.wait_ge(pp_split, 2 * (u - 1))
                sp.dma_start(pp_raw[:, u % 2], g.p_fm[l, t]).then_inc(pp_in[u % 2], 16)

            def load_x2a(t):
                sp.wait_ge(stored[t % 3], 16 * (t // 3 + 1))
                if t >= 2:
                    sp.wait_ge(turned, t - 1)
                sp.dma_start(h[:, t % 2, 0:HALF], tiles_of(g.x2, t)[:, 0:HALF]).then_inc(x2a_in[t % 2], 16)

            for u in range(2):
                load(u)
            for u in range(U):
                if u + 2 < U:
                    load(u + 2)
                if u < 4:
                    load_quarter(g, sp, first.pop(0))
                if u == 6:
                    sp.wait_ge(pw_split, 2)
                    sp.dma_start(pw_raw[:], g.w_ple[l, :, 1]).then_inc(pw_in, 16)
                if u in (13, 15, 17, 19) and nxt:
                    load_quarter(g, sp, nxt.pop(0))
                sp.wait_ge(x2_rows, 2 * (u + 1))
                c, t = u // NT, u % NT
                sp.dma_start(tiles_of(dst, t)[:, c * HALF:(c + 1) * HALF], x2[:, u % 3]).then_inc(stored[u % 3], 16)
                if l == 0 and c == 1:
                    load_x2a(t)
            for i in range(3):
                sp.wait_ge(stored[i], 16 * U // 3)

        @g.cur.gpsimd
        def _(pool):
            def rms(t):
                pool.wait_ge(squared, NT + t + 1)
                pool.tensor_tensor(ss[:, 1, t:t + 1], ss[:, 0, t:t + 1], ss[:, 1, t:t + 1], ALU.add).then_inc(pooled, 1)
                pool.wait_ge(pooled, 3 * t + 1)
                rms_scale(pool, g, ss[:, 1, t:t + 1], D, pooled, 3 * t + 1)

            def split(raw, parts, count, n):
                pool.tensor_tensor(parts[0], raw, g.zero[:, 0:1].broadcast_to([P, raw.shape[-1]]), ALU.add).then_inc(count, 1)
                pool.wait_ge(count, n + 1)
                pool.tensor_tensor(parts[1], raw, parts[0].bitcast(F32), ALU.subtract).then_inc(count, 1)

            second = list(quarters(f"gate{l}_b"))
            after = list(quarters("lat")) if l == 0 else []
            pool.wait_ge(pw_in, 16)
            split(pw_raw[:], [x[:, 0] for x in pw], pw_split, 0)
            for u in range(U):
                pool.wait_ge(pp_in[u % 2], 16 * (u // 2 + 1))
                if u >= 2:
                    pool.wait_ge(ple_mm, u - 1)
                split(pp_raw[:, u % 2], [x[:, u % 2] for x in pp], pp_split, 2 * u)
                if u == 8:
                    pool.wait_ge(pw_in, 32)
                    split(pw_raw[:], [x[:, 1] for x in pw], pw_split, 2)
                if u in (2, 3, 4, 5):
                    split_quarter(g, pool, second.pop(0))
                t = u - NT - 2
                if l == 0 and t >= 0:
                    rms(t)
                    if t % 3 == 0:
                        split_quarter(g, pool, after.pop(0))
            if l == 0:
                for t in range(NT - 2, NT):
                    rms(t)

        @g.cur.scalar
        def _(act):
            for u in range(U + 3):
                if u < U:
                    act.wait_ge(mm_done, u + 1)
                    if u >= 2 and l == 0:
                        act.wait_ge(squared, u - 1)
                    elif u >= 2:
                        act.wait_ge(x2_rows, 2 * (u - 2) + 1)
                    act.activation(th[:, u % 2], ps[:, u % 2], ACT.Tanh, scale=0.5).then_inc(tanhed, 1)
                if l == 0 and 1 <= u <= U:
                    v = u - 1
                    act.wait_ge(x2_rows, 2 * (v + 1))
                    act.activation(th[:, v % 2], x2[:, v % 3], ACT.Square, accum_out=ss[:, v // NT, v % NT:v % NT + 1]).then_inc(squared, 1)
                t = u - NT - 2
                if l == 0 and 0 <= t < NT:
                    split_hi(act, t)

        @g.cur.vector
        def _(dve):
            def split_lo(t):
                dve.wait_ge(hi, t + 1)
                at = lambda part: g.XT[part][:, :, t * P:(t + 1) * P]
                dve.tensor_tensor(at(1), ps_t[:, t % 2].rearrange("p (k c) -> p k c", c=P), at(0).bitcast(F32),
                                  ALU.subtract).then_inc(lo, 1)

            def h_row(t):
                if t == 0:
                    dve.wait_ge(gpre_in, 16)
                u, r = NT + t, ss[:, 1, t:t + 1]
                dve.wait_ge(pooled, 3 * (t + 1))
                dve.wait_ge(x2a_in[t % 2], 16 * (t // 2 + 1))
                if t >= 2:
                    dve.wait_ge(turned, t - 1)
                dve.scalar_tensor_tensor(h[:, t % 2, 0:HALF], h[:, t % 2, 0:HALF], r, gpre[:, 0:HALF], ALU.mult, ALU.mult).then_inc(h_rows, 1)
                dve.scalar_tensor_tensor(h[:, t % 2, HALF:D], x2[:, u % 3], r, gpre[:, HALF:D], ALU.mult, ALU.mult).then_inc(h_rows, 1)

            for u in range(U + 3):
                if u < U:
                    s = u % 3
                    dve.wait_ge(tanhed, u + 1)
                    dve.wait_ge(ple_mm, u + 1)
                    dve.wait_ge(rows_in[s], 16 * (u // 3 + 1))
                    if u >= 3:
                        dve.wait_ge(stored[s], 16 * (u // 3))
                        if l == 0:
                            dve.wait_ge(squared, u - 2)
                    dve.scalar_tensor_tensor(x2[:, s], th[:, u % 2], 1.0, ps_p[:, u % 2], ALU.add, ALU.mult).then_inc(x2_rows, 1)
                    dve.wait_ge(x2_rows, 2 * u + 1)
                    dve.scalar_tensor_tensor(x2[:, s], x2[:, s], 0.5, x1[:, s], ALU.mult, ALU.add).then_inc(x2_rows, 1)
                if l == 0 and 0 <= u - NT - 1 < NT:
                    h_row(u - NT - 1)
                if l == 0 and 0 <= u - NT - 2 < NT:
                    split_lo(u - NT - 2)

        @g.cur.tensor
        def _(pe):
            for u in range(U + 3):
                c, t = u // NT, u % NT
                if u < U:
                    name = f"gate{l}_" + "ab"[c]
                    if u >= 2:
                        pe.wait_ge(tanhed, u - 1)
                    i = 0
                    for k in range(KC):
                        wait_quarter(g, pe, name, t, k)
                        for a, m in THREE:
                            mm = pe.matmul(ps[:, u % 2], g.XT[a][:, k, t * P:(t + 1) * P], w_at(g, name, m, k * HALF, HALF),
                                           start=i == 0, stop=i == 3 * KC - 1)
                            i += 1
                    mm.then_inc(mm_done, 1)
                    pe.wait_ge(pp_split, 2 * (u + 1))
                    pe.wait_ge(pw_split, 2 * (c + 1))
                    if u >= 2:
                        pe.wait_ge(x2_rows, 2 * (u - 2) + 1)
                    for k in range(PLE // P):
                        for a, m in THREE:
                            mm = pe.matmul(ps_p[:, u % 2], pp[a][:, u % 2, k * P:(k + 1) * P], pw[m][:, c, k * HALF:(k + 1) * HALF],
                                           start=k + a + m == 0, stop=k == PLE // P - 1 and a == 1)
                    mm.then_inc(ple_mm, 1)
                v = u - NT - 2
                if l == 0 and 0 <= v < NT:
                    pe.wait_ge(h_rows, 2 * (v + 1))
                    if v >= 2:
                        pe.wait_ge(lo, v - 1)
                    rows_turned(pe, h[:, v % 2], ps_t[:, v % 2], g.ident[:], 8).then_inc(turned, 1)
        g.end()



def in_odd(g):
    nc = g.nc
    names = ["lat", "gc", "f", "gd"]
    NQ, NKV = 256, 128
    R0 = NQ + NKV
    with ExitStack() as st:
        sb = lambda name, shape, dt=F32: st.enter_context(nc.sbuf_tensor("io_" + name, shape, dt))
        stage = sb("stage", [P, 4, HALF])
        th = sb("tanh", [P, 2, HALF])
        rope = sb("rope", [P, NT, 2 * ROPE])
        ss = sb("ss", [P, NT, 2])
        tmp = sb("tmp", [P, 2, ROPE])
        ps = st.enter_context(nc.psum_tensor("io_ps", [P, 7, HALF], F32))
        junk = st.enter_context(nc.psum_tensor("io_junk", [P, HALF], F32))
        sem = lambda n: g.sem("io_" + n)
        mm_done, copied, tanhed, gated, squared, pooled, latent_ops, rope_in = (
            sem("mm"), sem("copied"), sem("tanhed"), sem("gated"), sem("squared"), sem("pooled"), sem("latent_ops"), sem("rope_in"))
        stored = [sem(f"stored{i}") for i in range(4)]
        NBANK = 7
        kinds = [k for n in names for k in [{"lat": "lat", "gc": "gate", "f": "copy", "gd": "gate"}[n]] * 12]
        n_copy = [sum(k != "gate" for k in kinds[:i]) for i in range(len(kinds) + 1)]
        n_gate = [sum(k == "gate" for k in kinds[:i]) for i in range(len(kinds) + 1)]
        LAT = 5

        def dest(u):
            n, j = names[u // 12], u % 12
            if n in ("lat", "gc"):
                return tiles_of(g.lat if n == "lat" else g.gate_c, j)
            c, b = FM_ORDER[j]
            return (g.f if n == "f" else g.gate_d)[c, :, b * 512:(b + 1) * 512]

        @g.block("in_odd").sync
        def _(sp):
            sp.dma_start(rope[:], g.c_rope_k).then_inc(rope_in, 16)
            for u, kd in enumerate(kinds):
                j, i = u % 12, PIDX[names[u // 12]]
                if j % 2 == 0 and j < 8:
                    load_quarter(g, sp, QBASE[i + 1] + j // 2)
                if kd == "lat":
                    sp.wait_ge(latent_ops, LAT * (u + 1))
                elif kd == "copy":
                    sp.wait_ge(copied, n_copy[u + 1])
                else:
                    sp.wait_ge(gated, n_gate[u + 1])
                sp.dma_start(dest(u), stage[:, u % 4]).then_inc(stored[u % 4], 16)
            for i in range(4):
                sp.wait_ge(stored[i], 16 * len(kinds) // 4)

        @g.cur.gpsimd
        def _(pool):
            qs = list(quarters("gc"))
            for t in range(NT):
                pool.wait_ge(squared, 2 * (t + 1))
                rms_scale(pool, g, ss[:, t, :], 1, pooled, 2 * t)
                if t % 2 == 1 and qs:
                    split_quarter(g, pool, qs.pop(0))
            for i, n in ((1, "f"), (2, "gd"), (3, "up")):
                for q in quarters(n):
                    if q == quarters(n)[0]:
                        pool.wait_ge(mm_done, 12 * i)
                    split_quarter(g, pool, q)

        @g.cur.scalar
        def _(act):
            def squares(t):
                for i, (a, b) in enumerate(((0, NQ), (NQ, R0))):
                    n = 2 * t + i
                    if n:
                        act.wait_ge(squared, n)
                    act.activation(junk[:, a:b], ps[:, t % NBANK, a:b], ACT.Square, scale=(b - a) ** -0.5,
                                   accum_out=ss[:, t, i:i + 1]).then_inc(squared, 1)

            for u, kd in enumerate(kinds):
                act.wait_ge(mm_done, u + 1)
                if kd == "gate":
                    i = n_gate[u]
                    if i >= 2:
                        act.wait_ge(gated, i - 1)
                    act.activation(th[:, i % 2], ps[:, u % NBANK], ACT.Tanh, scale=0.5).then_inc(tanhed, 1)
                else:
                    if kd == "lat":
                        squares(u)
                    if u >= 4:
                        act.wait_ge(stored[u % 4], 16 * (u // 4))
                    act.copy(stage[:, u % 4], ps[:, u % NBANK]).then_inc(copied, 1)

        @g.cur.vector
        def _(dve):
            dve.wait_ge(rope_in, 16)
            for u, kd in enumerate(kinds):
                x = stage[:, u % 4]
                if kd == "lat":
                    dve.wait_ge(copied, n_copy[u + 1])
                    dve.wait_ge(pooled, 2 * (u + 1))
                    n = LAT * u
                    dve.tensor_tensor(tmp[:, 0], x[:, R0:R0 + ROPE], rope[:, u, 0:ROPE], ALU.mult).then_inc(latent_ops, 1)
                    dve.tensor_tensor(tmp[:, 1], x[:, R0 + ROPE:R0 + 2 * ROPE], rope[:, u, ROPE:], ALU.mult).then_inc(latent_ops, 1)
                    dve.tensor_scalar(x[:, 0:NQ], x[:, 0:NQ], ss[:, u, 0:1], None, ALU.mult).then_inc(latent_ops, 1)
                    dve.tensor_scalar(x[:, NQ:R0], x[:, NQ:R0], ss[:, u, 1:2], None, ALU.mult).then_inc(latent_ops, 1)
                    dve.wait_ge(latent_ops, n + 2)
                    dve.tensor_tensor(x[:, R0 + DH:R0 + DH + ROPE], tmp[:, 0], tmp[:, 1], ALU.add).then_inc(latent_ops, 1)
                    dve.wait_ge(latent_ops, n + 5)
                elif kd == "gate":
                    i = n_gate[u]
                    dve.wait_ge(tanhed, i + 1)
                    if u >= 4:
                        dve.wait_ge(stored[u % 4], 16 * (u // 4))
                    dve.scalar_tensor_tensor(x, th[:, i % 2], 1.0, ps[:, u % NBANK], ALU.add, ALU.mult).then_inc(gated, 1)

        def free(pe, u):
            v = u - NBANK
            if v >= 0:
                if kinds[v] == "gate":
                    pe.wait_ge(gated, n_gate[v + 1])
                else:
                    pe.wait_ge(copied, n_copy[v + 1])

        @g.cur.tensor
        def _(pe):
            for i, n in enumerate(names):
                project(g, pe, n, n in ("f", "gd"), FM_ORDER, ps, 12 * i, free, mm_done, NBANK)
        g.end()



def latent(g):
    nc = g.nc
    with ExitStack() as st:
        sb = lambda name, shape, dt=F32: st.enter_context(nc.sbuf_tensor("la_" + name, shape, dt))
        rows = sb("rows", [P, 2, 4, HALF])
        L = [sb("hi_part", [P, 3, TOK], F32R), sb("lo_part", [P, 3, TOK], F32R)]
        kr = sb("kr", [P, TOK])
        stage = sb("stage", [P, 3, TOK])
        qscale = sb("qscale", [P, TOK])
        latg = sb("gain", [P, 3])
        ps_t = st.enter_context(nc.psum_tensor("la_ps_t", [P, 4, HALF], F32))
        ps = st.enter_context(nc.psum_tensor("la_ps", [P, 4, HALF], F32))
        sem = lambda n: g.sem("la_" + n)
        rows_in, consts_in, turned, hi, lo = [sem(f"rows_in{t}") for t in range(NT)], sem("consts_in"), sem("turned"), sem("hi"), sem("lo")
        mm_done, by_act, by_dve = sem("mm"), sem("by_act"), sem("by_dve")
        stored, kr_stored = [sem(f"stored{i}") for i in range(3)], sem("kr_stored")
        groups = [x for i in range(4) for x in (("k", i), ("q", 2 * i), ("q", 2 * i + 1), ("v", i))]
        n_act = [3 * sum(x[0] != "q" for x in groups[:i]) for i in range(len(groups) + 1)]
        n_dve = [3 * sum(x[0] == "q" for x in groups[:i]) for i in range(len(groups) + 1)]

        def evacuated(eng, u):
            if groups[u // 3][0] == "q":
                eng.wait_ge(by_dve, n_dve[u // 3] + u % 3 + 1)
            else:
                eng.wait_ge(by_act, n_act[u // 3] + u % 3 + 1)

        @g.block("latent").sync
        def _(sp):
            def load(b):
                if b >= 2:
                    sp.wait_ge(turned, 4 * (b - 1))
                for j in range(4):
                    sp.dma_start(rows[:, b % 2, j], tiles_of(g.lat, 4 * b + j)).then_inc(rows_in[4 * b + j], 16)

            load(0)
            sp.dma_start(latg[:], g.lat_g).then_inc(consts_in, 16)
            load(1)
            sp.dma_start(qscale[:], g.c_qscale).then_inc(consts_in, 16)
            load(2)
            for n in quarters("dft"):
                load_quarter(g, sp, n)
            sp.wait_ge(lo, 4 * NB)
            sp.dma_start(g.kr, kr[DH:DH + ROPE, :]).then_inc(kr_stored, 16)
            for i, (kind, n) in enumerate(groups):
                evacuated(sp, 3 * i + 2)
                src = stage[:, i % 3]
                if kind == "v":
                    dst = g.vv[3 * n * P:(3 * n + 3) * P, :].rearrange("(t p) c -> p t c", p=P)
                    src = src.rearrange("p (t c) -> p t c", c=HALF)
                elif kind == "k":
                    dst = g.kn[2 * n:2 * n + 2].rearrange("h d t -> (h d) t")
                else:
                    dst = g.qs[n]
                sp.dma_start(dst, src).then_inc(stored[i % 3], 16)
            for i in range(3):
                sp.wait_ge(stored[i], 16 * len(range(i, len(groups), 3)))
            sp.wait_ge(kr_stored, 16)

        @g.cur.gpsimd
        def _(pool):
            for n in quarters("dft"):
                split_quarter(g, pool, n)

        @g.cur.scalar
        def _(act):
            act.wait_ge(consts_in, 32)
            for b in range(NB):
                for k in range(3):
                    act.wait_ge(turned, 4 * b + k + 1)
                    act.activation(L[0][:, k, b * 512:(b + 1) * 512], ps_t[:, (4 * b + k) % 4], ACT.Copy,
                                   scale=latg[:, k:k + 1]).then_inc(hi, 1)
            for i, (kind, n) in enumerate(groups):
                if kind == "q":
                    continue
                if i >= 3:
                    act.wait_ge(stored[i % 3], 16 * (i // 3))
                for j in range(3):
                    u = 3 * i + j
                    act.wait_ge(mm_done, u + 1)
                    act.activation(stage[:, i % 3, j * 512:(j + 1) * 512], ps[:, u % 4], ACT.Copy,
                                   scale=0.5 if kind == "v" else 1.0).then_inc(by_act, 1)

        @g.cur.vector
        def _(dve):
            dve.wait_ge(consts_in, 32)
            for b in range(NB):
                for k in range(4):
                    r = 4 * b + k
                    cols = slice(b * 512, (b + 1) * 512)
                    if k < 3:
                        dve.wait_ge(hi, 3 * b + k + 1)
                        dve.scalar_tensor_tensor(L[1][:, k, cols], ps_t[:, r % 4], latg[:, k:k + 1], L[0][:, k, cols].bitcast(F32),
                                                 ALU.mult, ALU.subtract).then_inc(lo, 1)
                    else:
                        dve.wait_ge(turned, r + 1)
                        dve.tensor_copy(kr[:, cols], ps_t[:, r % 4]).then_inc(lo, 1)
            for i, (kind, n) in enumerate(groups):
                if kind != "q":
                    continue
                if i >= 3:
                    dve.wait_ge(stored[i % 3], 16 * (i // 3))
                for j in range(3):
                    u = 3 * i + j
                    cols = slice(j * 512, (j + 1) * 512)
                    dve.wait_ge(mm_done, u + 1)
                    dve.tensor_tensor(stage[:, i % 3, cols], ps[:, u % 4], qscale[:, cols], ALU.mult).then_inc(by_dve, 1)

        @g.cur.tensor
        def _(pe):
            for b in range(NB):
                for k in range(4):
                    r = 4 * b + k
                    if r >= 4:
                        pe.wait_ge(lo, r - 3)
                    for j in range(4):
                        if k == 0:
                            pe.wait_ge(rows_in[4 * b + j], 16)
                        tr = pe.transpose(ps_t[:, r % 4, j * P:(j + 1) * P], rows[:, b % 2, j, k * P:(k + 1) * P], g.ident[:])
                    tr.then_inc(turned, 1)
            wait_pair(g, pe, "up")
            pe.wait_ge(lo, 4 * NB)
            for i, (kind, n) in enumerate(groups):
                for j in range(3):
                    u = 3 * i + j
                    cols = slice(j * 512, (j + 1) * 512)
                    if u >= 4:
                        evacuated(pe, u - 4)
                    terms = []
                    for a, m in THREE:
                        if kind == "v":
                            terms.append((L[a][:, 2, (3 * n + j) * P:(3 * n + j + 1) * P], w_at(g, "up", m, 2560, 512)))
                        elif kind == "k":
                            terms.append((w_at(g, "up", a, 2048 + n * P, P), L[m][:, 2, cols]))
                        else:
                            terms += [(w_at(g, "up", a, k * 1024 + n * P, P), L[m][:, k, cols]) for k in range(2)]
                    for x, (lhs, rhs) in enumerate(terms):
                        mm = pe.matmul(ps[:, u % 4], lhs, rhs, start=x == 0, stop=x == len(terms) - 1)
                    mm.then_inc(mm_done, 1)
        g.end()



class Operands:
    LOADS, PREPS = 48, 6

    def __init__(self, g, st):
        sb = lambda name, shape, dt=F32: st.enter_context(g.nc.sbuf_tensor("ml_" + name, shape, dt))
        self.xq, self.xk = sb("xq", [P, TOK]), sb("xk", [P, TOK])
        self.xv = sb("xv", [P, NT, DH])
        self.Q = [sb("q_hi", [P, 2, TOK], F32R), sb("q_lo", [P, 2, TOK], F32R)]
        self.K = [sb("k_hi", [P, 2, TOK], F32R), sb("k_lo", [P, 2, TOK], F32R)]
        self.V = sb("v", [P, 2, NT, P], F32R)
        self.loaded, self.rope_loaded = g.sem("ml_loaded"), g.sem("ml_rope_loaded")
        self.prepped = g.sem("ml_prepped")

    def load_rope(self, g, sp):
        for r in (DH, DH + ROPE):
            sp.dma_start(self.xk[r:r + ROPE, :], g.kr).then_inc(self.rope_loaded, 16)

    def load(self, g, sp, h, cols):
        sp.dma_start(self.xq[:], g.qs[h]).then_inc(self.loaded, 16)
        sp.dma_start(self.xk[0:DH, :], g.kn[h]).then_inc(self.loaded, 16)
        sp.dma_start(self.xv[:], g.vv.rearrange("(t p) c -> p t c", p=P)[:, :, cols]).then_inc(self.loaded, 16)

    def prep(self, g, pool, h, s):
        zeros = g.zero[:, 0:1].broadcast_to([P, TOK])
        pool.wait_ge(self.loaded, h * self.LOADS + self.LOADS)
        pool.tensor_tensor(self.Q[0][:, s], self.xq[:], zeros, ALU.add).then_inc(self.prepped, 1)
        pool.tensor_tensor(self.K[0][:, s], self.xk[:], zeros, ALU.add).then_inc(self.prepped, 1)
        pool.tensor_tensor(self.V[:, s, :, 0:DH], self.xv[:], g.zero3, ALU.add).then_inc(self.prepped, 1)
        pool.wait_ge(self.prepped, h * self.PREPS + 3)
        pool.tensor_tensor(self.Q[1][:, s], self.xq[:], self.Q[0][:, s].bitcast(F32), ALU.subtract).then_inc(self.prepped, 1)
        pool.tensor_tensor(self.K[1][:, s], self.xk[:], self.K[0][:, s].bitcast(F32), ALU.subtract).then_inc(self.prepped, 1)
        pool.tensor_tensor(self.V[:, s, :, DH:P], self.xv[:], self.V[:, s, :, 0:DH].bitcast(F32), ALU.subtract).then_inc(self.prepped, 1)



def fnet(g, ml):
    nc = g.nc
    with ExitStack() as st:
        sb = lambda name, shape, dt=F32: st.enter_context(nc.sbuf_tensor("fn_" + name, shape, dt))
        f = sb("f", [P, 2, TOK])
        gd = sb("gate", [P, 2, TOK])
        EO = sb("eo", [P, 2, 2, TOK // 2])
        Y = [sb("y_hi", [P, 2, NT // 2, 2, P], F32R), sb("y_lo", [P, 2, NT // 2, 2, P], F32R)]
        fsum = sb("alternating", [P, 2, 2, 2])
        yh = sb("y_half", [1, 2, 2, P])
        a_sb = sb("a", [P, 2, HALF])
        S = sb("s", [P, TOK])
        dft_ch = sb("dft_ch", [P, 2 * P])
        falt = sb("falt", [P, 4, 2])
        alt = sb("alt", [1, HALF])
        ps_y = st.enter_context(nc.psum_tensor("fn_ps_y", [P, 2, HALF], F32))
        ps_yh = st.enter_context(nc.psum_tensor("fn_ps_yh", [P, HALF], F32))
        ps_a = st.enter_context(nc.psum_tensor("fn_ps_a", [P, 2, HALF], F32))
        ps_b = st.enter_context(nc.psum_tensor("fn_ps_b", [P, 2, HALF], F32))
        ps_half = st.enter_context(nc.psum_tensor("fn_ps_half", [P, HALF], F32))
        sem = lambda n: g.sem("fn_" + n)
        consts_in, f_in, gd_in = sem("consts_in"), [sem("f_in0"), sem("f_in1")], [sem("gd_in0"), sem("gd_in1")]
        odd_zero, folded, y_mm, y_hi, y_lo, yh_done = sem("odd_zero"), sem("folded"), sem("y_mm"), sem("y_hi"), sem("y_lo"), sem("yh_done")
        a_mm, b_mm, half_mm, a_copied, half_copied, unfolded = (
            sem("a_mm"), sem("b_mm"), sem("half_mm"), sem("a_copied"), sem("half_copied"), sem("unfolded"))
        mixed, stored = sem("mixed"), [sem("stored0"), sem("stored1")]
        NGR = 4
        FOLDS, ROUNDS = 8, NT // 4
        SEQ = [(0, SEQS[0]), (SEQS[0], SEQS[1])]

        @g.block("fnet").sync
        def _(sp):
            def load(c):
                if c >= 2:
                    sp.wait_ge(y_mm, (ROUNDS + 1) * (c - 1))
                sp.dma_start(f[:, c % 2], g.f[c]).then_inc(f_in[c % 2], 16)

            def load_gate(c):
                if c >= 2:
                    sp.wait_ge(stored[c % 2], 32 * (c // 2))
                sp.dma_start(gd[:, c % 2], g.gate_d[c]).then_inc(gd_in[c % 2], 16)

            load(0)
            for dst, src in ((dft_ch[:], g.c_dft_ch), (alt[:], g.c_alt)):
                sp.dma_start(dst, src).then_inc(consts_in, 16)
            ml.load_rope(g, sp)
            load(1)
            ml.load(g, sp, 0, slice(0, DH))
            load_gate(0)
            load_gate(1)
            for c in range(2, NGR):
                load(c)
            for c in range(NGR):
                for i, (t0, n) in enumerate(SEQ):
                    sp.wait_ge(mixed, 2 * c + i + 1)
                    sp.dma_start(g.dmix[c, :, t0:t0 + n], gd[:, c % 2, t0:t0 + n]).then_inc(stored[c % 2], 16)
                if c + 2 < NGR:
                    load_gate(c + 2)
            for i in range(2):
                sp.wait_ge(stored[i], 32 * NGR // 2)

        @g.cur.gpsimd
        def _(pool):
            pool.wait_ge(ml.rope_loaded, 32)
            ml.prep(g, pool, 0, 0)

        @g.cur.vector
        def _(dve):
            for i in range(2):
                dve.memset(EO[:, i, 1, 0:513:512], 0.0).then_inc(odd_zero, 1)

            def fold(c):
                x = f[:, c % 2]
                dve.wait_ge(f_in[c % 2], 16 * (c // 2 + 1))
                if c >= 2:
                    dve.wait_ge(y_mm, (ROUNDS + 1) * (c - 1))
                dve.tensor_copy(EO[:, c % 2, 0, 0:513:512], x[:, 0:1025:1024]).then_inc(folded, 1)
                for t0, n in SEQ:
                    for i, op in enumerate((ALU.add, ALU.subtract)):
                        dve.tensor_tensor(EO[:, c % 2, i, t0 // 2 + 1:t0 // 2 + n // 2], x[:, t0 + 1:t0 + n // 2],
                                          x[:, t0 + n - 1:t0 + n // 2:-1], op).then_inc(folded, 1)
                for i, (t0, n) in enumerate(SEQ):
                    dve.tensor_reduce(fsum[:, c % 2, i], x[:, t0:t0 + n].rearrange("p (s two) -> p two s", two=2), AX.X, ALU.add).then_inc(folded, 1)
                dve.wait_ge(folded, FOLDS * c + FOLDS - 1)
                dve.tensor_tensor(falt[:, c], fsum[:, c % 2, :, 0], fsum[:, c % 2, :, 1], ALU.subtract).then_inc(folded, 1)

            def split_lo(c):
                for r in range(ROUNDS):
                    i = ROUNDS * c + r
                    at = lambda part: Y[part][:, c % 2, 2 * r:2 * r + 2]
                    dve.wait_ge(y_hi, i + 1)
                    dve.tensor_tensor(at(1), ps_y[:, i % 2].rearrange("p (c e k) -> p c e k", c=2, e=2), at(0).bitcast(F32),
                                      ALU.subtract).then_inc(y_lo, 1)

            def unfold(c):
                for i, (t0, n) in enumerate(SEQ):
                    w, m = 2 * c + i, n // 2
                    dve.wait_ge(a_copied, w + 1)
                    dve.wait_ge(b_mm, w + 1)
                    if i == 0 and c:
                        dve.wait_ge(mixed, 2 * c)
                    dve.tensor_tensor(S[:, t0:t0 + m], a_sb[:, w % 2, 0:m], ps_b[:, w % 2, 0:m], ALU.add).then_inc(unfolded, 1)
                    dve.tensor_tensor(S[:, t0 + m + 1:t0 + n], a_sb[:, w % 2, m - 1:0:-1], ps_b[:, w % 2, m - 1:0:-1],
                                      ALU.subtract).then_inc(unfolded, 1)
                    gated(c, i)

            def gated(c, i):
                t0, n = SEQ[i]
                dve.wait_ge(gd_in[c % 2], 16 * (c // 2 + 1))
                dve.wait_ge(unfolded, 4 * c + 2 * i + 2)
                dve.wait_ge(half_copied, 2 * c + i + 1)
                dve.tensor_tensor(gd[:, c % 2, t0:t0 + n], S[:, t0:t0 + n], gd[:, c % 2, t0:t0 + n], ALU.mult).then_inc(mixed, 1)

            fold(0)
            fold(1)
            for c in range(NGR + 1):
                if c < NGR:
                    split_lo(c)
                if 1 <= c and c + 1 < NGR:
                    fold(c + 1)
                if c >= 1:
                    unfold(c - 1)

        @g.cur.scalar
        def _(act):
            def split_hi(c):
                for r in range(ROUNDS):
                    i = ROUNDS * c + r
                    act.wait_ge(y_mm, i + c + 1)
                    if r == 0 and c >= 2:
                        act.wait_ge(b_mm, 2 * (c - 1))
                    act.copy(Y[0][:, c % 2, 2 * r:2 * r + 2], ps_y[:, i % 2].rearrange("p (c e k) -> p c e k", c=2, e=2)).then_inc(y_hi, 1)
                act.wait_ge(y_mm, (ROUNDS + 1) * (c + 1))
                if c >= 2:
                    act.wait_ge(a_mm, 2 * (c - 1))
                for i, (t0, n) in enumerate(SEQ):
                    act.activation(yh[:, c % 2, i], ps_yh[0:1, i * P:(i + 1) * P], ACT.Copy, scale=0.5 * (n * P) ** -0.5).then_inc(yh_done, 1)

            def middle(c):
                for i, (t0, n) in enumerate(SEQ):
                    w, m = 2 * c + i, n // 2
                    act.wait_ge(a_mm, w + 1)
                    if w >= 2:
                        act.wait_ge(unfolded, 2 * (w - 1))
                    act.copy(a_sb[:, w % 2, 0:m], ps_a[:, w % 2, 0:m]).then_inc(a_copied, 1)
                    act.wait_ge(half_mm, c + 1)
                    if i == 0 and c:
                        act.wait_ge(mixed, 2 * c)
                    act.activation(S[:, t0 + m:t0 + m + 1], ps_half[:, i:i + 1], ACT.Copy, scale=0.5 * (n * P) ** -0.5).then_inc(half_copied, 1)

            for c in range(NGR + 1):
                if c < NGR:
                    split_hi(c)
                if c >= 1:
                    middle(c - 1)

        @g.cur.tensor
        def _(pe):
            def channels(c):
                pe.wait_ge(folded, FOLDS * c + 5)
                if c == 0:
                    pe.wait_ge(odd_zero, 2)
                    pe.wait_ge(consts_in, 32)
                for r in range(ROUNDS):
                    i = ROUNDS * c + r
                    if i >= 2:
                        pe.wait_ge(y_lo, i - 1)
                    for j in range(2):
                        for e in range(2):
                            mm = pe.matmul(ps_y[:, i % 2, (2 * j + e) * P:(2 * j + e + 1) * P],
                                           EO[:, c % 2, e, (2 * r + j) * P:(2 * r + j + 1) * P], dft_ch[:, e * P:(e + 1) * P],
                                           start=True, stop=True)
                    mm.then_inc(y_mm, 1)
                if c:
                    pe.wait_ge(yh_done, 2 * c)
                for i, (t0, n) in enumerate(SEQ):
                    mm = pe.matmul(ps_yh[0:1, i * P:(i + 1) * P], f[:, c % 2, t0 + n // 2:t0 + n // 2 + 1], dft_ch[:, 0:P],
                                   start=True, stop=True)
                mm.then_inc(y_mm, 1)

            def tokens(c):
                s = c % 2
                pe.wait_ge(y_lo, ROUNDS * (c + 1))
                pe.wait_ge(yh_done, 2 * (c + 1))
                pe.wait_ge(folded, FOLDS * (c + 1))
                if c:
                    pe.wait_ge(half_copied, 2 * c)
                pe.matmul(ps_half[:, 0:2], dft_ch[:, 0:P], falt[:, c], start=True, stop=True).then_inc(half_mm, 1)
                for i, (t0, n) in enumerate(SEQ):
                    w, m = 2 * c + i, n // 2
                    nk = m // P
                    if i == 0:
                        table = lambda e, part, k: w_at(g, "dft", part, (e * nk + k) * m, m)
                    else:
                        table = lambda e, part, k: w_at(g, "up", part, 3072 + (e * nk + k) * m, m)
                    k0 = t0 // 2 // P
                    for e, dst, done in ((0, ps_a, a_mm), (1, ps_b, b_mm)):
                        if w >= 2:
                            if e == 0:
                                pe.wait_ge(a_copied, w - 1)
                            else:
                                pe.wait_ge(unfolded, 2 * (w - 1))
                        if e == 0:
                            pe.matmul(dst[:, w % 2, 0:m], yh[:, s, i], alt[:, 0:m], start=True, stop=False)
                        for k in range(nk):
                            for a, b in THREE:
                                mm = pe.matmul(dst[:, w % 2, 0:m], Y[a][:, s, k0 + k, e], table(e, b, k),
                                               start=e == 1 and k + a + b == 0, stop=k == nk - 1 and a == 1)
                        mm.then_inc(done, 1)

            for c in range(NGR + 1):
                if c < NGR:
                    channels(c)
                if c >= 1:
                    tokens(c - 1)
        g.end()



KEYS = [(0, 8) if t < 8 else (8, 4) for t in range(NT)]
ML_BATCHES = [KEYS[t][1] // 4 for t in range(NT)]


def mla(g, ml):
    nc = g.nc
    with ExitStack() as st:
        sb = lambda name, shape, dt=F32: st.enter_context(nc.sbuf_tensor("mla_" + name, shape, dt))
        S = sb("s", [P, 2, 2 * HALF])
        mins = sb("min", [P, 3])
        sums, rinv = sb("sums", [P, NG, 2]), sb("rinv", [P, 2, 2])
        red = sb("red", [P, 2, 2, DH])
        PT = [sb("pt_hi", [P, 2, 8, 256], F32R), sb("pt_lo", [P, 2, 8, 256], F32R)]
        pv_sb = sb("pv", [P, 2, 256])
        out = sb("out", [P, NT, HALF])
        ps_s = st.enter_context(nc.psum_tensor("mla_ps_s", [P, 2, 2 * HALF], F32))
        ps_t = st.enter_context(nc.psum_tensor("mla_ps_t", [P, 2, HALF], F32))
        ps_pv = st.enter_context(nc.psum_tensor("mla_ps_pv", [P, HALF], F32))
        ps_back = st.enter_context(nc.psum_tensor("mla_ps_back", [P, HALF], F32))
        pl = Pipeline(g, "mla", minned=0, exped=2)
        attn_out = g.sem("mla_attn_out")
        act_copy, pe_back, dve_add, dve_norm = attention_tail(g, pl, ps_pv, ps_back, pv_sb, sums, rinv, red, out)

        nb = sum(ML_BATCHES)

        def bat(j):
            return nb * (j // NT) + sum(ML_BATCHES[:j % NT])

        @g.block("mla").sync
        def _(sp):
            def store(cols, tiles=slice(0, NT)):
                sp.dma_start(g.attn[1].rearrange("(t p) c -> p t c", p=P)[:, tiles, cols], out[:, tiles, cols]).then_inc(attn_out, 16)

            sp.wait_ge(ml.prepped, ml.PREPS)
            ml.load(g, sp, 1, slice(DH, 2 * DH))
            with sp.Fori(0, HEADS // 2 - 1) as pair:
                for s in (2, 3):
                    sp.wait_ge(ml.prepped, pair * 2 * ml.PREPS + s * ml.PREPS)
                    ml.load(g, sp, pair * 2 + s, bass.ds(pair * 2 * DH + s * DH, DH))
                pl.wait(sp, "normed", pair * 2 * NG + 2 * NG)
                store(bass.ds(pair * 2 * DH, 2 * DH))
            for n in quarters("out1_a"):
                load_quarter(g, sp, n)
            for q, tiles in ((4, slice(0, 8)), (NG, slice(8, NT))):
                pl.wait(sp, "normed", (HEADS - 1) * NG + q)
                store(slice(HALF - 2 * DH, HALF), tiles)
            sp.wait_ge(attn_out, 16 * (HEADS // 2 + 1))

        @g.cur.gpsimd
        def _(pool):
            with pool.Fori(0, HEADS // 2 - 1) as pair:
                for s in (1, 2):
                    pl.wait(pool, "weighed", pair * 2 * NG + (s - 1) * NG)
                    ml.prep(g, pool, pair * 2 + s, s % 2)
            pl.wait(pool, "weighed", (HEADS - 2) * NG)
            ml.prep(g, pool, HEADS - 1, 1)
            for n in quarters("out1_a"):
                split_quarter(g, pool, n)

        @g.cur.tensor
        def _(pe):
            pl.give(pe, "turned", "weighed", "back")

            def scores(h, j):
                t, s = j % NT, j // NT
                if t == 0:
                    pe.wait_ge(ml.prepped, h * ml.PREPS + (s + 1) * ml.PREPS)
                pl.wait(pe, "exped", h * NT + (j - 1))
                for half in range(KEYS[t][1] // 4):
                    k0 = KEYS[t][0] * P + half * 512
                    for a, m in THREE:
                        mm = pe.matmul(ps_s[:, j % 2, half * 512:(half + 1) * 512], ml.Q[a][:, s, t * P:(t + 1) * P],
                                       ml.K[m][:, s, k0:k0 + 512], start=a + m == 0, stop=a == 1)
                mm.then_inc(pl["scored"], 1)

            def turn(h, j, b):
                if b == 0:
                    pl.wait(pe, "exped", h * NT + (j + 1))
                q = bat(j) + b
                pl.wait(pe, "lo", h * nb + (q - 1))
                for i in range(4):
                    tr = pe.transpose(ps_t[:, q % 2, i * P:(i + 1) * P], S[:, j % 2, (4 * b + i) * P:(4 * b + i + 1) * P], g.ident[:])
                tr.then_inc(pl["turned"], 1)

            def weigh(h, q, half):
                if half == 0:
                    pl.wait(pe, "lo", h * nb + bat(2 * q + 2))
                    pl.wait(pe, "copied", h * NG + q)
                k0, n = KEYS[2 * q % NT]
                for c in range(half * n // 2, (half + 1) * n // 2):
                    for part in range(2):
                        mm = pe.matmul(ps_pv[:, 0:256], ml.V[:, q // NG % 2, k0 + c], PT[part][:, q % 2, c],
                                       start=c + part == 0, stop=c + part == n)
                if half:
                    mm.then_inc(pl["weighed"], 1)

            def body(h, steps, live):
                for step in steps:
                    if live(step):
                        scores(h, step)
                    if live(step - 2):
                        turn(h, step - 2, 0)
                    if live(step - 4 - step % 2):
                        weigh(h, (step - 4) // 2, step % 2)
                    if live(step - 2) and ML_BATCHES[(step - 2) % NT] == 2:
                        turn(h, step - 2, 1)
                    if step % 2 and live(step - 7):
                        pe_back(pe, h * NG, (step - 7) // 2)

            pair_loop(pe, body)

        @g.cur.scalar
        def _(act):
            pl.give(act, "copied", "exped")

            def exp(h, j):
                pl.wait(act, "minned", h * NT + (j + 1))
                w = KEYS[j % NT][1] * P
                act.activation(S[:, j % 2, 0:w], ps_s[:, j % 2, 0:w], ACT.Exp, bias=mins[:, j % 3:j % 3 + 1], scale=-1.0,
                               accum_out=sums[:, j % NT // 2, j % 2:j % 2 + 1]).then_inc(pl["exped"], 1)

            def hi(h, j):
                if j % 2 == 0:
                    pl.wait(act, "weighed", h * NG + (j // 2 - 1))
                for b in range(ML_BATCHES[j % NT]):
                    q = bat(j) + b
                    pl.wait(act, "turned", h * nb + (q + 1))
                    act.copy(PT[0][:, j // 2 % 2, 4 * b:4 * b + 4, j % 2 * P:(j % 2 + 1) * P],
                             ps_t[:, q % 2].rearrange("p (c k) -> p c k", k=P)).then_inc(pl["hi"], 1)

            def body(h, steps, live):
                for step in steps:
                    if live(step - 2):
                        hi(h, step - 2)
                    if step % 2 and live(step - 5):
                        act_copy(act, h * NG, (step - 5) // 2)
                    if live(step):
                        exp(h, step)

            pair_loop(act, body)

        @g.cur.vector
        def _(dve):
            pl.give(dve, "lo", "reduced")

            def minimum(h, j):
                pl.wait(dve, "scored", h * NT + (j + 1))
                dve.tensor_reduce(mins[:, j % 3:j % 3 + 1], ps_s[:, j % 2, 0:KEYS[j % NT][1] * P], AX.X, ALU.min).then_inc(pl["minned"], 1)

            def lo(h, j):
                for b in range(ML_BATCHES[j % NT]):
                    q = bat(j) + b
                    pl.wait(dve, "hi", h * nb + (q + 1))
                    at = lambda part: PT[part][:, j // 2 % 2, 4 * b:4 * b + 4, j % 2 * P:(j % 2 + 1) * P]
                    dve.tensor_tensor(at(1), ps_t[:, q % 2].rearrange("p (c k) -> p c k", k=P), at(0).bitcast(F32),
                                      ALU.subtract).then_inc(pl["lo"], 1)

            def body(h, steps, live):
                for step in steps:
                    if live(step):
                        minimum(h, step)
                    if step % 2 and live(step - 9):
                        q = (step - 9) // 2
                        dst = out[:, 2 * (q % NG):2 * (q % NG) + 2, bass.ds(h * DH + q // NG * DH, DH)]
                        dve_norm(dve, h * NG, q, dst)
                    if step % 2 == 0 and live(step - 8):
                        dve_add(dve, h * NG, (step - 8) // 2)
                    if live(step - 2):
                        lo(h, step - 2)

            pair_loop(dve, body)
        g.end()



def build(nc, io, phases=99):
    with ExitStack() as stack:
        g = Ctx(nc, stack)
        g.x, g.y, g.wall, g.dw, g.rpb, g.cln = (io[n] for n in ("x", "y", "wall", "dw", "rpb", "cln"))
        g.lat_g, g.p_fm, g.w_ple = io["lat_g"], io["p_fm"], io["w_ple"]
        g.g_pre_cols, g.g_pre_row, g.g_post = io["g_pre_cols"], io["g_pre_row"], io["g_post"]
        g.c_ident, g.c_cmask, g.c_imask, g.c_rope_k, g.c_qscale, g.c_dft_ch, g.c_alt = (
            io["c_" + n] for n in ("ident", "cmask", "imask", "rope_k", "qscale", "dft_ch", "alt"))
        g.dram()
        g.raw = g.sb("w_raw", [P, 2, QCOLS])
        g.W = [g.sb("w_hi_part", [P, 2, PAIRCOLS], F32R), g.sb("w_lo_part", [P, 2, PAIRCOLS], F32R)]
        g.ident = g.sb("ident", [P, P])
        g.zero = g.sb("zero", [P, 1])
        g.zero3 = g.zero[:].rearrange("p (a b) -> p a b", a=1).broadcast_to([P, NT, DH])
        g.mhalf = g.sb("minus_half", [P, 1])
        ring_sem = lambda name: nc.alloc_semaphore(name=name)
        g.raw_loaded = [ring_sem("raw_loaded0"), ring_sem("raw_loaded1")]
        g.w_hi, g.w_ready = ring_sem("w_hi"), ring_sem("w_ready")

        def with_rows(name, *fs):
            with nc.sbuf_tensor(f"{name}_xt_hi", [P, KC, TOK], F32R) as hi, nc.sbuf_tensor(f"{name}_xt_lo", [P, KC, TOK], F32R) as lo:
                g.XT = [hi, lo]
                for f in fs:
                    f()

        def with_operands(*fs):
            with ExitStack() as st:
                ml = Operands(g, st)
                for f in fs:
                    f(g, ml)

        steps = [
            lambda: with_rows("l0in", lambda: prologue(g), lambda: in_even(g)),
            lambda: natten(g),
            lambda: with_rows("l0out", lambda: out_proj(g, 0), lambda: gate(g, 0), lambda: in_odd(g)),
            lambda: (g.renew_semaphores(), latent(g)),
            lambda: with_operands(fnet, mla),
            lambda: with_rows("l1out", lambda: out_proj(g, 1), lambda: gate(g, 1)),
        ]
        for f in steps[:phases]:
            f()


def lay_out(inputs):
    f = {k: np.ascontiguousarray(np.asarray(v)) for k, v in inputs.items()}
    chunks = lambda w: w.reshape(-1, P, w.shape[-1]).transpose(1, 0, 2).reshape(P, -1)

    def pair(*parts):
        a = np.concatenate([chunks(x) for x in parts], axis=1)
        return np.concatenate([a, np.zeros((P, PAIRCOLS - a.shape[1]), np.float32)], axis=1)

    p_fm = np.concatenate([f["p_prompt"][:, 0], f["p_sample"][:, 0]], 1).reshape(2, NT, P, PLE // P, P).transpose(0, 1, 4, 3, 2)
    w_ple = f["w_ple"].reshape(2, PLE // P, P, 2, HALF).transpose(0, 2, 3, 1, 4)
    we, wo = f["w_in_e"][0], f["w_in_o"][0]
    q, k, v, ga, ua, ub, gb = np.split(we, 7, axis=1)
    cq, ckv, kr, gc, fi, gd = np.split(wo, [256, 384, 416, 928, 1440], axis=1)
    swap = lambda w: np.concatenate([w[..., ROPE // 2:], w[..., :ROPE // 2]], -1)
    uq = f["w_uq"][0].reshape(256, HEADS, DH + ROPE)
    uq = np.concatenate([uq, swap(uq[..., DH:])], -1).reshape(256, HEADS * P)
    ukv = f["w_ukv"][0].reshape(P, HEADS, 2 * DH)
    un, uv = ukv[..., :DH].reshape(P, 512), ukv[..., DH:].reshape(P, 512)
    ublk = lambda c: [ub[:, c * P:(c + 1) * P], ua[:, c * P:(c + 1) * P]]
    by = {
        "u0": pair(np.concatenate(ublk(0) + ublk(1), 1)), "u1": pair(np.concatenate(ublk(2) + ublk(3), 1)),
        "q": pair(q), "v": pair(v), "k": pair(k), "ga": pair(ga), "gb": pair(gb),
        "lat": pair(np.concatenate([cq, ckv, kr, swap(kr), np.zeros((D, 64), np.float32)], 1)),
        "gc": pair(gc), "f": pair(fi), "gd": pair(gd),
    }
    for l in range(2):
        w_out = f["w_out_e" if l == 0 else "w_out_o"][0]
        for h, c in (("a", 0), ("b", 1)):
            by[f"out{l}_{h}"] = pair(w_out[:, c * HALF:(c + 1) * HALF])
            by[f"gate{l}_{h}"] = pair(f["w_ple_gate"][l][:, c * HALF:(c + 1) * HALF])

    def dft(n, fn):
        a = np.arange(n // 2)
        return (fn(2 * np.pi * (np.outer(a, a) % n) / n) * 0.5 / np.sqrt(n * P)).astype(np.float32)

    by["up"] = pair(uq, un, uv, dft(512, np.cos), dft(512, np.sin))
    by["dft"] = pair(dft(1024, np.cos), dft(1024, np.sin))
    a = np.outer(np.arange(P), np.arange(P)) % P * (2 * np.pi / P)
    dft_ch = np.concatenate([np.cos(a), -np.sin(a)], 1).astype(np.float32)
    alt = (1.0 - 2.0 * (np.arange(HALF) % 2))[None]

    pos = np.concatenate([np.arange(s, dtype=np.float32) for s in SEQS])
    inv = (np.float32(10000.0) ** (-np.arange(0, ROPE, 2, dtype=np.float32) / np.float32(ROPE))).astype(np.float32)
    ang = pos[:, None] * inv[None, :]
    cos, sin = np.cos(ang).astype(np.float32), np.sin(ang).astype(np.float32)
    rope_k = np.concatenate([cos, cos, -sin, sin], 1).reshape(NT, P, 2 * ROPE).transpose(1, 0, 2)
    c = np.float32((DH + ROPE) ** -0.5)
    qscale = np.full((P, TOK), -c, np.float32)
    qscale[DH:] = -c * np.concatenate([cos, cos, -sin, sin], 1).T

    qc = np.arange(P) % GRID
    cs = np.clip(qc - 8, 0, GRID - 16)
    kc = np.arange(GRID)
    cmask = np.where((kc[None] >= cs[:, None]) & (kc[None] < cs[:, None] + 16), 0.0, BIG).astype(np.float32)
    imask = np.zeros((P, 10, GRID), np.float32)
    imask[:, 9] = BIG
    imask[:64, 8] = BIG
    imask[64:, 0] = BIG
    rpb = np.zeros((HEADS, 15, P), np.float32)
    rpb[:, :, 48:79] = f["rpb"][0]

    dw = np.concatenate([f["dw_w"][0].T, f["dw_b"][0][:, None]], 1).reshape(4, P, TAPS + 1).transpose(1, 0, 2)
    cols = lambda v: v.reshape(-1, P).T
    arrays = {
        "p_fm": p_fm.reshape(2, NT, P, PLE), "w_ple": w_ple.reshape(2, P, 2, 2 * HALF),
        "x": np.concatenate([f["x_prompt"][0], f["x_sample"][0]], 0),
        "wall": np.stack([by[n] for n in PAIRS]),
        "c_ident": np.eye(P, dtype=np.float32),
        "g_pre_cols": cols(f["g_pre"][0]), "g_pre_row": f["g_pre"][1:2], "g_post": f["g_post"],
        "cln": np.stack([f["cln_g"][0], f["cln_b"][0]]),
        "lat_g": np.concatenate([cols(f["q_norm_g"][0]), cols(f["kv_norm_g"][0])], 1),
        "dw": dw, "rpb": rpb, "c_cmask": cmask, "c_imask": imask.reshape(P, 640),
        "c_rope_k": rope_k, "c_qscale": qscale, "c_dft_ch": dft_ch, "c_alt": alt,
    }
    return {k: np.ascontiguousarray(v, np.float32) for k, v in arrays.items()}


def kernel(**inputs):
    import concourse.bacc as bacc
    from concourse.bass_utils import run_bass_kernel_spmd as run

    nc = bacc.Bacc("TRN2", target_bir_lowering=False, num_devices=1, dynamic_dma_scratch_size=1024)
    arrays = lay_out(inputs)
    io = {n: nc.dram_tensor(n, a.shape, F32, kind="ExternalInput").ap() for n, a in arrays.items()}
    io["y"] = nc.dram_tensor("y", (TOK, D), F32, kind="ExternalOutput").ap()
    build(nc, io)
    y = run(nc, [arrays], core_ids=[0]).results[0]["y"]
    return y[:SEQS[0]][None], y[SEQS[0]:][None]
```
